# Optimizing a Trainium2 kernel written in Bass

```python
import jax, jax.numpy as jnp
from jax import lax
import numpy as np
import math

D_MODEL = 1024
BATCH = 1
SEQ = 512
DEPTH = 2

N_MIXERS = 2
EPS = 1e-6

SSM_EXPAND = 2
SSM_D_INNER = SSM_EXPAND * D_MODEL
SSM_HEAD_DIM = 64
SSM_HEADS = SSM_D_INNER // SSM_HEAD_DIM
SSM_GROUPS = 8
SSM_HEADS_PER_GROUP = SSM_HEADS // SSM_GROUPS
SSM_STATE = 128
SSM_CONV = 4
SSM_CHUNK = 128
SSM_BC_DIM = SSM_GROUPS * SSM_STATE
SSM_CONV_DIM = SSM_D_INNER + 2 * SSM_BC_DIM
SSM_IN_DIM = SSM_D_INNER + SSM_CONV_DIM + SSM_HEADS

ATT_HEAD_DIM = 64
ATT_Q_HEADS = D_MODEL // ATT_HEAD_DIM
ATT_KV_HEADS = 4
ATT_GQA = ATT_Q_HEADS // ATT_KV_HEADS
ATT_WIDTH = ATT_Q_HEADS * ATT_HEAD_DIM
ATT_KV_WIDTH = ATT_KV_HEADS * ATT_HEAD_DIM
ATT_IN_DIM = 2 * ATT_WIDTH + 2 * ATT_KV_WIDTH
WINDOW = 128
ATT_BLOCK = 128
ROPE_THETA = 500000.0
ROPE_DIM = ATT_HEAD_DIM // 4

N_SSM_LAYERS = (DEPTH + 1) // 2
N_ATT_LAYERS = DEPTH // 2


def rmsnorm(x, w):
    xf = x.astype(jnp.float32)
    y = xf * lax.rsqrt(jnp.mean(xf * xf, axis=-1, keepdims=True) + EPS)
    return (y * w.astype(jnp.float32)).astype(x.dtype)

def causal_depthwise_conv(u, w, b):
    c = u.shape[-1]
    out = lax.conv_general_dilated(
        u, w[:, None, :].astype(u.dtype), window_strides=(1,),
        padding=((SSM_CONV - 1, 0),), dimension_numbers=('NWC', 'WIO', 'NWC'),
        feature_group_count=c)
    return out + b.astype(u.dtype)

def ssd_chunked(xs, dt, A, Bm, Cm):
    b, L = xs.shape[:2]
    c, l = L // SSM_CHUNK, SSM_CHUNK
    G, R, P, N = SSM_GROUPS, SSM_HEADS_PER_GROUP, SSM_HEAD_DIM, SSM_STATE
    x = (xs * dt[..., None]).reshape(b, c, l, G, R, P)
    a = jnp.moveaxis((dt * A).reshape(b, c, l, G, R), 2, -1)
    a_cs = jnp.cumsum(a, axis=-1)
    Bc = Bm.reshape(b, c, l, G, N)
    Cc = Cm.reshape(b, c, l, G, N)
    causal = jnp.tril(jnp.ones((l, l), dtype=bool))
    seg = a_cs[..., :, None] - a_cs[..., None, :]
    decay = jnp.exp(jnp.where(causal, seg, -jnp.inf))
    cb = jnp.einsum('bclgn,bcsgn->bcgls', Cc, Bc)
    y_diag = jnp.einsum('bcgrls,bcsgrp->bclgrp', cb[:, :, :, None] * decay, x)
    decay_to_end = jnp.exp(a_cs[..., -1:] - a_cs)
    states = jnp.einsum('bclgn,bcgrl,bclgrp->bcgrpn', Bc, decay_to_end, x)
    chunk_decay = jnp.exp(a_cs[..., -1])

    def step(h, inp):
        s, d = inp
        return h * d[..., None, None] + s, h

    h0 = jnp.zeros_like(states[:, 0])
    _, h_in = lax.scan(step, h0, (jnp.moveaxis(states, 1, 0), jnp.moveaxis(chunk_decay, 1, 0)))
    h_in = jnp.moveaxis(h_in, 0, 1)
    y_off = jnp.einsum('bclgn,bcgrpn,bcgrl->bclgrp', Cc, h_in, jnp.exp(a_cs))
    return (y_diag + y_off).reshape(b, L, SSM_HEADS, P)

def mamba2_mixer(h, w_in, conv_w, conv_b, dt_bias, a_log, d_skip, gate_norm, w_out):
    b, L, _ = h.shape
    f32 = jnp.float32
    z, xbc, dt = jnp.split(h @ w_in, [SSM_D_INNER, SSM_D_INNER + SSM_CONV_DIM], axis=-1)
    xbc = jax.nn.silu(causal_depthwise_conv(xbc, conv_w, conv_b))
    xs, Bm, Cm = jnp.split(xbc, [SSM_D_INNER, SSM_D_INNER + SSM_BC_DIM], axis=-1)
    xs = xs.reshape(b, L, SSM_HEADS, SSM_HEAD_DIM).astype(f32)
    Bm = Bm.reshape(b, L, SSM_GROUPS, SSM_STATE).astype(f32)
    Cm = Cm.reshape(b, L, SSM_GROUPS, SSM_STATE).astype(f32)
    dt = jax.nn.softplus(dt.astype(f32) + dt_bias.astype(f32))
    A = -jnp.exp(a_log.astype(f32))
    y = ssd_chunked(xs, dt, A, Bm, Cm) + d_skip.astype(f32)[:, None] * xs
    y = y.reshape(b, L, SSM_D_INNER) * jax.nn.silu(z.astype(f32))
    y = rmsnorm(y, gate_norm)
    return y.astype(h.dtype) @ w_out

def rope_tables(positions):
    inv = ROPE_THETA ** (-jnp.arange(0, ROPE_DIM, 2, dtype=jnp.float32) / ROPE_DIM)
    ang = positions.astype(jnp.float32)[..., None] * inv
    return jnp.cos(ang)[:, :, None, :], jnp.sin(ang)[:, :, None, :]

def apply_partial_rope(t, cos, sin):
    half = ROPE_DIM // 2
    t1, t2, rest = t[..., :half], t[..., half:ROPE_DIM], t[..., ROPE_DIM:]
    return jnp.concatenate([t1 * cos - t2 * sin, t2 * cos + t1 * sin, rest], axis=-1)

def swa_sink_mixer(h, cos, sin, w_in, sinks, w_out):
    b, L, _ = h.shape
    f32 = jnp.float32
    Hk, D, BLK = ATT_KV_HEADS, ATT_HEAD_DIM, ATT_BLOCK
    q, k, v, gate = jnp.split(
        h @ w_in, [ATT_WIDTH, ATT_WIDTH + ATT_KV_WIDTH, ATT_WIDTH + 2 * ATT_KV_WIDTH], axis=-1)
    q = apply_partial_rope(q.reshape(b, L, ATT_Q_HEADS, D).astype(f32), cos, sin)
    k = apply_partial_rope(k.reshape(b, L, Hk, D).astype(f32), cos, sin)
    v = v.reshape(b, L, Hk, D).astype(f32)
    nb = L // BLK
    qb = q.reshape(b, nb, BLK, Hk, ATT_GQA, D)

    def band(t):
        tp = jnp.pad(t, ((0, 0), (BLK, 0), (0, 0), (0, 0))).reshape(b, nb + 1, BLK, Hk, D)
        return jnp.concatenate([tp[:, :-1], tp[:, 1:]], axis=2)

    kb, vb = band(k), band(v)
    s = jnp.einsum('bnikgd,bnjkd->bnkgij', qb, kb) * (D ** -0.5)
    qi = jnp.arange(BLK)[:, None]
    kj = jnp.arange(2 * BLK)[None, :]
    dist = qi + BLK - kj
    blk = jnp.arange(nb)[:, None, None]
    valid = (dist >= 0) & (dist < WINDOW) & ((blk - 1) * BLK + kj >= 0)
    s = jnp.where(valid[None, :, None, None], s, -jnp.inf)
    sink = sinks.astype(f32).reshape(Hk, ATT_GQA)[None, None, :, :, None, None]
    m = jnp.maximum(jnp.max(s, axis=-1, keepdims=True), sink)
    p = jnp.exp(s - m)
    denom = jnp.sum(p, axis=-1, keepdims=True) + jnp.exp(sink - m)
    o = jnp.einsum('bnkgij,bnjkd->bnikgd', p / denom, vb)
    o = o.reshape(b, L, ATT_WIDTH) * jax.nn.silu(gate.astype(f32))
    return o.astype(h.dtype) @ w_out

def first_inputs(seed: int = 0) -> dict:
    key = jax.random.key(seed)
    ks = jax.random.split(key, 16)
    f32 = jnp.float32
    nS, nA = N_SSM_LAYERS, N_ATT_LAYERS
    x = jax.random.normal(ks[0], (BATCH, SEQ, D_MODEL), f32)
    positions = jnp.broadcast_to(jnp.arange(SEQ, dtype=jnp.int32), (BATCH, SEQ))
    pre_norm = 1.0 + 0.1 * jax.random.normal(ks[1], (DEPTH, D_MODEL), f32)
    post_norm = 1.0 + 0.1 * jax.random.normal(ks[2], (DEPTH, D_MODEL), f32)
    ssm_w_in = jax.random.normal(ks[3], (nS, D_MODEL, SSM_IN_DIM), f32) * D_MODEL ** -0.5
    ssm_conv_w = jax.random.normal(ks[4], (nS, SSM_CONV, SSM_CONV_DIM), f32) * SSM_CONV ** -0.5
    ssm_conv_b = 0.02 * jax.random.normal(ks[5], (nS, SSM_CONV_DIM), f32)
    dt0 = jnp.exp(jax.random.uniform(ks[6], (nS, SSM_HEADS), f32)
                  * (np.log(0.1) - np.log(0.001)) + np.log(0.001)).astype(f32)
    ssm_dt_bias = dt0 + jnp.log(-jnp.expm1(-dt0))
    ssm_a_log = jnp.log(jax.random.uniform(ks[7], (nS, SSM_HEADS), f32, 1.0, 16.0))
    ssm_d = 1.0 + 0.1 * jax.random.normal(ks[8], (nS, SSM_HEADS), f32)
    ssm_gate_norm = 1.0 + 0.1 * jax.random.normal(ks[9], (nS, SSM_D_INNER), f32)
    ssm_w_out = jax.random.normal(ks[10], (nS, SSM_D_INNER, D_MODEL), f32) * SSM_D_INNER ** -0.5
    att_w_in = jax.random.normal(ks[11], (nA, D_MODEL, ATT_IN_DIM), f32) * D_MODEL ** -0.5
    att_sinks = 0.5 * jax.random.normal(ks[12], (nA, ATT_Q_HEADS), f32)
    att_w_out = jax.random.normal(ks[13], (nA, ATT_WIDTH, D_MODEL), f32) * ATT_WIDTH ** -0.5
    return {"x": x, "positions": positions, "pre_norm": pre_norm, "post_norm": post_norm,
            "ssm_w_in": ssm_w_in, "ssm_conv_w": ssm_conv_w, "ssm_conv_b": ssm_conv_b,
            "ssm_dt_bias": ssm_dt_bias, "ssm_a_log": ssm_a_log, "ssm_d": ssm_d,
            "ssm_gate_norm": ssm_gate_norm, "ssm_w_out": ssm_w_out,
            "att_w_in": att_w_in, "att_sinks": att_sinks, "att_w_out": att_w_out}

def first_block(x, positions, pre_norm, post_norm, ssm_w_in, ssm_conv_w, ssm_conv_b,
              ssm_dt_bias, ssm_a_log, ssm_d, ssm_gate_norm, ssm_w_out,
              att_w_in, att_sinks, att_w_out):
    cos, sin = rope_tables(positions)
    for i in range(DEPTH):
        h = rmsnorm(x, pre_norm[i])
        j = i // N_MIXERS
        if i % N_MIXERS == 0:
            y = mamba2_mixer(h, ssm_w_in[j], ssm_conv_w[j], ssm_conv_b[j], ssm_dt_bias[j],
                             ssm_a_log[j], ssm_d[j], ssm_gate_norm[j], ssm_w_out[j])
        else:
            y = swa_sink_mixer(h, cos, sin, att_w_in[j], att_sinks[j], att_w_out[j])
        x = x + rmsnorm(y, post_norm[i])
    return x


N_META = 16
BLOCK_Q = 128
ROPE_THETA_2 = 10000.0
RMS_EPS = 1e-6
DA_HEADS = 8
DA_HEAD_DIM = 64
DSA_HEADS = 16
DSA_HEAD_DIM = 64
IDX_HEADS = 8
IDX_DIM = 64
TOPK_MAX = 256
DSA_QKV = DSA_HEADS * DSA_HEAD_DIM
DSA_SPLITS = [DSA_QKV, 2 * DSA_QKV, 3 * DSA_QKV,
              3 * DSA_QKV + IDX_HEADS * IDX_DIM,
              3 * DSA_QKV + IDX_HEADS * IDX_DIM + IDX_DIM]
DSA_IN_WIDTH = DSA_SPLITS[-1] + IDX_HEADS
ROPE_DIM_2 = 64
BIG_SCORE = 1e30
FFN_HIDDEN = 2816
CONV_WIDTH = 3


def rms_norm(x, g):
    xf = x.astype(jnp.float32)
    y = xf * lax.rsqrt(jnp.mean(xf * xf, axis=-1, keepdims=True) + RMS_EPS)
    return (y * g.astype(jnp.float32)).astype(x.dtype)

def rope_tables_2(T, dim):
    inv = ROPE_THETA_2 ** (-jnp.arange(0, dim, 2, dtype=jnp.float32) / dim)
    ang = jnp.arange(T, dtype=jnp.float32)[:, None] * inv[None, :]
    return jnp.cos(ang), jnp.sin(ang)

def apply_rope(x, cos, sin):
    shape = (1, cos.shape[0]) + (1,) * (x.ndim - 3) + (cos.shape[1],)
    c = cos.reshape(shape)
    s = sin.reshape(shape)
    x1, x2 = jnp.split(x.astype(jnp.float32), 2, axis=-1)
    return jnp.concatenate([x1 * c - x2 * s, x2 * c + x1 * s], axis=-1).astype(x.dtype)

def sweep_blocks(fn, T):
    out = lax.map(fn, jnp.arange(T // BLOCK_Q) * BLOCK_Q)
    out = jnp.moveaxis(out, 0, 1)
    return out.reshape((out.shape[0], T) + out.shape[3:])

def diff_attention(h, w_qkv, lq1, lk1, lq2, lk2, subln, w_o, cos, sin, lambda_init):
    B, T, _ = h.shape
    q, k, v = jnp.split(h @ w_qkv, 3, axis=-1)
    q = apply_rope(q.reshape(B, T, DA_HEADS, 2, DA_HEAD_DIM), cos, sin) * (DA_HEAD_DIM ** -0.5)
    k = apply_rope(k.reshape(B, T, DA_HEADS, 2, DA_HEAD_DIM), cos, sin)
    v = v.reshape(B, T, DA_HEADS, 2 * DA_HEAD_DIM)
    f32 = jnp.float32
    lam = (jnp.exp(jnp.sum(lq1.astype(f32) * lk1.astype(f32)))
           - jnp.exp(jnp.sum(lq2.astype(f32) * lk2.astype(f32))) + lambda_init)
    k_pos = jnp.arange(T)

    def block(start):
        q_pos = start + jnp.arange(BLOCK_Q)
        qb = lax.dynamic_slice_in_dim(q, start, BLOCK_Q, axis=1)
        s = jnp.einsum('bqhcd,bkhcd->bhcqk', qb, k).astype(f32)
        s = jnp.where(k_pos[None, :] <= q_pos[:, None], s, -jnp.inf)
        p = jax.nn.softmax(s, axis=-1)
        a = p[:, :, 0] - lam * p[:, :, 1]
        return jnp.einsum('bhqk,bkhe->bqhe', a.astype(v.dtype), v)

    o = sweep_blocks(block, T)
    o = rms_norm(o, subln) * (1.0 - lambda_init)
    return o.reshape(B, T, DA_HEADS * 2 * DA_HEAD_DIM) @ w_o

def dsa_attention(h, w_in, idx_k_norm, w_o, cos, sin, n_keys):
    B, T, _ = h.shape
    q, k, v, qi, ki, wi = jnp.split(h @ w_in, DSA_SPLITS, axis=-1)
    q = apply_rope(q.reshape(B, T, DSA_HEADS, DSA_HEAD_DIM), cos, sin) * (DSA_HEAD_DIM ** -0.5)
    k = apply_rope(k.reshape(B, T, DSA_HEADS, DSA_HEAD_DIM), cos, sin)
    v = v.reshape(B, T, DSA_HEADS, DSA_HEAD_DIM)
    qi = apply_rope(qi.reshape(B, T, IDX_HEADS, IDX_DIM), cos, sin)
    ki = apply_rope(rms_norm(ki, idx_k_norm), cos, sin)
    wi = wi * (IDX_HEADS ** -0.5)
    topk = min(TOPK_MAX, n_keys // 4)
    k_pos = jnp.arange(T)
    f32 = jnp.float32
    gather = jax.vmap(lambda arr, idx: arr[idx])

    def block(start):
        q_pos = start + jnp.arange(BLOCK_Q)
        qb = lax.dynamic_slice_in_dim(q, start, BLOCK_Q, axis=1)
        qib = lax.dynamic_slice_in_dim(qi, start, BLOCK_Q, axis=1)
        wb = lax.dynamic_slice_in_dim(wi, start, BLOCK_Q, axis=1)
        raw = jnp.einsum('bqhd,bkd->bqhk', qib, ki).astype(f32) * (IDX_DIM ** -0.5)
        score = jnp.einsum('bqhk,bqh->bqk', jax.nn.relu(raw), wb.astype(f32))
        causal = k_pos[None, :] <= q_pos[:, None]
        score = jnp.where(causal & (k_pos < N_META)[None, :], BIG_SCORE, score)
        score = jnp.where(causal, score, -jnp.inf)
        top_val, top_idx = lax.top_k(score, topk)
        valid = top_val > -jnp.inf
        ks = gather(k, top_idx)
        vs = gather(v, top_idx)
        s = jnp.einsum('bqhd,bqjhd->bhqj', qb, ks).astype(f32)
        s = jnp.where(valid[:, None], s, -jnp.inf)
        p = jax.nn.softmax(s, axis=-1)
        return jnp.einsum('bhqj,bqjhd->bqhd', p.astype(vs.dtype), vs)

    o = sweep_blocks(block, T)
    return o.reshape(B, T, DSA_QKV) @ w_o

def conv_ffn(h, w_up, conv_w, conv_b, w_down):
    u = h @ w_up
    T = u.shape[1]
    up = jnp.pad(u, ((0, 0), (CONV_WIDTH - 1, 0), (0, 0)))
    c = conv_b + sum(conv_w[j] * up[:, j:j + T] for j in range(CONV_WIDTH))
    g, val = jnp.split(c, 2, axis=-1)
    return (jax.nn.silu(g) * val) @ w_down

def second_inputs(seed: int = 0) -> dict:
    key = jax.random.key(seed)
    ks = iter(jax.random.split(key, 32))
    n_a = (DEPTH + 1) // 2
    n_b = DEPTH // 2
    D, F = D_MODEL, FFN_HIDDEN

    def nrm(shape, scale):
        return jax.random.normal(next(ks), shape, jnp.float32) * scale

    def gain(shape):
        return 1.0 + nrm(shape, 0.02)

    return {
        "x": nrm((BATCH, SEQ, D), 1.0),
        "meta_tokens": nrm((N_META, D), 1.0),
        "da_norm": gain((n_a, D)),
        "da_w_qkv": nrm((n_a, D, 3 * D), D ** -0.5),
        "da_lambda_q1": nrm((n_a, DA_HEAD_DIM), 0.1),
        "da_lambda_k1": nrm((n_a, DA_HEAD_DIM), 0.1),
        "da_lambda_q2": nrm((n_a, DA_HEAD_DIM), 0.1),
        "da_lambda_k2": nrm((n_a, DA_HEAD_DIM), 0.1),
        "da_subln": gain((n_a, 2 * DA_HEAD_DIM)),
        "da_w_o": nrm((n_a, DA_HEADS * 2 * DA_HEAD_DIM, D), D ** -0.5),
        "dsa_norm": gain((n_b, D)),
        "dsa_w_in": nrm((n_b, D, DSA_IN_WIDTH), D ** -0.5),
        "dsa_idx_k_norm": gain((n_b, IDX_DIM)),
        "dsa_w_o": nrm((n_b, DSA_QKV, D), DSA_QKV ** -0.5),
        "ffn_norm": gain((DEPTH, D)),
        "ffn_w_up": nrm((DEPTH, D, 2 * F), D ** -0.5),
        "ffn_conv_w": nrm((DEPTH, CONV_WIDTH, 2 * F), CONV_WIDTH ** -0.5),
        "ffn_conv_b": nrm((DEPTH, 2 * F), 0.02),
        "ffn_w_down": nrm((DEPTH, F, D), F ** -0.5),
        "final_norm": gain((D,)),
    }

def second_block(x, meta_tokens, da_norm, da_w_qkv, da_lambda_q1, da_lambda_k1,
              da_lambda_q2, da_lambda_k2, da_subln, da_w_o, dsa_norm, dsa_w_in,
              dsa_idx_k_norm, dsa_w_o, ffn_norm, ffn_w_up, ffn_conv_w, ffn_conv_b,
              ffn_w_down, final_norm):
    B, L, D = x.shape
    T = L + N_META
    T_pad = ((T + BLOCK_Q - 1) // BLOCK_Q) * BLOCK_Q
    meta = jnp.broadcast_to(meta_tokens[None].astype(x.dtype), (B, N_META, D))
    h = jnp.concatenate([meta, x], axis=1)
    h = jnp.pad(h, ((0, 0), (0, T_pad - T), (0, 0)))
    cos, sin = rope_tables_2(T_pad, ROPE_DIM_2)
    for i in range(DEPTH):
        j = i // 2
        if i % 2 == 0:
            lambda_init = 0.8 - 0.6 * math.exp(-0.3 * i)
            h = h + diff_attention(rms_norm(h, da_norm[j]), da_w_qkv[j],
                                   da_lambda_q1[j], da_lambda_k1[j],
                                   da_lambda_q2[j], da_lambda_k2[j],
                                   da_subln[j], da_w_o[j], cos, sin, lambda_init)
        else:
            h = h + dsa_attention(rms_norm(h, dsa_norm[j]), dsa_w_in[j],
                                  dsa_idx_k_norm[j], dsa_w_o[j], cos, sin, L)
        h = h + conv_ffn(rms_norm(h, ffn_norm[i]), ffn_w_up[i], ffn_conv_w[i],
                         ffn_conv_b[i], ffn_w_down[i])
    h = rms_norm(h, final_norm)
    return h[:, N_META:N_META + L]


def setup_inputs(seed=0):
    out = dict(first_inputs(seed))
    for name, value in second_inputs(seed + 1).items():
        if name != "x":
            out[name + "_2"] = value
    return out


def reference(
    x, positions, pre_norm, post_norm, ssm_w_in, ssm_conv_w, ssm_conv_b, ssm_dt_bias, ssm_a_log,
    ssm_d, ssm_gate_norm, ssm_w_out, att_w_in, att_sinks, att_w_out, meta_tokens_2, da_norm_2,
    da_w_qkv_2, da_lambda_q1_2, da_lambda_k1_2, da_lambda_q2_2, da_lambda_k2_2, da_subln_2,
    da_w_o_2, dsa_norm_2, dsa_w_in_2, dsa_idx_k_norm_2, dsa_w_o_2, ffn_norm_2, ffn_w_up_2,
    ffn_conv_w_2, ffn_conv_b_2, ffn_w_down_2, final_norm_2,
):
    x = first_block(
        x, positions, pre_norm, post_norm, ssm_w_in, ssm_conv_w, ssm_conv_b, ssm_dt_bias,
        ssm_a_log, ssm_d, ssm_gate_norm, ssm_w_out, att_w_in, att_sinks, att_w_out,
    )
    return second_block(
        x, meta_tokens_2, da_norm_2, da_w_qkv_2, da_lambda_q1_2, da_lambda_k1_2, da_lambda_q2_2,
        da_lambda_k2_2, da_subln_2, da_w_o_2, dsa_norm_2, dsa_w_in_2, dsa_idx_k_norm_2,
        dsa_w_o_2, ffn_norm_2, ffn_w_up_2, ffn_conv_w_2, ffn_conv_b_2, ffn_w_down_2,
        final_norm_2,
    )


_drawn_inputs = setup_inputs


def setup_inputs(seed=0):
    import zlib

    import numpy as np

    out = dict(_drawn_inputs(seed))
    spreads = {}
    factors = {'att_sinks': 5.256,
     'da_norm_2': 3.997,
     'da_lambda_q1_2': 8.0,
     'da_lambda_k1_2': 3.408,
     'da_lambda_q2_2': 2.951,
     'da_subln_2': 5.237,
     'dsa_norm_2': 6.074,
     'dsa_idx_k_norm_2': 8.0,
     'ffn_norm_2': 4.202,
     'ffn_conv_b_2': 4.296}
    for name, (base, spread) in spreads.items():
        noise = np.random.default_rng([zlib.crc32(name.encode()), seed]).standard_normal(out[name].shape)
        drawn = base * np.exp(spread * noise) if base else spread * noise
        out[name] = __import__('jax').numpy.asarray(drawn.astype(out[name].dtype))
    for name, factor in factors.items():
        out[name] = (out[name] * factor).astype(out[name].dtype)
    return out
```

```python
import concourse.bass as bass
from concourse import mybir
from contextlib import ExitStack
import numpy as np

F32 = mybir.dt.float32
BF16 = mybir.dt.bfloat16
I32 = mybir.dt.int32
ACT = mybir.ActivationFunctionType
ALU = mybir.AluOpType
AX = mybir.AxisListType

P = 128
DM = 1024
KT = DM // P
SEQ = 512
META = 16
T2 = SEQ + META
HALF = T2 // 2
NEG = -1e30
EPS = 1e-6
DI = 2048
GROUPS = 8
CHUNKS = SEQ // P
SSM_HEADS = 32
RPG = SSM_HEADS // GROUPS
KV = 4
FF = 2816
FT = FF // P
FK = FT // 2
TOPK = 128
TILES = [(a, min(P, T2 - a)) for a in range(0, T2, P)]
ACCEPT = 0.2

V_PRE, V_POST, V_GATE, V_CB = 0, 16, 32, 48
V_DA, V_DSA, V_FFN, V_FIN, V_SUB, V_IDX = 80, 88, 96, 112, 120, 121
V_CW = P
V_ROWS = [122, 128, 88, 88, 88, 88]


def constants():
    eye = np.eye(P, dtype=np.float32)
    ones = np.ones((P, P), np.float32)
    tri = np.triu(ones)
    rot1, rot2 = np.zeros((P, P), np.float32), np.zeros((P, P), np.float32)
    for m in range(P):
        b, d = m - m % 64, m % 64
        if d < 8:
            rot1[b + d + 8, m] = -1
        elif d < 16:
            rot1[b + d - 8, m] = 1
        if d < 32:
            rot2[b + d + 32, m] = -1
        else:
            rot2[b + d - 32, m] = 1
    causal = np.where(tri.T > 0, 0, NEG).astype(np.float32)
    before = np.where(np.arange(P)[None] > np.arange(P)[:, None], 0, NEG).astype(np.float32)
    d = np.arange(P) % 64
    inv1 = np.float32(500000.0) ** (-(2 * (d % 8)).astype(np.float32) / np.float32(16))
    inv1 = np.where(d < 16, inv1, 0).astype(np.float32)[:, None]
    inv2 = (np.float32(10000.0) ** (-(2 * (d % 32)).astype(np.float32) / np.float32(64))).astype(np.float32)
    ang = (np.arange(T2, dtype=np.float32)[None] * inv2[:, None]).astype(np.float32)
    cos2, sin2 = np.cos(ang).astype(np.float32), np.sin(ang).astype(np.float32)
    return np.concatenate([eye, ones, tri, rot1, rot2, before, causal, cos2, sin2, inv1], axis=1)


def wait(eng, sem, value):
    if not isinstance(value, int) or value > 0:
        eng.wait_ge(sem, value)


class Steps:

    def __init__(self, sem):
        self.sem, self.per, self.base, self.k = sem, 0, 0, 0

    def begin(self, i):
        self.base, self.k = i * self.per, 0

    def mark(self, ins):
        ins.then_inc(self.sem, 1)
        self.k += 1

    def settle(self, eng):
        eng.wait_ge(self.sem, self.base + self.k)

    def end(self):
        self.per = self.per or self.k
        assert self.per == self.k


class Stream:

    def __init__(self, iterations, units, kt, source, dmas=1):
        self.iterations, self.units, self.kt, self.source, self.dmas = iterations, units, kt, source, dmas


class Core:
    def __init__(self, nc, a, out, ctx):
        self.nc, self.a, self.out, self.ctx = nc, a, out, ctx
        sb = self.sb
        self.SLOTS = 6
        self.ring = sb("ring", [P, self.SLOTS, FK * P])
        self.res = sb("res", [P, KT, T2])
        self.h = sb("h", [P, KT, T2])
        self.wide = sb("wide", [P, FT, T2])
        self.cst = sb("cst", [P, 7 * P + 2 * T2 + 1])
        c = self.cst
        self.ident, self.ones, self.tri = c[:, 0:P], c[:, P:2 * P], c[:, 2 * P:3 * P]
        self.rot1, self.rot2 = c[:, 3 * P:4 * P], c[:, 4 * P:5 * P]
        self.maskf = c[:, 5 * P:7 * P]
        self.cos2, self.sin2 = c[:, 7 * P:7 * P + T2], c[:, 7 * P + T2:7 * P + 2 * T2]
        self.inv1 = c[:, 7 * P + 2 * T2:7 * P + 2 * T2 + 1]
        self.identb = sb("identb", [P, P], BF16)
        self.maskb = sb("maskb", [P, 2 * P], BF16)
        self.cos1, self.sin1 = sb("cos1", [P, SEQ]), sb("sin1", [P, SEQ])
        self.vec = sb("vec", [P, 6 * P])
        self.eps = sb("eps", [P, 1])
        self.sub8 = sb("sub8", [P, 1])
        self.neglam = sb("neglam", [P, 1])
        self.drow = sb("drow", [P, 4, SSM_HEADS])
        self.dexp = sb("dexp", [P, 16])
        self.nsink = sb("nsink", [P, 16])
        self.wdt = sb("wdt", [P, KT, SSM_HEADS])
        self.ps = ctx.enter_context(nc.psum_tensor("ps", [P, 8, 512], F32))
        self.loaded = [self.sem(f"weights_loaded{s}") for s in range(self.SLOTS)]
        self.granted = self.sem("refills_granted")
        self.loads = [0] * self.SLOTS
        self.norm_sems = [self.sem("norm_" + x) for x in ("squares", "summed", "rstd", "steps")]
        self.norm_base = [0, 0, 0, 0]

    def sb(self, name, shape, dt=F32, ctx=None):
        return (ctx or self.ctx).enter_context(self.nc.sbuf_tensor(name, shape, dt))

    def sem(self, name):
        return self.ctx.enter_context(self.nc.semaphore(name))

    def col(self, c):
        return self.vec[:, c:c + 1] if isinstance(c, int) else self.vec[:, bass.ds(c, 1)]

    def slot(self, u, kt):
        return self.ring[:, u, 0:kt * P].rearrange("p (k n) -> p k n", k=kt)

    def load(self, sp, st, i, u, done=None, value=0):
        if done is not None:
            sp.wait_ge(done, value)
            sp.sem_inc(self.granted, 1)
        for c0, n, w, r0, c in st.source(i, u):
            sp.dma_start(self.slot(u, st.kt)[:, :, c0:c0 + n], cols(w, r0, st.kt, c, n)).then_inc(self.loaded[u], 16)

    def start_stream(self, st):
        st.base = list(self.loads)
        for u in range(st.units):
            self.loads[u] += 16 * st.dmas * st.iterations

    def weights_ready(self, pe, st, i, u):
        pe.wait_ge(self.loaded[u], st.base[u] + 16 * st.dmas * (i + 1))

    def stream(self, sp, st, nxt, done, per_iteration, of_unit):
        def refill(i):
            for u in range(st.units):
                self.load(sp, st, i, u, done, per_iteration * (i - 1) + of_unit(u))
        if st.iterations > 1:
            with sp.Fori(1, st.iterations) as i:
                refill(i)
        if nxt is not None:
            for u in range(nxt.units):
                if u < st.units:
                    sp.wait_ge(done, per_iteration * (st.iterations - 1) + of_unit(u))
                self.load(sp, nxt, 0, u)


def cols(w, r0, kt, c, n=P):
    return w[r0:r0 + kt * P, bass.ds(c, n)].rearrange("(k p) n -> p k n", p=P)


def both(ap):
    return ap.rearrange("p (a n) -> p a n", a=2)


def halves(T):
    return [(0, SEQ)] if T == SEQ else [(0, HALF), (HALF, HALF)]


def setup(k, first):
    nc, a, ps = k.nc, k.a, k.ps
    with ExitStack() as ctx:
        def sb(n, s, d=F32):
            return k.sb(n, s, d, ctx)
        xin, meta = sb("xin", [P, 4, DM]), sb("metain", [META, DM])
        stage = sb("stage", [P, 6, P])
        posi, ang, turns = sb("posi", [P, SEQ], I32), sb("ang", [P, SEQ]), sb("turns", [P, SEQ])
        lam = sb("lam", [P, 4, 64])
        lprod, lsum = sb("lprod", [P, 2, 64]), sb("lsum", [P, 2])
        s_cst, s_x, s_row, s_small = k.sem("const_loaded"), k.sem("x_loaded"), k.sem("rows_loaded"), k.sem("small_loaded")
        s_xt, s_xfree = k.sem("x_transposed"), k.sem("x_stored")
        s_vt, s_v, s_a, s_pos = k.sem("vec_transposed"), k.sem("setup_vector"), k.sem("setup_scalar"), k.sem("pos_loaded")
        const = nc.inline_tensor(constants(), name="shape_constants").ap()
        rows = []

        def put(tile, r, src, n, w=P, c=0):
            rows.append((stage[r:r + n, tile, c:c + w], src))
        for l in range(2):
            put(0, V_PRE + 8 * l, a["pre_norm"][l].rearrange("(r c) -> r c", c=P), 8)
            put(0, V_POST + 8 * l, a["post_norm"][l].rearrange("(r c) -> r c", c=P), 8)
            put(0, V_FFN + 8 * l, a["ffn_norm_2"][l].rearrange("(r c) -> r c", c=P), 8)
            w = a["ffn_conv_w_2"][l].rearrange("j (r c) -> (j r) c", c=P)
            put(2 + 2 * l, 0, w[0:4 * FT], 4 * FT)
            put(3 + 2 * l, 0, w[4 * FT:6 * FT], 2 * FT)
            put(3 + 2 * l, 2 * FT, a["ffn_conv_b_2"][l].rearrange("(r c) -> r c", c=P), 2 * FT)
        put(0, V_GATE, a["ssm_gate_norm"][0].rearrange("(r c) -> r c", c=P), 16)
        put(0, V_CB, a["ssm_conv_b"][0].rearrange("(r c) -> r c", c=P), 32)
        put(0, V_DA, a["da_norm_2"][0].rearrange("(r c) -> r c", c=P), 8)
        put(0, V_DSA, a["dsa_norm_2"][0].rearrange("(r c) -> r c", c=P), 8)
        put(0, V_FIN, a["final_norm_2"].rearrange("(r c) -> r c", c=P), 8)
        put(0, V_SUB, a["da_subln_2"], 1)
        put(0, V_IDX, a["dsa_idx_k_norm_2"], 1, 64)
        put(0, V_IDX, a["dsa_idx_k_norm_2"], 1, 64, 64)
        put(1, 0, a["ssm_conv_w"][0].rearrange("j (r c) -> (j r) c", c=P), 4 * 32)
        small = [(k.drow[:, j, :], a[n].to_broadcast([P, SSM_HEADS]))
                 for j, n in enumerate(["ssm_d", "ssm_dt_bias", "ssm_a_log"])]
        small += [(k.nsink[:], a["att_sinks"].to_broadcast([P, 16]))]
        small += [(lam[:, j, :], a[n].to_broadcast([P, 64]))
                  for j, n in enumerate(["da_lambda_q1_2", "da_lambda_q2_2", "da_lambda_k1_2", "da_lambda_k2_2"])]

        with nc.Block() as block:
            @block.sync
            def _(sp):
                sp.dma_start(k.cst[:], const).then_inc(s_cst, 16)
                sp.dma_start(xin[:], a["x"][0].rearrange("(t p) d -> p t d", p=P)).then_inc(s_x, 16)
                sp.dma_start(meta[:], a["meta_tokens_2"]).then_inc(s_x, 16)
                for u in range(first.units):
                    k.load(sp, first, 0, u)

            @block.gpsimd
            def _(pool):
                pool.dma_start(k.wdt[:], cols(a["ssm_w_in"][0], 0, KT, 6144, SSM_HEADS)).then_inc(s_small, 16)
                for dst, src in small:
                    pool.dma_start(dst, src).then_inc(s_small, 16)
                pool.dma_start(posi[:], a["positions"].to_broadcast([P, SEQ])).then_inc(s_pos, 16)
                pool.wait_ge(s_small, 16 * (1 + len(small)))
                pool.wait_ge(s_pos, 16)

            @block.tensor
            def _(pe):
                pe.wait_ge(s_cst, 16)
                pe.wait_ge(s_x, 32)
                for f in range(KT):
                    wait(pe, s_xfree, f - 3)
                    for t in range(4):
                        m = nc.tensor.transpose(ps[:, f % 4, t * P:(t + 1) * P], xin[:, t, f * P:(f + 1) * P], k.ident)
                    m.then_inc(s_xt, 1)
                for f in range(KT):
                    m = nc.tensor.transpose(ps[:, 4, f * META:(f + 1) * META], meta[:, f * P:(f + 1) * P], k.ident[0:META, 0:META])
                m.then_inc(s_xt, 1)
                pe.wait_ge(s_row, 16 * len(rows))
                for t, n in enumerate(V_ROWS):
                    m = nc.tensor.transpose(ps[:, 5 + t // 3, (t % 3) * P:(t % 3) * P + n], stage[0:n, t, :], k.ident[0:n, 0:n])
                m.then_inc(s_vt, 1)

            @block.scalar
            def _(act):
                for dst, src in rows:
                    act.dma_start(dst, src).then_inc(s_row, 16)
                act.wait_ge(s_v, 1)
                nc.scalar.activation(k.drow[:, 3, :], k.drow[:, 2, :], ACT.Exp).then_inc(s_a, 1)
                nc.scalar.activation(lsum[:], lsum[:], ACT.Exp).then_inc(s_a, 1)
                act.wait_ge(s_v, 3)
                nc.scalar.activation(k.sin1[:], ang[:], ACT.Sin).then_inc(s_a, 1)
                nc.scalar.activation(k.cos1[:], turns[:], ACT.Sin).then_inc(s_a, 1)

            @block.vector
            def _(dve):
                steps = Steps(k.sem("setup_steps"))

                def do(ins):
                    steps.mark(ins)
                    steps.settle(dve)
                do(nc.vector.memset(k.eps[:], EPS))
                dve.wait_ge(s_small, 16 * (1 + len(small)))
                do(nc.vector.tensor_tensor(lprod[:], lam[:, 0:2, :], lam[:, 2:4, :], ALU.mult))
                nc.vector.reduce_sum(lsum[:], lprod[:], AX.X).then_inc(s_v, 1)
                for b in range(2):
                    do(nc.vector.tensor_copy(k.dexp[64 * b:64 * b + 64, :],
                                             k.drow[64 * b:64 * b + 64, 0, :].rearrange("p (f b) -> p b f", b=2)[:, b, :]))
                do(nc.vector.tensor_scalar(k.nsink[:], k.nsink[:], -1.0, None, ALU.mult))
                dve.wait_ge(s_cst, 16)
                dve.wait_ge(s_pos, 16)
                do(nc.vector.tensor_copy(ang[:], posi[:]))
                do(nc.vector.tensor_scalar(ang[:], ang[:], k.inv1, None, ALU.mult))
                do(nc.vector.tensor_scalar(turns[:], ang[:], float(1 / (2 * np.pi)), 12582912.0, ALU.mult, ALU.add))
                do(nc.vector.tensor_scalar(turns[:], turns[:], 12582912.0, None, ALU.subtract))
                c1 = 6.28125
                c2 = float(np.float32(int((2 * np.pi - c1) * 2 ** 21) / 2 ** 21))
                c3 = float(np.float32(2 * np.pi - c1 - c2))
                for c in (c1, c2, c3):
                    do(nc.vector.scalar_tensor_tensor(ang[:], turns[:], -c, ang[:], ALU.mult, ALU.add))
                pi = float(np.nextafter(np.float32(np.pi), np.float32(0)))
                nc.vector.tensor_scalar(ang[:], ang[:], -pi, pi, ALU.max, ALU.min).then_inc(s_v, 1)
                dve.wait_ge(s_v, 2)
                do(nc.vector.scalar_tensor_tensor(turns[:], ang[:], -1.0, ang[:], ALU.mult, ALU.max))
                nc.vector.tensor_scalar(turns[:], turns[:], -1.0, float(np.pi / 2), ALU.mult, ALU.add).then_inc(s_v, 1)
                do(nc.vector.tensor_copy(k.identb[:], k.ident))
                do(nc.vector.tensor_copy(k.maskb[:], k.maskf))
                for f in range(KT):
                    dve.wait_ge(s_xt, f + 1)
                    nc.vector.tensor_copy(k.res[:, f, META:T2], ps[:, f % 4, :]).then_inc(s_xfree, 1)
                dve.wait_ge(s_xt, KT + 1)
                do(nc.vector.tensor_copy(k.res[:, :, 0:META], ps[:, 4, 0:KT * META].rearrange("p (f t) -> p f t", f=KT)))
                dve.wait_ge(s_vt, 1)
                for t, n in enumerate(V_ROWS):
                    do(nc.vector.tensor_copy(k.vec[:, t * P:t * P + n], ps[:, 5 + t // 3, (t % 3) * P:(t % 3) * P + n]))
                do(nc.vector.tensor_scalar(k.sub8[:], k.col(V_SUB), 1.0 - ACCEPT, None, ALU.mult))
                dve.wait_ge(s_a, 4)
                do(nc.vector.tensor_scalar(k.drow[:, 3, :], k.drow[:, 3, :], -1.0, None, ALU.mult))
                do(nc.vector.tensor_tensor(k.neglam[:], lsum[:, 1:2], lsum[:, 0:1], ALU.subtract))
                do(nc.vector.tensor_scalar(k.neglam[:], k.neglam[:], -ACCEPT, None, ALU.add))


def norm(k, name, src, kt, T, gain, dst, add=False):
    nc, ps = k.nc, k.ps
    width = float(kt * P)
    with ExitStack() as ctx:
        sq = k.sb(name + "_sq", [P, 4, T], F32, ctx)
        rstd = k.sb(name + "_rstd", [P, T], F32, ctx)
        lnv = k.sb(name + "_ln", [P, T], F32, ctx)
        tmp = k.sb(name + "_tmp", [P, 2, T], F32, ctx) if add else None
        s_sq, s_used, s_r, s_t = k.norm_sems
        b_sq, b_used, b_r, b_t = k.norm_base
        for x, more in enumerate((kt, kt, 2, (2 if add else 1) * kt)):
            k.norm_base[x] += more
        hs = halves(T)
        total = ps[:, 6, :] if T == SEQ else ps[:, 6:8, 0:HALF]

        def view(x):
            return x if T == SEQ else both(x)
        with nc.Block() as block:
            @block.scalar
            def _(act):
                for f in range(kt):
                    if f >= 4:
                        act.wait_ge(s_used, b_used + f - 3)
                    nc.scalar.activation(sq[:, f % 4, :], src(f), ACT.Square).then_inc(s_sq, 1)
                act.wait_ge(s_used, b_used + kt)
                nc.scalar.activation(view(lnv[:]), total, ACT.Ln, scale=1.0 / width, bias=k.eps[:]).then_inc(s_r, 1)
                act.wait_ge(s_r, b_r + 1)
                nc.scalar.activation(rstd[:], lnv[:], ACT.Exp, scale=-0.5).then_inc(s_r, 1)

            @block.tensor
            def _(pe):
                for f in range(kt):
                    pe.wait_ge(s_sq, b_sq + f + 1)
                    for b, (c, n) in enumerate(hs):
                        m = nc.tensor.matmul(ps[:, 6 + b, 0:n], k.ones, sq[:, f % 4, c:c + n], start=f == 0, stop=f == kt - 1)
                    m.then_inc(s_used, 1)

            @block.vector
            def _(dve):
                dve.wait_ge(s_r, b_r + 2)
                for f in range(kt):
                    if add:
                        if f >= 2:
                            dve.wait_ge(s_t, b_t + 2 * f - 2)
                        nc.vector.scalar_tensor_tensor(tmp[:, f % 2, :], src(f), k.col(gain + f), rstd[:], ALU.mult, ALU.mult).then_inc(s_t, 1)
                        dve.wait_ge(s_t, b_t + 2 * f + 1)
                        nc.vector.tensor_tensor(dst(f), dst(f), tmp[:, f % 2, :], ALU.add).then_inc(s_t, 1)
                    else:
                        nc.vector.scalar_tensor_tensor(dst(f), src(f), k.col(gain + f), rstd[:], ALU.mult, ALU.mult).then_inc(s_t, 1)


def ssm_dt(k, dts):
    nc, ps = k.nc, k.ps
    with ExitStack() as ctx:
        n = CHUNKS * SSM_HEADS

        def sb(x):
            return k.sb("dt_" + x, [P, CHUNKS, SSM_HEADS], F32, ctx)
        raw, e, u, r, big = sb("raw"), sb("e"), sb("u"), sb("r"), sb("big")
        s_pe, s_act = k.sem("dt_products"), k.sem("dt_scalar")
        steps = Steps(k.sem("dt_steps"))
        with nc.Block() as block:
            @block.tensor
            def _(pe):
                for c in range(CHUNKS):
                    for f in range(KT):
                        m = nc.tensor.matmul(ps[:, 2, c * SSM_HEADS:(c + 1) * SSM_HEADS], k.h[:, f, c * P:(c + 1) * P],
                                             k.wdt[:, f, :], start=f == 0, stop=f == KT - 1)
                m.then_inc(s_pe, 1)
                pe.wait_ge(steps.sem, 13)
                a_all = dts[:, 0, :, :].rearrange("p c h -> p (c h)")
                nc.tensor.matmul(ps[:, 3, 0:n], k.tri, a_all, start=True, stop=True)
                nc.tensor.matmul(ps[:, 4, 0:n], k.ones, a_all, start=True, stop=True).then_inc(s_pe, 1)

            @block.scalar
            def _(act):
                act.wait_ge(steps.sem, 3)
                nc.scalar.activation(e[:], e[:], ACT.Exp, scale=-1.0).then_inc(s_act, 1)
                act.wait_ge(steps.sem, 4)
                nc.scalar.activation(big[:], u[:], ACT.Ln).then_inc(s_act, 1)
                act.wait_ge(steps.sem, 15)
                nc.scalar.activation(dts[:, 3, :, :], e[:], ACT.Exp).then_inc(s_act, 1)
                nc.scalar.activation(dts[:, 4, :, :], ps[:, 4, 0:n].rearrange("p (c h) -> p c h", c=CHUNKS), ACT.Exp).then_inc(s_act, 1)

            @block.vector
            def _(dve):
                def do(ins):
                    steps.mark(ins)
                    steps.settle(dve)

                def head(q):
                    return k.drow[:, q:q + 1, :].to_broadcast([P, CHUNKS, SSM_HEADS])
                v = nc.vector
                dve.wait_ge(s_pe, 1)
                do(v.tensor_tensor(raw[:], ps[:, 2, 0:n].rearrange("p (c h) -> p c h", c=CHUNKS), head(1), ALU.add))
                do(v.tensor_scalar(r[:], raw[:], -1.0, None, ALU.mult))
                do(v.tensor_tensor(e[:], raw[:], r[:], ALU.max))
                dve.wait_ge(s_act, 1)
                do(v.tensor_scalar(u[:], e[:], 1.0, None, ALU.add))
                dve.wait_ge(s_act, 2)
                do(v.tensor_scalar(u[:], u[:], 1.0, None, ALU.subtract))
                do(v.tensor_scalar(r[:], u[:], 1e-30, None, ALU.max))
                do(v.reciprocal(r[:], r[:]))
                do(v.tensor_tensor(r[:], r[:], big[:], ALU.mult))
                do(v.scalar_tensor_tensor(r[:], u[:], 0.0, r[:], ALU.is_le, ALU.add))
                do(v.tensor_tensor(r[:], r[:], e[:], ALU.mult))
                do(v.scalar_tensor_tensor(dts[:, 2, :, :], raw[:], 0.0, r[:], ALU.max, ALU.add))
                do(v.tensor_copy(u[:], dts[:, 2, :, :]))
                do(v.tensor_tensor(dts[:, 0, :, :], u[:], head(3), ALU.mult))
                dve.wait_ge(s_pe, 2)
                pre, tot = (ps[:, b, 0:n].rearrange("p (c h) -> p c h", c=CHUNKS) for b in (3, 4))
                do(v.tensor_copy(dts[:, 1, :, :], pre))
                do(v.tensor_tensor(e[:], tot, dts[:, 1, :, :], ALU.subtract))
                steps.end()


def ssm(k, st, nxt, dts):
    nc, ps = k.nc, k.ps
    v = nc.vector
    with ExitStack() as ctx:
        def sb(n, s, d=F32):
            return k.sb("ssm_" + n, s, d, ctx)
        u, cv = sb("u", [P, 4, 3 + SEQ]), sb("conv", [P, 4, SEQ])
        zs, gs = sb("z", [P, 2, SEQ]), sb("group", [P, 5 * CHUNKS, RPG])
        xt, xd, bt = sb("xdt", [P, 2 * P]), sb("xend", [P, 2 * P]), sb("btok", [P, P])
        cbm, seg, mm = sb("cb", [P, P]), sb("seg", [P, RPG, P]), sb("m", [P, RPG, P])
        ebc, cs = sb("ebc", [P, RPG, P]), sb("cs", [P, RPG, P])
        hs, ht, yg = sb("state", [P, 2 * P]), sb("statet", [P, 2 * P]), sb("yg", [P, 2, SEQ])
        sem = {x: k.sem("ssm_" + x) for x in (
            "lin_done", "lin_free", "conv", "silu", "group", "tr", "cb", "bc", "xt", "xd", "cbm", "seg", "m",
            "bt", "ebc", "dec", "cs", "y", "state", "gate")}
        steps = Steps(k.sem("ssm_steps"))
        TR, CB, BC, Y, S = ps[:, 2, :], ps[:, 3, :], ps[:, 4, :], (ps[:, 5, :], ps[:, 6, :]), ps[:, 7, :]

        def scal(q, c, r=None):
            return gs[:, q * CHUNKS + c, :] if r is None else gs[:, q * CHUNKS + c, r:r + 1]

        with nc.Block() as block:
            @block.sync
            def _(sp):
                k.stream(sp, st, nxt, sem["lin_done"], 6, lambda x: x + 1)

            @block.tensor
            def _(pe):
                def piece(i, p):
                    k.weights_ready(pe, st, i, p)
                    wait(pe, sem["lin_free"], 6 * i + p - 1)
                    w = k.slot(p, KT)
                    for f in range(KT):
                        m = nc.tensor.matmul(ps[:, p % 2, :], w[:, f, :], k.h[:, f, 0:SEQ], start=f == 0, stop=f == KT - 1)
                    m.then_inc(sem["lin_done"], 1)

                def prep(s, c):
                    n, t = 4 * s + c, slice(c * P, (c + 1) * P)
                    wait(pe, sem["silu"], 4 * s + 4)
                    wait(pe, sem["xt"], n)
                    wait(pe, sem["bt"], n)
                    for q in range(3):
                        m = nc.tensor.transpose(TR[:, q * P:(q + 1) * P], cv[:, q, t], k.ident)
                    m.then_inc(sem["tr"], 1)
                    wait(pe, sem["cbm"], n)
                    nc.tensor.matmul(CB[:, 0:P], cv[:, 2, t], cv[:, 3, t], start=True, stop=True).then_inc(sem["cb"], 1)
                    wait(pe, sem["ebc"], 3 * s + max(c - 1, 0))
                    wait(pe, sem["seg"], n)
                    for r in range(RPG):
                        m = nc.tensor.matmul(BC[:, r * P:(r + 1) * P], scal(0, c, r).to_broadcast([P, P]), k.tri, start=True, stop=True)
                    m.then_inc(sem["bc"], 1)

                def out(s, c):
                    n = 4 * s + c
                    wait(pe, sem["m"], n + 1)
                    if c == 0:
                        wait(pe, sem["gate"], 2 * s)
                    else:
                        wait(pe, sem["state"], 3 * s + c)
                        wait(pe, sem["cs"], 3 * s + c)
                    for r in range(RPG):
                        o = Y[r // 2][64 * (r % 2):64 * (r % 2) + 64, c * P:(c + 1) * P]
                        m = nc.tensor.matmul(o, xt[:, 64 * r:64 * r + 64], mm[:, r, :], start=True, stop=c == 0)
                        if c:
                            m = nc.tensor.matmul(o, hs[:, 64 * r:64 * r + 64], cs[:, r, :], start=False, stop=True)
                    if c < CHUNKS - 1:
                        wait(pe, sem["bt"], n + 1)
                        wait(pe, sem["xd"], n + 1)
                        m = nc.tensor.matmul(S[:, 0:2 * P], bt[:], xd[:], start=True, stop=True)
                    m.then_inc(sem["y"], 1)

                def step(i, lin=True, scan=True):
                    for p in range(6):
                        if lin:
                            piece(i, p)
                        if scan:
                            if 1 <= p <= 4:
                                out(i - 1, p - 1)
                            if p <= 3:
                                prep(i - 1, p)
                step(0, scan=False)
                step(1)
                with pe.Fori(2, GROUPS) as i:
                    step(i)
                step(GROUPS, lin=False)

            @block.scalar
            def _(act):
                def evict(i, p):
                    act.wait_ge(sem["lin_done"], 6 * i + p + 1)
                    if p < 4:
                        wait(act, sem["conv"], 4 * i - 3 + p if not isinstance(i, int) or i else 0)
                        nc.scalar.activation(u[:, p, 3:3 + SEQ], ps[:, p % 2, :], ACT.Copy).then_inc(sem["lin_free"], 1)
                    else:
                        wait(act, sem["gate"], 2 * i)
                        nc.scalar.activation(zs[:, p - 4, :], ps[:, p % 2, :], ACT.Silu).then_inc(sem["lin_free"], 1)

                def chunk(s, c):
                    n = 4 * s + c
                    act.wait_ge(sem["xt"], n + 1)
                    wait(act, sem["y"], n)
                    nc.scalar.activation(bt[:], TR[:, 2 * P:3 * P], ACT.Copy).then_inc(sem["bt"], 1)
                    act.wait_ge(sem["seg"], n + 1)
                    nc.scalar.activation(seg[:], seg[:], ACT.Exp).then_inc(sem["dec"], 1)
                    if c:
                        wait(act, sem["cs"], 3 * s + c - 1)
                        nc.scalar.activation(ebc[:].rearrange("p r l -> p (r l)"), BC, ACT.Exp).then_inc(sem["ebc"], 1)

                def step(i, lin=True, scan=True):
                    if scan:
                        for q in range(4):
                            act.wait_ge(sem["conv"], 4 * (i - 1) + q + 1)
                            nc.scalar.activation(cv[:, q, :], cv[:, q, :], ACT.Silu).then_inc(sem["silu"], 1)
                    for p in range(6):
                        if lin:
                            evict(i, p)
                        if scan and p < 4:
                            chunk(i - 1, p)
                step(0, scan=False)
                step(1)
                with act.Fori(2, GROUPS) as i:
                    step(i)
                step(GROUPS, lin=False)

            @block.gpsimd
            def _(pool):
                def scaled_c(s):
                    for c in range(1, CHUNKS):
                        pool.wait_ge(sem["ebc"], 3 * s + c)
                        wait(pool, sem["y"], 4 * s + c)
                        nc.gpsimd.tensor_tensor(cs[:], ebc[:], cv[:, 3:4, c * P:(c + 1) * P].to_broadcast([P, RPG, P]),
                                                ALU.mult).then_inc(sem["cs"], 1)
                scaled_c(0)
                with pool.Fori(1, GROUPS) as s:
                    scaled_c(s)

            @block.vector
            def _(dve):
                def do(ins):
                    steps.mark(ins)
                    steps.settle(dve)

                def conv(s, q):
                    tile = (2 * s, 2 * s + 1, 16 + s, 24 + s)[q]
                    dve.wait_ge(sem["lin_free"], 6 * s + q + 1)
                    acc = cv[:, q, :]
                    do(v.tensor_scalar(acc, u[:, q, 0:SEQ], k.col(V_CW + tile), k.col(V_CB + tile), ALU.mult, ALU.add))
                    for j in range(1, 4):
                        ins = v.scalar_tensor_tensor(acc, u[:, q, j:j + SEQ], k.col(V_CW + 32 * j + tile), acc, ALU.mult, ALU.add)
                        if j < 3:
                            do(ins)
                        else:
                            ins.then_inc(sem["conv"], 1)

                def chunk(s, c):
                    n, b4 = 4 * s + c, [P, RPG, 64]
                    dve.wait_ge(sem["tr"], n + 1)
                    wait(dve, sem["y"], n)
                    x4 = xt[:].rearrange("p (r d) -> p r d", r=RPG)
                    v.tensor_tensor(x4, TR[:, 0:2 * P].rearrange("p (r d) -> p r d", r=RPG),
                                    scal(2, c).unsqueeze(2).to_broadcast(b4), ALU.mult).then_inc(sem["xt"], 1)
                    dve.wait_ge(sem["cb"], n + 1)
                    v.tensor_tensor(cbm[:], CB[:, 0:P], k.tri, ALU.mult).then_inc(sem["cbm"], 1)
                    dve.wait_ge(sem["xt"], n + 1)
                    v.tensor_tensor(xd[:].rearrange("p (r d) -> p r d", r=RPG), x4,
                                    scal(3, c).unsqueeze(2).to_broadcast(b4), ALU.mult).then_inc(sem["xd"], 1)
                    dve.wait_ge(sem["bc"], n + 1)
                    for r in range(RPG):
                        ins = v.tensor_scalar(seg[:, r, :], BC[:, r * P:(r + 1) * P], scal(1, c, r), 0.0, ALU.subtract, ALU.min)
                    ins.then_inc(sem["seg"], 1)
                    dve.wait_ge(sem["dec"], n + 1)
                    dve.wait_ge(sem["cbm"], n + 1)
                    v.tensor_tensor(mm[:], seg[:], cbm[:].unsqueeze(1).to_broadcast([P, RPG, P]), ALU.mult).then_inc(sem["m"], 1)
                    if c == CHUNKS - 1:
                        return
                    if c:
                        do(v.tensor_tensor(ht[:].rearrange("p (r d) -> p r d", r=RPG), hs[:].rearrange("p (r d) -> p r d", r=RPG),
                                           scal(4, c).unsqueeze(2).to_broadcast(b4), ALU.mult))
                        dve.wait_ge(sem["y"], n + 1)
                        v.tensor_tensor(hs[:], ht[:], S[:, 0:2 * P], ALU.add).then_inc(sem["state"], 1)
                    else:
                        dve.wait_ge(sem["y"], n + 1)
                        v.tensor_copy(hs[:], S[:, 0:2 * P]).then_inc(sem["state"], 1)
                    dve.wait_ge(sem["state"], 3 * s + c + 1)

                def gate(s):
                    dve.wait_ge(sem["y"], 4 * s + 4)
                    dve.wait_ge(sem["lin_free"], 6 * s + 6)
                    for j in range(2):
                        do(v.scalar_tensor_tensor(yg[:, j, :], cv[:, j, :], k.dexp[:, bass.ds(2 * s + j, 1)], Y[j], ALU.mult, ALU.add))
                        v.tensor_tensor(k.wide[:, bass.ds(2 * s + j, 1), 0:SEQ].rearrange("p a t -> p (a t)"), yg[:, j, :],
                                        zs[:, j, :], ALU.mult).then_inc(sem["gate"], 1)

                def step(s):
                    steps.begin(s)
                    do(v.tensor_copy(gs[:], dts[:].rearrange("p q c h -> p (q c) h")[:, :, bass.ds(RPG * s, RPG)]))
                    for q in range(4):
                        conv(s, q)
                    for c in range(CHUNKS):
                        chunk(s, c)
                    gate(s)
                    steps.end()
                v.memset(u[:, :, 0:3], 0.0).then_inc(sem["group"], 1)
                dve.wait_ge(sem["group"], 1)
                step(0)
                with dve.Fori(1, GROUPS) as s:
                    step(s)


def project(k, name, st, nxt, ksplit, rhs, T, store):
    nc, ps = k.nc, k.ps
    hs = halves(T)
    per = st.units // ksplit * len(hs)
    s_done, s_free = k.sem(name + "_done"), k.sem(name + "_free")
    with nc.Block() as block:
        @block.sync
        def _(sp):
            k.stream(sp, st, nxt, s_done, per, lambda u: (u // ksplit + 1) * len(hs))

        @block.tensor
        def _(pe):
            def step(i):
                for u in range(st.units):
                    tile, part = divmod(u, ksplit)
                    k.weights_ready(pe, st, i, u)
                    w = k.slot(u, st.kt)
                    for b, (c, n) in enumerate(hs):
                        q = tile * len(hs) + b
                        if part == 0:
                            wait(pe, s_free, per * i + q - 1)
                        for f in range(st.kt):
                            m = nc.tensor.matmul(ps[:, q % 2, 0:n], w[:, f, :], rhs(part * st.kt + f)[:, c:c + n],
                                                 start=part == 0 and f == 0, stop=part == ksplit - 1 and f == st.kt - 1)
                        if part == ksplit - 1:
                            m.then_inc(s_done, 1)
            step(0)
            with pe.Fori(1, st.iterations) as i:
                step(i)

        @block.vector
        def _(dve):
            with dve.Fori(0, st.iterations) as i:
                for q in range(per):
                    dve.wait_ge(s_done, per * i + q + 1)
                    tile, b = divmod(q, len(hs))
                    c, n = hs[b]
                    store(per // len(hs) * i + tile, c, n, ps[:, q % 2, 0:n]).then_inc(s_free, 1)


def swa(k, st, nxt):
    nc, ps = k.nc, k.ps
    v = nc.vector
    with ExitStack() as ctx:
        def sb(n, s, d=F32):
            return k.sb("swa_" + n, s, d, ctx)
        raw, rop = sb("raw", [P, 3, SEQ]), sb("roped", [P, 3, SEQ])
        vT, vt, gate = sb("vT", [P, SEQ]), sb("v", [P, 4, 64]), sb("gate", [P, 2 * KV, SEQ])
        t1, t2 = sb("t1", [P, SEQ]), sb("t2", [P, SEQ])
        p, pn, pt = sb("p", [P, 4, 2 * P]), sb("pn", [P, 4, 2 * P]), sb("pt", [P, 4, 2, P])
        mx, nm, den, es, rd = (sb(x, [P, 4]) for x in ("mx", "nm", "den", "es", "rd"))
        nsg = sb("nsg", [P, 4])
        sem = {x: k.sem("swa_" + x) for x in (
            "lin_done", "lin_free", "rot", "rope", "vtr", "v", "s", "nm", "exp", "es", "pn", "t", "pt", "pv", "out")}
        steps = Steps(k.sem("swa_steps"))
        S = ps[:, 2:4, :].rearrange("p b (x j) -> p (b x) j", x=2)
        PT = ps[:, 4:6, :].rearrange("p b (x j) -> p (b x) j", x=2)
        O = (ps[:, 6, :], ps[:, 7, :])
        order = (0, 2, 3)
        HEAD = (0, 2, 1, 3)

        with nc.Block() as block:
            @block.sync
            def _(sp):
                k.stream(sp, st, nxt, sem["lin_done"], 6, lambda x: x + 1)

            @block.tensor
            def _(pe):
                def piece(i, q):
                    k.weights_ready(pe, st, i, q)
                    wait(pe, sem["lin_free"], 6 * i + q - 1)
                    w = k.slot(q, KT)
                    for f in range(KT):
                        m = nc.tensor.matmul(ps[:, q % 2, :], w[:, f, :], k.h[:, f, 0:SEQ], start=f == 0, stop=f == KT - 1)
                    m.then_inc(sem["lin_done"], 1)

                def rot(s, q):
                    pe.wait_ge(sem["lin_free"], 6 * s + order[q] + 1)
                    if q == 0:
                        wait(pe, sem["pt"], 4 * s)
                    if q == 2:
                        pe.wait_ge(sem["rope"], 3 * s + 1)
                    nc.tensor.matmul(ps[:, 4 + q % 2, :], k.rot1, raw[:, q, :], start=True, stop=True).then_inc(sem["rot"], 1)

                def vtr(s):
                    pe.wait_ge(sem["lin_free"], 6 * s + 2)
                    wait(pe, sem["exp"], 16 * s)
                    for t in range(4):
                        m = nc.tensor.transpose(ps[:, 2, t * P:(t + 1) * P], vT[:, t * P:(t + 1) * P], k.ident)
                    m.then_inc(sem["vtr"], 1)

                def scores(s, n):
                    if n == 0:
                        pe.wait_ge(sem["v"], s + 1)
                        pe.wait_ge(sem["rope"], 3 * s + 3)
                    else:
                        pe.wait_ge(sem["exp"], 16 * s + 4 * n)
                    k0 = 0 if n else P
                    for x, r in enumerate(HEAD):
                        h = slice(64 * (r % 2), 64 * (r % 2) + 64)
                        nc.tensor.matmul(S[:, x, k0:2 * P], k.identb[:], k.maskb[:, k0:2 * P], start=True, stop=False)
                        m = nc.tensor.matmul(S[:, x, k0:2 * P], rop[h, 1 + r // 2, n * P:(n + 1) * P],
                                             rop[h, 0, (n - 1) * P + k0:(n + 1) * P], start=False, stop=True)
                    m.then_inc(sem["s"], 1)

                def trans(s, n):
                    pe.wait_ge(sem["pn"], 4 * s + n + 1)
                    wait(pe, sem["pt"], 4 * s + n)
                    for r in range(4):
                        for b in range(0 if n else 1, 2):
                            m = nc.tensor.transpose(PT[:, r, b * P:(b + 1) * P], pn[:, r, b * P:(b + 1) * P], k.ident)
                    m.then_inc(sem["t"], 1)

                def pv(s, n):
                    pe.wait_ge(sem["pt"], 4 * s + n + 1)
                    if n == 0:
                        wait(pe, sem["out"], 2 * s)
                    for x, r in enumerate(HEAD):
                        o = O[r // 2][64 * (r % 2):64 * (r % 2) + 64, n * P:(n + 1) * P]
                        for b in range(0 if n else 1, 2):
                            m = nc.tensor.matmul(o, vt[:, n - 1 + b, :], pt[:, x, b, :], start=b == 0 or not n, stop=b == 1)
                    m.then_inc(sem["pv"], 1)

                def step(i, lin=True, att=True):
                    s = i - 1
                    for q in range(6):
                        if att:
                            if q == 0:
                                rot(s, 0), rot(s, 1)
                            if q == 1:
                                rot(s, 2), vtr(s)
                            if q == 2:
                                scores(s, 0)
                            if q == 3:
                                trans(s, 0), scores(s, 1)
                            if q == 4:
                                pv(s, 0), trans(s, 1), scores(s, 2)
                            if q == 5:
                                pv(s, 1), trans(s, 2), scores(s, 3)
                        if lin:
                            piece(i, q)
                    if att:
                        pv(s, 2), trans(s, 3), pv(s, 3)
                step(0, att=False)
                step(1)
                with pe.Fori(2, KV) as i:
                    step(i)
                step(KV, lin=False)

            @block.scalar
            def _(act):
                def evict(i, q):
                    act.wait_ge(sem["lin_done"], 6 * i + q + 1)
                    src = ps[:, q % 2, :]
                    if q in order:
                        wait(act, sem["rope"], 3 * i - 2 + order.index(q) if not isinstance(i, int) or i else 0)
                        nc.scalar.activation(raw[:, order.index(q), :], src, ACT.Copy).then_inc(sem["lin_free"], 1)
                    elif q == 1:
                        wait(act, sem["vtr"], i)
                        nc.scalar.activation(vT[:], src, ACT.Copy).then_inc(sem["lin_free"], 1)
                    else:
                        nc.scalar.activation(gate[:, bass.ds(2 * i + q - 4, 1), :].rearrange("p a t -> p (a t)"), src, ACT.Silu).then_inc(sem["lin_free"], 1)

                def vtok(s):
                    act.wait_ge(sem["vtr"], s + 1)
                    wait(act, sem["pv"], 4 * s)
                    nc.scalar.activation(vt[:], ps[:, 2, :].rearrange("p (t d) -> p t d", t=4)[:, :, 0:64], ACT.Copy).then_inc(sem["v"], 1)

                def exps(s, n):
                    act.wait_ge(sem["nm"], 4 * s + n + 1)
                    wait(act, sem["pn"], 4 * s + n)
                    k0 = 0 if n else P
                    for r in range(4):
                        nc.scalar.activation(p[:, r, k0:2 * P], S[:, r, k0:2 * P], ACT.Exp, bias=nm[:, r:r + 1], scale=0.125,
                                             accum_out=den[:, r:r + 1]).then_inc(sem["exp"], 1)
                    nc.scalar.activation(es[:], es[:], ACT.Exp).then_inc(sem["es"], 1)

                def store_pt(s, n):
                    act.wait_ge(sem["t"], 4 * s + n + 1)
                    wait(act, sem["pv"], 4 * s + n)
                    b0 = 0 if n else 1
                    nc.scalar.activation(pt[:, :, b0:2, :], PT.rearrange("p r (b q) -> p r b q", b=2)[:, :, b0:2, :],
                                         ACT.Copy).then_inc(sem["pt"], 1)

                def step(i, lin=True, att=True):
                    s = i - 1
                    for q in range(6):
                        if att:
                            if q == 2:
                                vtok(s)
                                exps(s, 0)
                            if q >= 3:
                                store_pt(s, q - 3)
                                exps(s, q - 2)
                        if lin:
                            evict(i, q)
                    if att:
                        store_pt(s, 3)
                step(0, att=False)
                step(1)
                with act.Fori(2, KV) as i:
                    step(i)
                step(KV, lin=False)

            @block.vector
            def _(dve):
                def do(ins):
                    steps.mark(ins)
                    steps.settle(dve)

                def step(s):
                    steps.begin(s)
                    do(v.tensor_copy(nsg[:].rearrange("p (b f) -> p f b", b=2),
                                     k.nsink[:, bass.ds(4 * s, 4)].rearrange("p (f b) -> p f b", b=2)))
                    for q in range(3):
                        dve.wait_ge(sem["lin_free"], 6 * s + order[q] + 1)
                        do(v.tensor_tensor(t1[:], raw[:, q, :], k.cos1[:], ALU.mult))
                        dve.wait_ge(sem["rot"], 3 * s + q + 1)
                        do(v.tensor_tensor(t2[:], ps[:, 4 + q % 2, :], k.sin1[:], ALU.mult))
                        v.tensor_tensor(rop[:, q, :], t1[:], t2[:], ALU.add).then_inc(sem["rope"], 1)
                        dve.wait_ge(sem["rope"], 3 * s + q + 1)
                    for n in range(4):
                        k0 = 0 if n else P
                        dve.wait_ge(sem["s"], 4 * s + n + 1)
                        do(v.reduce_max(mx[:], S[:, :, k0:2 * P], AX.X))
                        do(v.scalar_tensor_tensor(nm[:], mx[:], -0.125, nsg[:], ALU.mult, ALU.min))
                        v.tensor_tensor(es[:], nm[:], nsg[:], ALU.subtract).then_inc(sem["nm"], 1)
                        dve.wait_ge(sem["es"], 4 * s + n + 1)
                        do(v.tensor_tensor(rd[:], den[:], es[:], ALU.add))
                        do(v.reciprocal(rd[:], rd[:]))
                        wait(dve, sem["t"], 4 * s + n)
                        w = 2 * P - k0
                        v.tensor_tensor(pn[:, :, k0:2 * P], p[:, :, k0:2 * P], rd[:].unsqueeze(2).to_broadcast([P, 4, w]),
                                        ALU.mult).then_inc(sem["pn"], 1)
                    dve.wait_ge(sem["pv"], 4 * s + 4)
                    dve.wait_ge(sem["lin_free"], 6 * s + 6)
                    for j in range(2):
                        v.tensor_tensor(k.wide[:, bass.ds(2 * s + j, 1), 0:SEQ].rearrange("p a t -> p (a t)"), O[j],
                                        gate[:, bass.ds(2 * s + j, 1), :].rearrange("p a t -> p (a t)"), ALU.mult).then_inc(sem["out"], 1)
                    steps.end()
                step(0)
                with dve.Fori(1, KV) as s:
                    step(s)


def pairs(k, name, st, nxt, diff, mb=None):
    nc, ps = k.nc, k.ps
    v = nc.vector
    NI = 8
    with ExitStack() as ctx:
        def sb(n, s, d=F32):
            return k.sb(f"{name}_{n}", s, d, ctx)
        raw, rop, t1, t2 = sb("raw", [P, 2, T2]), sb("roped", [P, 2, T2]), sb("t1", [P, T2]), sb("t2", [P, T2])
        vT, vt = sb("vT", [P, T2]), sb("v", [P, 5, P])
        maps = 1 if diff else 2
        p, pn = sb("p", [P, 2, T2]), sb("pn", [P, maps, T2])
        pt, mx, nm, den, rd = sb("pt", [P, maps, 512]), sb("mx", [P, 2]), sb("nm", [P, 2]), sb("den", [P, 2]), sb("rd", [P, 2])
        ptl = sb("ptl", [META, maps, META])
        osb, osq, lnv, rstd = (sb(x, [P, T2]) for x in ("o", "osq", "ln", "rstd")) if diff else (None,) * 4
        sem = {x: k.sem(f"{name}_{x}") for x in (
            "lin_done", "lin_free", "rot", "rope", "vtr", "v", "s", "nm", "exp", "pn", "t", "pt", "pv", "o", "osq", "oss", "rstd", "out")}
        steps = Steps(k.sem(name + "_steps"))
        S = ps[:, 2:6, :].rearrange("p (c x) j -> p c (x j)", c=2)
        TP = ps[:, 6:8, :]
        O = ps[:, 7, :] if diff else ps[:, 3, P:3 * P]

        def blocks(n):
            return [(b, *TILES[b]) for b in range(n + 1)]

        with nc.Block() as block:
            @block.sync
            def _(sp):
                k.stream(sp, st, nxt, sem["lin_done"], 6, lambda x: 2 * x + 2)

            @block.tensor
            def _(pe):
                def piece(i, q):
                    u, b = divmod(q, 2)
                    k.weights_ready(pe, st, i, u)
                    wait(pe, sem["lin_free"], 6 * i + q - 1)
                    w = k.slot(u, KT)
                    for f in range(KT):
                        m = nc.tensor.matmul(ps[:, b, 0:HALF], w[:, f, :], k.h[:, f, b * HALF:(b + 1) * HALF], start=f == 0, stop=f == KT - 1)
                    m.then_inc(sem["lin_done"], 1)

                def before(s):
                    pe.wait_ge(sem["lin_free"], 6 * s + 6)
                    wait(pe, sem["exp"], 10 * s)
                    if diff:
                        wait(pe, sem["rstd"], 2 * s)
                    wait(pe, sem["o"], 5 * s)
                    for q in range(2):
                        for b in range(2):
                            m = nc.tensor.matmul(ps[:, 2 + 2 * q + b, 0:HALF], k.rot2, raw[:, q, b * HALF:(b + 1) * HALF], start=True, stop=True)
                        m.then_inc(sem["rot"], 1)
                    wait(pe, sem["pt"], 5 * s)
                    for t, (c, n) in enumerate(TILES):
                        m = nc.tensor.transpose(ps[0:n, 6 + t // 4, (t % 4) * P:(t % 4 + 1) * P], vT[:, c:c + n], k.ident)
                    m.then_inc(sem["vtr"], 1)

                def scores(s, n):
                    c, nq = TILES[n]
                    N = c + nq
                    if n == 0:
                        pe.wait_ge(sem["rope"], 2 * s + 2)
                    for x in range(2):
                        h = slice(64 * x, 64 * x + 64)
                        for lo, hi in (((0, c), (c, N)) if diff else ((0, min(N, 512)), (512, N))):
                            if lo >= hi:
                                continue
                            masked = not diff or lo == c
                            m = nc.tensor.matmul(S[0:nq, x, lo:hi], rop[h, 0, c:N], rop[h, 1, lo:hi], start=True, stop=not masked)
                            if masked:
                                mask = k.maskb[0:nq, P:P + nq] if diff else mb[0:nq, n, lo:hi]
                                m = nc.tensor.matmul(S[0:nq, x, lo:hi], k.identb[0:nq, 0:nq], mask, start=False, stop=True)
                    m.then_inc(sem["s"], 1)

                def trans(s, n):
                    _, nq = TILES[n]
                    if n == 0:
                        pe.wait_ge(sem["v"], s + 1)
                    if n < 4:
                        wait(pe, sem["pt"], 5 * s + n)
                        pe.wait_ge(sem["pn"], 5 * s + n + 1)
                    if n == 3 and not diff:
                        pe.wait_ge(sem["o"], 5 * s + 3)
                    for x in range(maps):
                        for b, a, w in blocks(n):
                            m = nc.tensor.transpose(TP[0:w, x, b * nq:(b + 1) * nq], pn[0:nq, x, a:a + w], k.ident[0:nq, 0:nq])
                    m.then_inc(sem["t"], 1)

                def pv(s, n):
                    _, nq = TILES[n]
                    pe.wait_ge(sem["pt"], 5 * s + n + 1)
                    wait(pe, sem["o"], 5 * s + n)
                    if n == 3:
                        pe.wait_ge(sem["pn"], 5 * s + 5)
                    for x in range(maps):
                        d = slice(0, P) if diff else slice(64 * x, 64 * x + 64)
                        for b, a, w in blocks(n):
                            r = pt[0:w, x, b * nq:(b + 1) * nq] if b < 4 else ptl[:, x, :]
                            m = nc.tensor.matmul(O[d, 0:nq], vt[0:w, b, d], r, start=b == 0, stop=b == n)
                    m.then_inc(sem["pv"], 1)

                def step(i, lin=True, att=True):
                    s = i - 1
                    for q in range(6):
                        if att:
                            if q == 0:
                                before(s)
                            if q >= 3:
                                pv(s, q - 3)
                            if q >= 2:
                                trans(s, q - 2)
                            if 1 <= q <= 5:
                                scores(s, q - 1)
                        if lin:
                            piece(i, q)
                    if att:
                        pv(s, 3), trans(s, 4), pv(s, 4)
                        if diff:
                            pe.wait_ge(sem["osq"], s + 1)
                            pe.wait_ge(sem["exp"], 10 * s + 10)
                            for b in range(2):
                                m = nc.tensor.matmul(ps[:, 2 + b, 0:HALF], k.ones, osq[:, b * HALF:(b + 1) * HALF], start=True, stop=True)
                            m.then_inc(sem["oss"], 1)
                step(0, att=False)
                step(1)
                with pe.Fori(2, NI) as i:
                    step(i)
                step(NI, lin=False)

            @block.scalar
            def _(act):
                def evict(i, q):
                    u, b = divmod(q, 2)
                    act.wait_ge(sem["lin_done"], 6 * i + q + 1)
                    if u < 2:
                        wait(act, sem["rope"], 2 * i)
                        dst = raw[:, u, b * HALF:(b + 1) * HALF]
                    else:
                        wait(act, sem["vtr"], i)
                        dst = vT[:, b * HALF:(b + 1) * HALF]
                    nc.scalar.activation(dst, ps[:, b, 0:HALF], ACT.Copy).then_inc(sem["lin_free"], 1)

                def vtok(s):
                    act.wait_ge(sem["vtr"], s + 1)
                    wait(act, sem["pv"], 5 * s)
                    nc.scalar.activation(vt[:, 0:4, :].rearrange("p t d -> p (t d)"), ps[:, 6, :], ACT.Copy)
                    nc.scalar.activation(vt[0:META, 4, :], ps[0:META, 7, 0:P], ACT.Copy).then_inc(sem["v"], 1)

                def exps(s, n):
                    c, nq = TILES[n]
                    act.wait_ge(sem["nm"], 5 * s + n + 1)
                    wait(act, sem["pn"], 5 * s + n)
                    for x in range(2):
                        nc.scalar.activation(p[0:nq, x, 0:c + nq], S[0:nq, x, 0:c + nq], ACT.Exp, bias=nm[0:nq, x:x + 1], scale=0.125,
                                             accum_out=den[0:nq, x:x + 1]).then_inc(sem["exp"], 1)

                def store_pt(s, n):
                    _, nq = TILES[n]
                    act.wait_ge(sem["t"], 5 * s + n + 1)
                    wait(act, sem["pv"], 5 * s + n)
                    if n == 4:
                        nc.scalar.activation(ptl[:], TP[0:META, 0:maps, 4 * META:5 * META], ACT.Copy)
                    w = min(n + 1, 4) * nq
                    nc.scalar.activation(pt[:, :, 0:w], TP[:, 0:maps, 0:w], ACT.Copy).then_inc(sem["pt"], 1)

                def store_o(s, n):
                    c, nq = TILES[n]
                    act.wait_ge(sem["pv"], 5 * s + n + 1)
                    if diff and n == 0:
                        wait(act, sem["out"], s)
                    dst = osb[:, c:c + nq] if diff else k.wide[:, bass.ds(s, 1), c:c + nq].rearrange("p a t -> p (a t)")
                    nc.scalar.activation(dst, O[:, 0:nq], ACT.Copy).then_inc(sem["o"], 1)

                def step(i, lin=True, att=True):
                    s = i - 1
                    for q in range(6):
                        if att:
                            if q == 0:
                                vtok(s)
                            if q >= 3:
                                store_o(s, q - 3)
                            if q >= 2:
                                store_pt(s, q - 2)
                            if q >= 1:
                                exps(s, q - 1)
                        if lin:
                            evict(i, q)
                    if att:
                        store_o(s, 3), store_pt(s, 4), store_o(s, 4)
                        if diff:
                            act.wait_ge(sem["o"], 5 * s + 5)
                            nc.scalar.activation(osq[:], osb[:], ACT.Square).then_inc(sem["osq"], 1)
                            act.wait_ge(sem["oss"], s + 1)
                            wait(act, sem["out"], s)
                            nc.scalar.activation(both(lnv[:]), ps[:, 2:4, 0:HALF], ACT.Ln, scale=1.0 / P, bias=k.eps[:]).then_inc(sem["rstd"], 1)
                            act.wait_ge(sem["rstd"], 2 * s + 1)
                            nc.scalar.activation(rstd[:], lnv[:], ACT.Exp, scale=-0.5).then_inc(sem["rstd"], 1)
                step(0, att=False)
                step(1)
                with act.Fori(2, NI) as i:
                    step(i)
                step(NI, lin=False)

            @block.vector
            def _(dve):
                def do(ins):
                    steps.mark(ins)
                    steps.settle(dve)

                def step(s):
                    steps.begin(s)
                    for q in range(2):
                        dve.wait_ge(sem["lin_free"], 6 * s + 2 * q + 2)
                        do(v.tensor_tensor(t1[:], raw[:, q, :], k.cos2, ALU.mult))
                        dve.wait_ge(sem["rot"], 2 * s + q + 1)
                        do(v.tensor_tensor(both(t2[:]), ps[:, 2 + 2 * q:4 + 2 * q, 0:HALF], both(k.sin2), ALU.mult))
                        v.tensor_tensor(rop[:, q, :], t1[:], t2[:], ALU.add).then_inc(sem["rope"], 1)
                        dve.wait_ge(sem["rope"], 2 * s + q + 1)
                    for n, (c, nq) in enumerate(TILES):
                        N = c + nq
                        dve.wait_ge(sem["s"], 5 * s + n + 1)
                        if diff:
                            do(v.reduce_max(mx[0:nq, :], S[0:nq, :, 0:N], AX.X))
                        else:
                            for x in range(2):
                                do(v.reduce_max(mx[0:nq, x:x + 1], S[0:nq, x, 0:N], AX.X))
                        v.tensor_scalar(nm[0:nq, :], mx[0:nq, :], -0.125, None, ALU.mult).then_inc(sem["nm"], 1)
                        dve.wait_ge(sem["exp"], 10 * s + 2 * n + 2)
                        do(v.reciprocal(rd[0:nq, :], den[0:nq, :]))
                        wait(dve, sem["t"], 5 * s + n)
                        if diff:
                            do(v.tensor_scalar(rd[0:nq, 1:2], rd[0:nq, 1:2], k.neglam[0:nq, :], None, ALU.mult))
                            do(v.tensor_scalar(pn[0:nq, 0, 0:N], p[0:nq, 1, 0:N], rd[0:nq, 1:2], None, ALU.mult))
                            v.scalar_tensor_tensor(pn[0:nq, 0, 0:N], p[0:nq, 0, 0:N], rd[0:nq, 0:1], pn[0:nq, 0, 0:N],
                                                   ALU.mult, ALU.add).then_inc(sem["pn"], 1)
                        else:
                            do(v.tensor_scalar(pn[0:nq, 0, 0:N], p[0:nq, 0, 0:N], rd[0:nq, 0:1], None, ALU.mult))
                            v.tensor_scalar(pn[0:nq, 1, 0:N], p[0:nq, 1, 0:N], rd[0:nq, 1:2], None, ALU.mult).then_inc(sem["pn"], 1)
                    if diff:
                        dve.wait_ge(sem["rstd"], 2 * s + 2)
                        v.scalar_tensor_tensor(k.wide[:, bass.ds(s, 1), :].rearrange("p a t -> p (a t)"), osb[:], k.sub8[:], rstd[:],
                                               ALU.mult, ALU.mult).then_inc(sem["out"], 1)
                    steps.end()
                step(0)
                with dve.Fori(1, NI) as s:
                    step(s)


def index(k, st, nxt, mb):
    nc, ps, a = k.nc, k.ps, k.a
    v = nc.vector
    NH = 8
    with ExitStack() as ctx:
        def sb(n, s, d=F32):
            return k.sb("idx_" + n, s, d, ctx)
        raw, rop, t1, t2 = sb("raw", [P, 5, T2]), sb("roped", [P, 5, T2]), sb("t1", [P, T2]), sb("t2", [P, T2])
        wwi, wi = sb("wwi", [P, KT, NH]), sb("wi", [P, 5, NH])
        kn, lnv, rstd = sb("kn", [P, T2]), sb("ln", [P, T2]), sb("rstd", [P, T2])
        rel, sc, m8 = sb("rel", [P, 2, T2]), sb("sc", [P, T2]), sb("m8", [P, 8])
        s_wi, s_done, s_free, s_wip, s_sq, s_ss, s_r, s_kn, s_rot, s_rope, s_s, s_rel, s_acc, s_ones = (k.sem("idx_" + x) for x in (
            "wi_loaded", "lin_done", "lin_free", "wi_product", "squares", "summed", "rstd", "kn", "rot", "rope", "scores", "relu", "acc", "m"))
        steps = Steps(k.sem("idx_steps"))
        order = [4, 0, 1, 2, 3]
        with nc.Block() as block:
            @block.sync
            def _(sp):
                sp.dma_start(wwi[:], cols(a["dsa_w_in_2"][0], 0, KT, 3648, NH)).then_inc(s_wi, 16)
                k.stream(sp, st, nxt, s_done, 10, lambda u: 2 * order.index(u) + 2)

            @block.tensor
            def _(pe):
                for j, u in enumerate(order):
                    k.weights_ready(pe, st, 0, u)
                    w = k.slot(u, KT)
                    for b in range(2):
                        wait(pe, s_free, 2 * j + b - 1)
                        for f in range(KT):
                            m = nc.tensor.matmul(ps[:, b, 0:HALF], w[:, f, :], k.h[:, f, b * HALF:(b + 1) * HALF], start=f == 0, stop=f == KT - 1)
                        m.then_inc(s_done, 1)
                pe.wait_ge(s_wi, 16)
                for t, (c, n) in enumerate(TILES):
                    for f in range(KT):
                        m = nc.tensor.matmul(ps[0:n, 6, t * NH:(t + 1) * NH], k.h[:, f, c:c + n], wwi[:, f, :], start=f == 0, stop=f == KT - 1)
                m.then_inc(s_wip, 1)
                pe.wait_ge(s_sq, 1)
                for b in range(2):
                    m = nc.tensor.matmul(ps[:, 4 + b, 0:HALF], k.ones, kn[:, b * HALF:(b + 1) * HALF], start=True, stop=True)
                m.then_inc(s_ss, 1)
                for j, u in enumerate([0, 1, 2, 3, 4]):
                    if u == 4:
                        pe.wait_ge(s_kn, 1)
                    else:
                        pe.wait_ge(s_free, 2 * order.index(u) + 2)
                    wait(pe, s_rope, j)
                    for b in range(2):
                        m = nc.tensor.matmul(ps[:, 2 + b, 0:HALF], k.rot2, raw[:, u, b * HALF:(b + 1) * HALF], start=True, stop=True)
                    m.then_inc(s_rot, 1)
                pe.wait_ge(s_rope, 5)
                for n in range(5):
                    c, nq = TILES[n]
                    N = c + nq
                    for x in range(NH):
                        q = NH * n + x
                        h = slice(64 * (x % 2), 64 * (x % 2) + 64)
                        wait(pe, s_rel, q - 1)
                        for lo, hi in ((0, min(N, 512)), (512, N)):
                            if lo < hi:
                                m = nc.tensor.matmul(ps[0:nq, 2 * (q % 2) + lo // 512, 0:hi - lo], rop[h, x // 2, c:N], rop[h, 4, lo:hi], start=True, stop=True)
                        m.then_inc(s_s, 1)

            @block.scalar
            def _(act):
                for j, u in enumerate(order):
                    for b in range(2):
                        act.wait_ge(s_done, 2 * j + b + 1)
                        nc.scalar.activation(raw[:, u, b * HALF:(b + 1) * HALF], ps[:, b, 0:HALF], ACT.Copy).then_inc(s_free, 1)
                nc.scalar.activation(kn[:], raw[:, 4, :], ACT.Square).then_inc(s_sq, 1)
                act.wait_ge(s_ss, 1)
                nc.scalar.activation(both(lnv[:]), ps[:, 4:6, 0:HALF], ACT.Ln, scale=1.0 / P, bias=k.eps[:]).then_inc(s_r, 1)
                act.wait_ge(s_r, 1)
                nc.scalar.activation(rstd[:], lnv[:], ACT.Exp, scale=-0.5).then_inc(s_r, 1)
                for n in range(5):
                    c, nq = TILES[n]
                    N = c + nq
                    for x in range(NH):
                        q = NH * n + x
                        act.wait_ge(s_s, q + 1)
                        wait(act, s_acc, q - 1)
                        flat = ps[0:nq, 2 * (q % 2):2 * (q % 2) + 2, :].rearrange("p b j -> p (b j)")
                        nc.scalar.activation(rel[0:nq, q % 2, 0:N], flat[:, 0:N], ACT.Relu, scale=0.125).then_inc(s_rel, 1)

            @block.vector
            def _(dve):
                def do(ins):
                    steps.mark(ins)
                    steps.settle(dve)
                dve.wait_ge(s_wip, 1)
                for t, (c, n) in enumerate(TILES):
                    do(v.tensor_scalar(wi[0:n, t, :], ps[0:n, 6, t * NH:(t + 1) * NH], float(NH ** -0.5), None, ALU.mult))
                for j, u in enumerate([0, 1, 2, 3, 4]):
                    if u == 4:
                        dve.wait_ge(s_r, 2)
                        v.scalar_tensor_tensor(raw[:, 4, :], raw[:, 4, :], k.col(V_IDX), rstd[:], ALU.mult, ALU.mult).then_inc(s_kn, 1)
                        dve.wait_ge(s_kn, 1)
                    else:
                        dve.wait_ge(s_free, 2 * order.index(u) + 2)
                    do(v.tensor_tensor(t1[:], raw[:, u, :], k.cos2, ALU.mult))
                    dve.wait_ge(s_rot, j + 1)
                    do(v.tensor_tensor(both(t2[:]), ps[:, 2:4, 0:HALF], both(k.sin2), ALU.mult))
                    v.tensor_tensor(rop[:, u, :], t1[:], t2[:], ALU.add).then_inc(s_rope, 1)
                    dve.wait_ge(s_rope, j + 1)
                for n in range(5):
                    c, nq = TILES[n]
                    N = c + nq
                    for x in range(NH):
                        q = NH * n + x
                        dve.wait_ge(s_rel, q + 1)
                        w = wi[0:nq, n, x:x + 1]
                        if x == 0:
                            v.tensor_scalar(sc[0:nq, 0:N], rel[0:nq, q % 2, 0:N], w, None, ALU.mult).then_inc(s_acc, 1)
                        else:
                            v.scalar_tensor_tensor(sc[0:nq, 0:N], rel[0:nq, q % 2, 0:N], w, sc[0:nq, 0:N], ALU.mult, ALU.add).then_inc(s_acc, 1)
                        dve.wait_ge(s_acc, q + 1)
                    if n == 0:
                        do(v.tensor_copy(mb[:, 0, 0:P], k.maskb[:, P:2 * P]))
                        continue
                    do(v.memset(sc[0:nq, 0:META], 1e30))
                    do(v.scalar_tensor_tensor(sc[0:nq, c:N], k.maskf[0:nq, P:P + nq], 1e8, sc[0:nq, c:N], ALU.mult, ALU.add))
                    for _ in range(TOPK // 8):
                        do(v.max(m8[0:nq, :], sc[0:nq, 0:N]))
                        do(v.match_replace(sc[0:nq, 0:N], m8[0:nq, :], sc[0:nq, 0:N], -3e38))
                    do(v.tensor_scalar(mb[0:nq, n, 0:N], sc[0:nq, 0:N], -2e38, NEG, ALU.is_gt, ALU.mult))
                steps.end()


def ffn_up(k, name, l, st, nxt):
    nc, ps = k.nc, k.ps
    v = nc.vector
    w0, w2 = (2 + 2 * l) * P, (3 + 2 * l) * P
    with ExitStack() as ctx:
        u = k.sb(name + "_u", [P, 4, 2 + T2], F32, ctx)
        cc = k.sb(name + "_c", [P, 4, T2], F32, ctx)
        s_done, s_free, s_conv, s_silu, s_out = (k.sem(f"{name}_{x}") for x in ("done", "free", "conv", "silu", "out"))
        steps = Steps(k.sem(name + "_steps"))
        with nc.Block() as block:
            @block.sync
            def _(sp):
                k.stream(sp, st, nxt, s_done, 8, lambda x: 2 * x + 2)

            @block.tensor
            def _(pe):
                def step(i):
                    for x in range(4):
                        k.weights_ready(pe, st, i, x)
                        w = k.slot(x, KT)
                        for b in range(2):
                            wait(pe, s_free, 8 * i + 2 * x + b - 1)
                            for f in range(KT):
                                m = nc.tensor.matmul(ps[:, b, 0:HALF], w[:, f, :], k.h[:, f, b * HALF:(b + 1) * HALF], start=f == 0, stop=f == KT - 1)
                            m.then_inc(s_done, 1)
                step(0)
                with pe.Fori(1, st.iterations) as i:
                    step(i)

            @block.scalar
            def _(act):
                def step(i):
                    for y in range(2):
                        for x in (2 * y, 2 * y + 1):
                            for b in range(2):
                                act.wait_ge(s_done, 8 * i + 2 * x + b + 1)
                                wait(act, s_conv, 4 * i - 3 + x if not isinstance(i, int) or i else 0)
                                nc.scalar.activation(u[:, x, 2 + b * HALF:2 + (b + 1) * HALF], ps[:, b, 0:HALF], ACT.Copy).then_inc(s_free, 1)
                        act.wait_ge(s_conv, 4 * i + 2 * y + 1)
                        nc.scalar.activation(cc[:, 2 * y, :], cc[:, 2 * y, :], ACT.Silu).then_inc(s_silu, 1)
                step(0)
                with act.Fori(1, st.iterations) as i:
                    step(i)

            @block.vector
            def _(dve):
                def do(ins):
                    steps.mark(ins)
                    steps.settle(dve)

                def step(i):
                    steps.begin(i)
                    for y in range(2):
                        for x in (2 * y, 2 * y + 1):
                            tile = 2 * i + y + FT * (x % 2)
                            dve.wait_ge(s_free, 8 * i + 2 * x + 2)
                            acc = cc[:, x, :]
                            do(v.tensor_scalar(acc, u[:, x, 0:T2], k.col(w0 + tile), k.col(w2 + 2 * FT + tile), ALU.mult, ALU.add))
                            do(v.scalar_tensor_tensor(acc, u[:, x, 1:1 + T2], k.col(w0 + 2 * FT + tile), acc, ALU.mult, ALU.add))
                            v.scalar_tensor_tensor(acc, u[:, x, 2:2 + T2], k.col(w2 + tile), acc, ALU.mult, ALU.add).then_inc(s_conv, 1)
                            dve.wait_ge(s_conv, 4 * i + x + 1)
                        dve.wait_ge(s_silu, 2 * i + y + 1)
                        v.tensor_tensor(k.wide[:, bass.ds(2 * i + y, 1), :].rearrange("p a t -> p (a t)"), cc[:, 2 * y, :], cc[:, 2 * y + 1, :],
                                        ALU.mult).then_inc(s_out, 1)
                        dve.wait_ge(s_out, 2 * i + y + 1)
                    steps.end()
                first = k.sem(name + "_zero")
                v.memset(u[:, :, 0:2], 0.0).then_inc(first, 1)
                dve.wait_ge(first, 1)
                step(0)
                with dve.Fori(1, st.iterations) as i:
                    step(i)


def finish(k):
    nc, ps = k.nc, k.ps
    with ExitStack() as ctx:
        o = k.sb("out_tok", [P, 4, DM], F32, ctx)
        s_t, s_c, s_out = k.sem("fin_transposed"), k.sem("fin_copied"), k.sem("out_stored")
        with nc.Block() as block:
            @block.tensor
            def _(pe):
                for t in range(4):
                    for g in range(2):
                        for f in range(4):
                            m = nc.tensor.transpose(ps[:, 2 * t + g, f * P:(f + 1) * P],
                                                    k.h[:, 4 * g + f, META + t * P:META + (t + 1) * P], k.ident)
                    m.then_inc(s_t, 1)

            @block.scalar
            def _(act):
                for t in range(4):
                    act.wait_ge(s_t, t + 1)
                    nc.scalar.activation(o[:, t, :].rearrange("p (b n) -> p b n", b=2), ps[:, 2 * t:2 * t + 2, :], ACT.Copy).then_inc(s_c, 1)

            @block.sync
            def _(sp):
                for t in range(4):
                    sp.wait_ge(s_c, t + 1)
                    sp.dma_start(k.out[0, t * P:(t + 1) * P, :], o[:, t, :]).then_inc(s_out, 16)
                sp.wait_ge(s_out, 64)


def build(nc, a, out, probe=None, dump=None):
    with ExitStack() as ctx:
        k = Core(nc, a, out, ctx)
        v = nc.vector
        w_in, w_att, w_da, w_dsa = a["ssm_w_in"][0], a["att_w_in"][0], a["da_w_qkv_2"][0], a["dsa_w_in_2"][0]

        def one(w, kt, col, row=lambda i, u: 0):
            return lambda i, u: [(0, P, w, row(i, u), col(i, u))]

        def twice(w, c):
            return [(0, 64, w, 0, c), (64, 64, w, 0, c)]

        def split(w, kt, n=1):
            return Stream(2 * n, 4, kt, lambda i, u: [(0, P, w, (u % n) * kt * P, i * (4 // n * P) + (u // n) * P)])

        def ssm_col(g, u):
            return (2048 + 256 * g, 2176 + 256 * g, 4096 + P * g, 5120 + P * g, 256 * g, 128 + 256 * g)[u]

        def swa_unit(j, u):
            two = (u == 0, u == 1)
            if two[0] or two[1]:
                return twice(w_att, 1024 + 256 * u + 64 * j)
            c = (256 * j, 128 + 256 * j, 1536 + 256 * j, 1664 + 256 * j)[u - 2]
            return [(0, 64, w_att, 0, c), (64, 64, w_att, 0, c + 64)]

        def idx_unit(i, u):
            if u == 4:
                return twice(w_dsa, 3584)
            return [(0, 64, w_dsa, 0, 3072 + P * u), (64, 64, w_dsa, 0, 3136 + P * u)]

        def up(l):
            w = a["ffn_w_up_2"][l]
            return Stream(FT // 2, 4, KT, one(w, KT, lambda i, u: i * (2 * P) + (u // 2) * P + (u % 2) * FF))
        S = {
            "ssm": Stream(GROUPS, 6, KT, one(w_in, KT, ssm_col)),
            "ssm_out": split(a["ssm_w_out"][0], KT, 2),
            "swa": Stream(KV, 6, KT, swa_unit, dmas=2),
            "swa_out": split(a["att_w_out"][0], KT),
            "da": Stream(8, 3, KT, one(w_da, KT, lambda i, u: i * P + u * DM)),
            "da_out": split(a["da_w_o_2"][0], KT),
            "up0": up(0), "down0": split(a["ffn_w_down_2"][0], FK, 2),
            "idx": Stream(1, 5, KT, idx_unit, dmas=2),
            "dsa": Stream(8, 3, KT, one(w_dsa, KT, lambda i, u: i * P + u * DM)),
            "dsa_out": split(a["dsa_w_o_2"][0], KT),
            "up1": up(1), "down1": split(a["ffn_w_down_2"][1], FK, 2),
        }
        names = list(S)
        for n in names:
            k.start_stream(S[n])
        following = {n: (S[names[j + 1]] if j + 1 < len(names) else None) for j, n in enumerate(names)}
        if probe:
            order = ["ssm", "swa", "da", "ffn0", "dsa", "ffn1"]
            ends = {"ssm": "ssm_out", "swa": "swa_out", "da": "da_out", "ffn0": "down0", "dsa": "dsa_out", "ffn1": "down1"}
            following[ends[probe]] = None

        def done(x):
            if probe != x:
                return False
            s = k.sem("dumped")
            with nc.Block() as block:
                @block.sync
                def _(sp):
                    sp.dma_start(dump, k.res[:]).then_inc(s, 16)
                    sp.wait_ge(s, 16)
            return True

        def h1(f):
            return k.h[:, f, 0:SEQ]

        def r1(f):
            return k.res[:, f, META:T2]

        def wide1(f):
            return k.wide[:, f, 0:SEQ]

        def h2(f):
            return k.h[:, f, :]

        def r2(f):
            return k.res[:, f, :]

        def wide2(f):
            return k.wide[:, f, :]

        def to_y(t, c, n, src):
            return v.tensor_copy(k.h[:, bass.ds(t, 1), c:c + n].rearrange("p a t -> p (a t)"), src)

        def to_res(t, c, n, src):
            dst = k.res[:, bass.ds(t, 1), c:c + n].rearrange("p a t -> p (a t)")
            return v.tensor_tensor(dst, src, dst, ALU.add)

        setup(k, S["ssm"])
        norm(k, "n1", r1, KT, SEQ, V_PRE, h1)
        with ExitStack() as own:
            dts = k.sb("dts", [P, 5, CHUNKS, SSM_HEADS], F32, own)
            ssm_dt(k, dts)
            ssm(k, S["ssm"], following["ssm"], dts)
        norm(k, "n2", wide1, 2 * KT, SEQ, V_GATE, wide1)
        project(k, "ssm_out", S["ssm_out"], following["ssm_out"], 2, wide1, SEQ, to_y)
        norm(k, "n3", h1, KT, SEQ, V_POST, r1, add=True)
        if done("ssm"):
            return
        norm(k, "n4", r1, KT, SEQ, V_PRE + 8, h1)
        swa(k, S["swa"], following["swa"])
        project(k, "swa_out", S["swa_out"], following["swa_out"], 1, wide1, SEQ, to_y)
        norm(k, "n5", h1, KT, SEQ, V_POST + 8, r1, add=True)
        if done("swa"):
            return
        norm(k, "n6", r2, KT, T2, V_DA, h2)
        pairs(k, "da", S["da"], following["da"], True)
        project(k, "da_out", S["da_out"], following["da_out"], 1, wide2, T2, to_res)
        if done("da"):
            return
        norm(k, "n7", r2, KT, T2, V_FFN, h2)
        ffn_up(k, "up0", 0, S["up0"], following["up0"])
        project(k, "down0", S["down0"], following["down0"], 2, wide2, T2, to_res)
        if done("ffn0"):
            return
        norm(k, "n8", r2, KT, T2, V_DSA, h2)
        with ExitStack() as own:
            mb = k.sb("mb", [P, 5, T2], BF16, own)
            index(k, S["idx"], following["idx"], mb)
            pairs(k, "dsa", S["dsa"], following["dsa"], False, mb)
        project(k, "dsa_out", S["dsa_out"], following["dsa_out"], 1, wide2, T2, to_res)
        if done("dsa"):
            return
        norm(k, "n9", r2, KT, T2, V_FFN + 8, h2)
        ffn_up(k, "up1", 1, S["up1"], following["up1"])
        project(k, "down1", S["down1"], following["down1"], 2, wide2, T2, to_res)
        if done("ffn1"):
            return
        norm(k, "n10", r2, KT, T2, V_FIN, h2)
        finish(k)


def kernel(**inputs):
    import concourse.bacc as bacc
    from concourse.bass_utils import run_bass_kernel_spmd

    nc = bacc.Bacc("TRN2", target_bir_lowering=False, num_devices=1)
    arrays, aps = {}, {}
    for name, x in inputs.items():
        x = np.ascontiguousarray(x)
        arrays["in_" + name] = x
        aps[name] = nc.dram_tensor("in_" + name, x.shape, mybir.dt.from_np(x.dtype), kind="ExternalInput").ap()
    out = nc.dram_tensor("out", (1, SEQ, DM), F32, kind="ExternalOutput").ap()
    build(nc, aps, out)
    r = run_bass_kernel_spmd(nc, [arrays], core_ids=[0])
    return r.results[0]["out"]
```

```python
import concourse.bass as bass
from concourse import mybir
from contextlib import ExitStack
import numpy as np

F32 = mybir.dt.float32
F32R = mybir.dt.float32r
BF16 = mybir.dt.bfloat16
I32 = mybir.dt.int32
ACT = mybir.ActivationFunctionType
ALU = mybir.AluOpType
AX = mybir.AxisListType

P = 128
DM = 1024
KT = DM // P
SEQ = 512
META = 16
T2 = SEQ + META
HALF = T2 // 2
NEG = -1e30
EPS = 1e-6
DI = 2048
GROUPS = 8
CHUNKS = SEQ // P
SSM_HEADS = 32
RPG = SSM_HEADS // GROUPS
KV = 4
FF = 2816
FT = FF // P
FK = FT // 2
TOPK = 128
TILES = [(a, min(P, T2 - a)) for a in range(0, T2, P)]
LAMBDA_INIT = 0.2

V_PRE, V_POST, V_GATE, V_CB = 0, 16, 32, 48
V_DA, V_DSA, V_FFN, V_FIN, V_SUB, V_IDX = 80, 88, 96, 112, 120, 121
V_CW = P
V_ROWS = [122, 128, 88, 88, 88, 88]


def constants():
    eye = np.eye(P, dtype=np.float32)
    ones = np.ones((P, P), np.float32)
    tri = np.triu(ones)
    rot1, rot2 = np.zeros((P, P), np.float32), np.zeros((P, P), np.float32)
    for m in range(P):
        b, d = m - m % 64, m % 64
        if d < 8:
            rot1[b + d + 8, m] = -1
        elif d < 16:
            rot1[b + d - 8, m] = 1
        if d < 32:
            rot2[b + d + 32, m] = -1
        else:
            rot2[b + d - 32, m] = 1
    causal = np.where(tri.T > 0, 0, NEG).astype(np.float32)
    before = np.where(np.arange(P)[None] > np.arange(P)[:, None], 0, NEG).astype(np.float32)
    d = np.arange(P) % 64
    inv1 = np.float32(500000.0) ** (-(2 * (d % 8)).astype(np.float32) / np.float32(16))
    inv1 = np.where(d < 16, inv1, 0).astype(np.float32)[:, None]
    inv2 = (np.float32(10000.0) ** (-(2 * (d % 32)).astype(np.float32) / np.float32(64))).astype(np.float32)
    ang = (np.arange(T2, dtype=np.float32)[None] * inv2[:, None]).astype(np.float32)
    cos2, sin2 = np.cos(ang).astype(np.float32), np.sin(ang).astype(np.float32)
    return np.concatenate([eye, ones, tri, rot1, rot2, before, causal, cos2, sin2, inv1], axis=1)


def wait(eng, sem, value):
    if not isinstance(value, int) or value > 0:
        eng.wait_ge(sem, value)


class Steps:

    def __init__(self, sem):
        self.sem, self.per, self.base, self.k = sem, 0, 0, 0

    def begin(self, i):
        self.base, self.k = i * self.per, 0

    def mark(self, ins):
        ins.then_inc(self.sem, 1)
        self.k += 1

    def settle(self, eng):
        eng.wait_ge(self.sem, self.base + self.k)

    def end(self):
        self.per = self.per or self.k
        assert self.per == self.k


class Stream:

    def __init__(self, iterations, units, kt, source, dmas=1):
        self.iterations, self.units, self.kt, self.source, self.dmas = iterations, units, kt, source, dmas
        self.depth = 2 if units % 2 == 0 else 3
        assert iterations == 1 or units % self.depth == 0

    def after(self, i, u, d):
        u += d
        if u >= self.units:
            i, u = i + 1, u - self.units
        return None if isinstance(i, int) and i >= self.iterations else (i, u)


class Core:
    def __init__(self, nc, a, out, ctx):
        self.nc, self.a, self.out, self.ctx = nc, a, out, ctx
        sb = self.sb
        self.SLOTS = 6
        self.ring = sb("ring", [P, self.SLOTS * KT * P])
        self.parts = sb("parts", [P, self.SLOTS * KT * P], F32R)
        self.res = sb("res", [P, KT, T2])
        self.h, self.h_parts = self.two_names("h", [P, 2 * KT, T2])
        self.wide, self.wide_parts = self.two_names("wide", [P, FT, T2])
        self.cst = sb("cst", [P, 7 * P + 2 * T2 + 1])
        c = self.cst
        self.ident, self.ones, self.tri = c[:, 0:P], c[:, P:2 * P], c[:, 2 * P:3 * P]
        self.rot1, self.rot2 = c[:, 3 * P:4 * P], c[:, 4 * P:5 * P]
        self.maskf = c[:, 5 * P:7 * P]
        self.cos2, self.sin2 = c[:, 7 * P:7 * P + T2], c[:, 7 * P + T2:7 * P + 2 * T2]
        self.inv1 = c[:, 7 * P + 2 * T2:7 * P + 2 * T2 + 1]
        self.identb = sb("identb", [P, P], BF16)
        self.maskb = sb("maskb", [P, 2 * P], BF16)
        self.cos1, self.sin1 = sb("cos1", [P, SEQ]), sb("sin1", [P, SEQ])
        self.vec = sb("vec", [P, 6 * P])
        self.eps = sb("eps", [P, 1])
        self.sub8 = sb("sub8", [P, 1])
        self.neglam = sb("neglam", [P, 1])
        self.drow = sb("drow", [P, 4, SSM_HEADS])
        self.dexp = sb("dexp", [P, 16])
        self.nsink = sb("nsink", [P, 16])
        self.wdt = sb("wdt", [P, KT, SSM_HEADS])
        self.ps = ctx.enter_context(nc.psum_tensor("ps", [P, 8, 512], F32))
        self.loaded = [self.sem(f"weights_loaded{s}") for s in range(self.SLOTS)]
        self.granted = self.sem("refills_granted")
        self.w_high, self.w_low = self.sem("weights_high"), self.sem("weights_low")
        self.split = 0
        self.loads = [0] * self.SLOTS
        self.acc, self.sq, self.rstd = sb("norm_acc", [P, T2]), sb("norm_sq", [P, T2]), sb("norm_rstd", [P, T2])
        names = ("high", "low", "squared", "accumulated", "summed", "rstd_steps", "post_steps", "normalised")
        self.nsem = {x: self.sem("norm_" + x) for x in names}
        self.ncount = {x: 0 for x in names}

    def two_names(self, name, shape):
        with self.nc.sbuf_tensor(name, shape, F32) as plain:
            pass
        return plain, self.sb(name + "_parts", shape, F32R)

    def sb(self, name, shape, dt=F32, ctx=None):
        return (ctx or self.ctx).enter_context(self.nc.sbuf_tensor(name, shape, dt))

    def sem(self, name):
        return self.ctx.enter_context(self.nc.semaphore(name))

    def col(self, c):
        return self.vec[:, c:c + 1] if isinstance(c, int) else self.vec[:, bass.ds(c, 1)]

    def slot(self, u, kt):
        return self.ring[:, u * kt * P:(u + 1) * kt * P]

    def part(self, st, u, low):
        at = (2 * (u % st.depth) + low) * st.kt * P
        return self.parts[:, at:at + st.kt * P]

    def load(self, sp, st, i, u, refill=False):
        if refill:
            sp.wait_ge(self.w_low, st.first + st.units * (i - 1) + u + 1)
            sp.sem_inc(self.granted, 1)
        slot = self.slot(u, st.kt).rearrange("p (k n) -> p k n", k=st.kt)
        for c0, n, w, r0, c in st.source(i, u):
            sp.dma_start(slot[:, :, c0:c0 + n], cols(w, r0, st.kt, c, n)).then_inc(self.loaded[u], 16)

    def start_stream(self, st):
        st.base = list(self.loads)
        st.first = self.split
        self.split += st.units * st.iterations
        for u in range(st.units):
            self.loads[u] += 16 * st.dmas * st.iterations

    def stream(self, sp, st, nxt):
        if st.iterations > 1:
            with sp.Fori(1, st.iterations) as i:
                for u in range(st.units):
                    self.load(sp, st, i, u, refill=True)
        if nxt is not None:
            sp.wait_ge(self.w_low, st.first + st.units * st.iterations)
            for u in range(nxt.units):
                self.load(sp, nxt, 0, u)

    def high(self, act, st, at):
        if at is None:
            return
        i, u = at
        act.wait_ge(self.loaded[u], st.base[u] + 16 * st.dmas * (i + 1))
        self.nc.scalar.activation(self.part(st, u, 0), self.slot(u, st.kt), ACT.Copy).then_inc(self.w_high, 1)

    def low(self, pool, st, at):
        if at is None:
            return
        i, u = at
        pool.wait_ge(self.w_high, st.first + st.units * i + u + 1)
        self.nc.gpsimd.tensor_tensor(self.part(st, u, 1), self.slot(u, st.kt), self.part(st, u, 0).bitcast(F32), ALU.subtract).then_inc(self.w_low, 1)

    def split_ready(self, pe, st, i, u):
        pe.wait_ge(self.w_low, st.first + st.units * i + u + 1)

    def high_first(self, act, st):
        for u in range(st.depth):
            self.high(act, st, (0, u))

    def low_all(self, pool, st):
        with pool.Fori(0, st.iterations) as i:
            for u in range(st.units):
                self.low(pool, st, (i, u))

    def product(self, st, u, out, x, start=True, stop=True, before=None):
        hi, lo = self.part(st, u, 0), self.part(st, u, 1)
        for f in range(st.kt):
            if before is not None:
                before(f)
            xh, xl = x(f)
            n = slice(f * P, (f + 1) * P)
            for j, (w, b) in enumerate(((hi, xh), (hi, xl), (lo, xh))):
                m = self.nc.tensor.matmul(out, w[:, n], b, start=start and f == j == 0, stop=stop and f == st.kt - 1 and j == 2)
        return m

    def hx(self, c, n):
        return lambda f: (self.h_parts[:, f, c:c + n], self.h_parts[:, KT + f, c:c + n])


class Spread:

    def __init__(self, k, kt, x, high, low):
        self.k, self.kt, self.x, self.high, self.low = k, kt, x, high, low
        self.base = dict(k.ncount)
        k.ncount["high"] += kt
        k.ncount["low"] += kt

    def act(self, act, f):
        k = self.k
        k.nc.scalar.activation(self.high(f), self.x(f), ACT.Copy).then_inc(k.nsem["high"], 1)

    def dve(self, dve, f):
        k = self.k
        dve.wait_ge(k.nsem["high"], self.base["high"] + f + 1)
        k.nc.vector.tensor_tensor(self.low(f), self.x(f), self.high(f).bitcast(F32), ALU.subtract).then_inc(k.nsem["low"], 1)

    def ready(self, pe, f):
        pe.wait_ge(self.k.nsem["low"], self.base["low"] + f + 1)

    def parts(self, c, n):
        return lambda f: (self.high(f)[:, c:c + n], self.low(f)[:, c:c + n])


def cols(w, r0, kt, c, n=P):
    return w[r0:r0 + kt * P, bass.ds(c, n)].rearrange("(k p) n -> p k n", p=P)


def both(ap):
    return ap.rearrange("p (a n) -> p a n", a=2)


def halves(T):
    return [(0, SEQ)] if T == SEQ else [(0, HALF), (HALF, HALF)]


def setup(k, first):
    nc, a, ps = k.nc, k.a, k.ps
    with ExitStack() as ctx:
        def sb(n, s, d=F32):
            return k.sb(n, s, d, ctx)
        xin, meta = sb("xin", [P, 4, DM]), sb("metain", [META, DM])
        stage = sb("stage", [P, 6, P])
        posi, ang, turns = sb("posi", [P, SEQ], I32), sb("ang", [P, SEQ]), sb("turns", [P, SEQ])
        lam = sb("lam", [P, 4, 64])
        lprod, lsum = sb("lprod", [P, 2, 64]), sb("lsum", [P, 2])
        s_cst, s_x, s_row, s_small = k.sem("const_loaded"), k.sem("x_loaded"), k.sem("rows_loaded"), k.sem("small_loaded")
        s_xt, s_xfree = k.sem("x_transposed"), k.sem("x_stored")
        s_vt, s_v, s_a, s_pos = k.sem("vec_transposed"), k.sem("setup_vector"), k.sem("setup_scalar"), k.sem("pos_loaded")
        ns = k.nsem
        k.ncount["squared"] += KT
        k.ncount["accumulated"] += KT + 1
        const = nc.inline_tensor(constants(), name="shape_constants").ap()
        rows = []

        def put(tile, r, src, n, w=P, c=0):
            rows.append((stage[r:r + n, tile, c:c + w], src))
        for l in range(2):
            put(0, V_PRE + 8 * l, a["pre_norm"][l].rearrange("(r c) -> r c", c=P), 8)
            put(0, V_POST + 8 * l, a["post_norm"][l].rearrange("(r c) -> r c", c=P), 8)
            put(0, V_FFN + 8 * l, a["ffn_norm_2"][l].rearrange("(r c) -> r c", c=P), 8)
            w = a["ffn_conv_w_2"][l].rearrange("j (r c) -> (j r) c", c=P)
            put(2 + 2 * l, 0, w[0:4 * FT], 4 * FT)
            put(3 + 2 * l, 0, w[4 * FT:6 * FT], 2 * FT)
            put(3 + 2 * l, 2 * FT, a["ffn_conv_b_2"][l].rearrange("(r c) -> r c", c=P), 2 * FT)
        put(0, V_GATE, a["ssm_gate_norm"][0].rearrange("(r c) -> r c", c=P), 16)
        put(0, V_CB, a["ssm_conv_b"][0].rearrange("(r c) -> r c", c=P), 32)
        put(0, V_DA, a["da_norm_2"][0].rearrange("(r c) -> r c", c=P), 8)
        put(0, V_DSA, a["dsa_norm_2"][0].rearrange("(r c) -> r c", c=P), 8)
        put(0, V_FIN, a["final_norm_2"].rearrange("(r c) -> r c", c=P), 8)
        put(0, V_SUB, a["da_subln_2"], 1)
        put(0, V_IDX, a["dsa_idx_k_norm_2"], 1, 64)
        put(0, V_IDX, a["dsa_idx_k_norm_2"], 1, 64, 64)
        put(1, 0, a["ssm_conv_w"][0].rearrange("j (r c) -> (j r) c", c=P), 4 * 32)
        small = [(k.drow[:, j, :], a[n].to_broadcast([P, SSM_HEADS]))
                 for j, n in enumerate(["ssm_d", "ssm_dt_bias", "ssm_a_log"])]
        small += [(k.nsink[:], a["att_sinks"].to_broadcast([P, 16]))]
        small += [(lam[:, j, :], a[n].to_broadcast([P, 64]))
                  for j, n in enumerate(["da_lambda_q1_2", "da_lambda_q2_2", "da_lambda_k1_2", "da_lambda_k2_2"])]

        with nc.Block() as block:
            @block.sync
            def _(sp):
                sp.dma_start(k.cst[:], const).then_inc(s_cst, 16)
                sp.dma_start(xin[:], a["x"][0].rearrange("(t p) d -> p t d", p=P)).then_inc(s_x, 16)
                sp.dma_start(meta[:], a["meta_tokens_2"]).then_inc(s_x, 16)
                for u in range(first.units):
                    k.load(sp, first, 0, u)

            @block.gpsimd
            def _(pool):
                pool.dma_start(k.wdt[:], cols(a["ssm_w_in"][0], 0, KT, 6144, SSM_HEADS)).then_inc(s_small, 16)
                for dst, src in small:
                    pool.dma_start(dst, src).then_inc(s_small, 16)
                pool.dma_start(posi[:], a["positions"].to_broadcast([P, SEQ])).then_inc(s_pos, 16)
                pool.wait_ge(s_small, 16 * (1 + len(small)))
                pool.wait_ge(s_pos, 16)

            @block.tensor
            def _(pe):
                pe.wait_ge(s_cst, 16)
                pe.wait_ge(s_x, 32)
                for f in range(KT):
                    wait(pe, s_xfree, f - 3)
                    for t in range(4):
                        m = nc.tensor.transpose(ps[:, f % 4, t * P:(t + 1) * P], xin[:, t, f * P:(f + 1) * P], k.ident)
                    m.then_inc(s_xt, 1)
                for f in range(KT):
                    m = nc.tensor.transpose(ps[:, 4, f * META:(f + 1) * META], meta[:, f * P:(f + 1) * P], k.ident[0:META, 0:META])
                m.then_inc(s_xt, 1)
                pe.wait_ge(s_row, 16 * len(rows))
                for t, n in enumerate(V_ROWS):
                    m = nc.tensor.transpose(ps[:, 5 + t // 3, (t % 3) * P:(t % 3) * P + n], stage[0:n, t, :], k.ident[0:n, 0:n])
                m.then_inc(s_vt, 1)

            @block.scalar
            def _(act):
                for dst, src in rows:
                    act.dma_start(dst, src).then_inc(s_row, 16)
                act.wait_ge(s_v, 1)
                nc.scalar.activation(k.drow[:, 3, :], k.drow[:, 2, :], ACT.Exp).then_inc(s_a, 1)
                nc.scalar.activation(lsum[:], lsum[:], ACT.Exp).then_inc(s_a, 1)
                act.wait_ge(s_v, 3)
                nc.scalar.activation(k.sin1[:], ang[:], ACT.Sin).then_inc(s_a, 1)
                nc.scalar.activation(k.cos1[:], turns[:], ACT.Sin).then_inc(s_a, 1)
                for f in range(KT):
                    act.wait_ge(s_xfree, f + 1)
                    act.wait_ge(ns["accumulated"], f + 1)
                    nc.scalar.activation(k.sq[:, 0:SEQ], k.res[:, f, META:T2], ACT.Square).then_inc(ns["squared"], 1)

            @block.vector
            def _(dve):
                steps = Steps(k.sem("setup_steps"))

                def do(ins):
                    steps.mark(ins)
                    steps.settle(dve)
                do(nc.vector.memset(k.eps[:], EPS))
                dve.wait_ge(s_small, 16 * (1 + len(small)))
                do(nc.vector.tensor_tensor(lprod[:], lam[:, 0:2, :], lam[:, 2:4, :], ALU.mult))
                nc.vector.reduce_sum(lsum[:], lprod[:], AX.X).then_inc(s_v, 1)
                for b in range(2):
                    do(nc.vector.tensor_copy(k.dexp[64 * b:64 * b + 64, :],
                                             k.drow[64 * b:64 * b + 64, 0, :].rearrange("p (f b) -> p b f", b=2)[:, b, :]))
                do(nc.vector.tensor_scalar(k.nsink[:], k.nsink[:], -1.0, None, ALU.mult))
                dve.wait_ge(s_cst, 16)
                dve.wait_ge(s_pos, 16)
                do(nc.vector.tensor_copy(ang[:], posi[:]))
                do(nc.vector.tensor_scalar(ang[:], ang[:], k.inv1, None, ALU.mult))
                do(nc.vector.tensor_scalar(turns[:], ang[:], float(1 / (2 * np.pi)), 12582912.0, ALU.mult, ALU.add))
                do(nc.vector.tensor_scalar(turns[:], turns[:], 12582912.0, None, ALU.subtract))
                c1 = 6.28125
                c2 = float(np.float32(int((2 * np.pi - c1) * 2 ** 21) / 2 ** 21))
                c3 = float(np.float32(2 * np.pi - c1 - c2))
                for c in (c1, c2, c3):
                    do(nc.vector.scalar_tensor_tensor(ang[:], turns[:], -c, ang[:], ALU.mult, ALU.add))
                pi = float(np.nextafter(np.float32(np.pi), np.float32(0)))
                nc.vector.tensor_scalar(ang[:], ang[:], -pi, pi, ALU.max, ALU.min).then_inc(s_v, 1)
                dve.wait_ge(s_v, 2)
                do(nc.vector.scalar_tensor_tensor(turns[:], ang[:], -1.0, ang[:], ALU.mult, ALU.max))
                nc.vector.tensor_scalar(turns[:], turns[:], -1.0, float(np.pi / 2), ALU.mult, ALU.add).then_inc(s_v, 1)
                do(nc.vector.tensor_copy(k.identb[:], k.ident))
                do(nc.vector.tensor_copy(k.maskb[:], k.maskf))
                nc.vector.memset(k.acc[:], 0.0).then_inc(ns["accumulated"], 1)
                for f in range(KT + 1):
                    if f < KT:
                        dve.wait_ge(s_xt, f + 1)
                        nc.vector.tensor_copy(k.res[:, f, META:T2], ps[:, f % 4, :]).then_inc(s_xfree, 1)
                    if f:
                        dve.wait_ge(ns["accumulated"], f)
                        dve.wait_ge(ns["squared"], f)
                        nc.vector.tensor_tensor(k.acc[:, 0:SEQ], k.acc[:, 0:SEQ], k.sq[:, 0:SEQ], ALU.add).then_inc(ns["accumulated"], 1)
                dve.wait_ge(s_xt, KT + 1)
                do(nc.vector.tensor_copy(k.res[:, :, 0:META], ps[:, 4, 0:KT * META].rearrange("p (f t) -> p f t", f=KT)))
                dve.wait_ge(s_vt, 1)
                for t, n in enumerate(V_ROWS):
                    do(nc.vector.tensor_copy(k.vec[:, t * P:t * P + n], ps[:, 5 + t // 3, (t % 3) * P:(t % 3) * P + n]))
                do(nc.vector.tensor_scalar(k.sub8[:], k.col(V_SUB), 1.0 - LAMBDA_INIT, None, ALU.mult))
                dve.wait_ge(s_a, 4)
                do(nc.vector.tensor_scalar(k.drow[:, 3, :], k.drow[:, 3, :], -1.0, None, ALU.mult))
                do(nc.vector.tensor_tensor(k.neglam[:], lsum[:, 1:2], lsum[:, 0:1], ALU.subtract))
                do(nc.vector.tensor_scalar(k.neglam[:], k.neglam[:], -LAMBDA_INIT, None, ALU.add))


class Norm:

    def __init__(self, k, src, kt, T, gain, dst, post=None, parts=None):
        self.spread = Spread(k, kt, dst, *parts) if parts else None
        self.k, self.src, self.kt, self.T, self.gain, self.dst, self.post = k, src, kt, T, gain, dst, post
        self.base = dict(k.ncount)
        c = k.ncount
        c["summed"] += 1 + (kt if post else 0)
        c["rstd_steps"] += 4 if post else 2
        c["squared"] += kt if post else 0
        c["post_steps"] += 2 * kt if post else 0
        c["normalised"] += kt

    @staticmethod
    def view(x, T):
        return x[:, 0:SEQ] if T == SEQ else both(x)

    def sum_over_partitions(self, T, bank, x, first=True, last=True):
        k = self.k
        for b, (c, w) in enumerate(halves(T)):
            m = k.nc.tensor.matmul(k.ps[:, bank + b, 0:w], k.ones, x[:, c:c + w], start=first, stop=last)
        m.then_inc(k.nsem["summed"], 1)

    def pe(self, pe):
        k, n, at = self.k, self.k.nsem, self.base
        pe.wait_ge(n["accumulated"], at["accumulated"])
        if self.post:
            self.sum_over_partitions(SEQ, 5, k.acc)
            for f in range(self.kt):
                pe.wait_ge(n["squared"], at["squared"] + f + 1)
                self.sum_over_partitions(self.T, 6, self.post[4][:, f % 4, :], f == 0, f == self.kt - 1)
        else:
            self.sum_over_partitions(self.T, 6, k.acc)

    def ready(self, pe, f):
        if self.spread:
            self.spread.ready(pe, f)
            return
        pe.wait_ge(self.k.nsem["normalised"], self.base["normalised"] + f + 1)

    def rms(self, act, j, T, bank, summed):
        nc, k, n, at = self.k.nc, self.k, self.k.nsem, self.base
        act.wait_ge(n["summed"], at["summed"] + summed)
        total = k.ps[:, bank, :] if T == SEQ else k.ps[:, bank:bank + 2, 0:HALF]
        nc.scalar.activation(self.view(k.sq, T), total, ACT.Ln, scale=1.0 / (self.kt * P), bias=k.eps[:]).then_inc(n["rstd_steps"], 1)
        act.wait_ge(n["rstd_steps"], at["rstd_steps"] + 2 * j + 1)
        nc.scalar.activation(k.rstd[:, 0:T], k.sq[:, 0:T], ACT.Exp, scale=-0.5).then_inc(n["rstd_steps"], 1)

    def act(self, act):
        nc, n, at = self.k.nc, self.k.nsem, self.base
        if not self.post:
            self.rms(act, 0, self.T, 6, 1)
            self.high(act)
            return
        self.rms(act, 0, SEQ, 5, 1)
        for f in range(self.kt):
            act.wait_ge(n["post_steps"], at["post_steps"] + 2 * f + 2)
            if f >= 4:
                act.wait_ge(n["summed"], at["summed"] + f - 2)
            nc.scalar.activation(self.post[4][:, f % 4, :], self.src(f), ACT.Square).then_inc(n["squared"], 1)
        self.rms(act, 1, self.T, 6, 1 + self.kt)
        self.high(act)

    def high(self, act):
        if self.spread:
            for f in range(self.kt):
                act.wait_ge(self.k.nsem["normalised"], self.base["normalised"] + f + 1)
                self.spread.act(act, f)

    def dve(self, dve):
        nc, k, n, at = self.k.nc, self.k, self.k.nsem, self.base
        dve.wait_ge(n["rstd_steps"], at["rstd_steps"] + 2)
        if self.post:
            y, gain, res, tmp, _ = self.post
            for f in range(self.kt):
                if f >= 2:
                    dve.wait_ge(n["post_steps"], at["post_steps"] + 2 * f - 2)
                nc.vector.scalar_tensor_tensor(tmp[:, f % 2, :], y(f), k.col(gain + f), k.rstd[:, 0:SEQ], ALU.mult, ALU.mult).then_inc(n["post_steps"], 1)
                dve.wait_ge(n["post_steps"], at["post_steps"] + 2 * f + 1)
                nc.vector.tensor_tensor(res(f), res(f), tmp[:, f % 2, :], ALU.add).then_inc(n["post_steps"], 1)
            dve.wait_ge(n["rstd_steps"], at["rstd_steps"] + 4)
        for f in range(self.kt):
            nc.vector.scalar_tensor_tensor(self.dst(f), self.src(f), k.col(self.gain + f), k.rstd[:, 0:self.T],
                                           ALU.mult, ALU.mult).then_inc(n["normalised"], 1)
            if self.spread and f:
                self.spread.dve(dve, f - 1)
        if self.spread:
            self.spread.dve(dve, self.kt - 1)


class StepSizes:

    def __init__(self, k, dts, ctx):
        self.k, self.dts = k, dts
        self.n = CHUNKS * SSM_HEADS
        self.raw, self.e, self.u, self.r, self.big = (
            k.sb("dt_" + x, [P, CHUNKS, SSM_HEADS], F32, ctx) for x in ("raw", "e", "u", "r", "big"))
        self.s_pe, self.s_act = k.sem("dt_products"), k.sem("dt_scalar")
        self.steps = Steps(k.sem("dt_steps"))

    def pe_raw(self, pe):
        nc, k = self.k.nc, self.k
        for c in range(CHUNKS):
            for f in range(2 * KT):
                m = nc.tensor.matmul(k.ps[:, 2, c * SSM_HEADS:(c + 1) * SSM_HEADS], k.h_parts[:, f, c * P:(c + 1) * P].bitcast(F32),
                                     k.wdt[:, f % KT, :], start=f == 0, stop=f == 2 * KT - 1)
        m.then_inc(self.s_pe, 1)

    def pe_sums(self, pe):
        nc, k, n = self.k.nc, self.k, self.n
        pe.wait_ge(self.steps.sem, 13)
        a_all = self.dts[:, 0, :, :].rearrange("p c h -> p (c h)")
        nc.tensor.matmul(k.ps[:, 3, 0:n], k.tri, a_all, start=True, stop=True)
        nc.tensor.matmul(k.ps[:, 4, 0:n], k.ones, a_all, start=True, stop=True).then_inc(self.s_pe, 1)

    def act_softplus(self, act):
        nc = self.k.nc
        act.wait_ge(self.steps.sem, 3)
        nc.scalar.activation(self.e[:], self.e[:], ACT.Exp, scale=-1.0).then_inc(self.s_act, 1)
        act.wait_ge(self.steps.sem, 4)
        nc.scalar.activation(self.big[:], self.u[:], ACT.Ln).then_inc(self.s_act, 1)

    def act_decays(self, act):
        nc, dts = self.k.nc, self.dts
        act.wait_ge(self.steps.sem, 15)
        nc.scalar.activation(dts[:, 3, :, :], self.e[:], ACT.Exp).then_inc(self.s_act, 1)
        nc.scalar.activation(dts[:, 4, :, :], self.k.ps[:, 4, 0:self.n].rearrange("p (c h) -> p c h", c=CHUNKS), ACT.Exp).then_inc(self.s_act, 1)

    def dve(self, dve):
        k, n, dts, steps = self.k, self.n, self.dts, self.steps
        raw, e, u, r, big = self.raw, self.e, self.u, self.r, self.big

        def do(ins):
            steps.mark(ins)
            steps.settle(dve)

        def head(q):
            return k.drow[:, q:q + 1, :].to_broadcast([P, CHUNKS, SSM_HEADS])
        v = k.nc.vector
        dve.wait_ge(self.s_pe, 1)
        do(v.tensor_tensor(raw[:], k.ps[:, 2, 0:n].rearrange("p (c h) -> p c h", c=CHUNKS), head(1), ALU.add))
        do(v.tensor_scalar(r[:], raw[:], -1.0, None, ALU.mult))
        do(v.tensor_tensor(e[:], raw[:], r[:], ALU.max))
        dve.wait_ge(self.s_act, 1)
        do(v.tensor_scalar(u[:], e[:], 1.0, None, ALU.add))
        dve.wait_ge(self.s_act, 2)
        do(v.tensor_scalar(u[:], u[:], 1.0, None, ALU.subtract))
        do(v.tensor_scalar(r[:], u[:], 1e-30, None, ALU.max))
        do(v.reciprocal(r[:], r[:]))
        do(v.tensor_tensor(r[:], r[:], big[:], ALU.mult))
        do(v.scalar_tensor_tensor(r[:], u[:], 0.0, r[:], ALU.is_le, ALU.add))
        do(v.tensor_tensor(r[:], r[:], e[:], ALU.mult))
        do(v.scalar_tensor_tensor(dts[:, 2, :, :], raw[:], 0.0, r[:], ALU.max, ALU.add))
        do(v.tensor_copy(u[:], dts[:, 2, :, :]))
        do(v.tensor_tensor(dts[:, 0, :, :], u[:], head(3), ALU.mult))
        dve.wait_ge(self.s_pe, 2)
        pre, tot = (k.ps[:, b, 0:n].rearrange("p (c h) -> p c h", c=CHUNKS) for b in (3, 4))
        do(v.tensor_copy(dts[:, 1, :, :], pre))
        do(v.tensor_tensor(e[:], tot, dts[:, 1, :, :], ALU.subtract))
        dve.wait_ge(self.s_act, 4)


def ssm(k, st, nxt, pre):
    nc, ps = k.nc, k.ps
    v = nc.vector
    with ExitStack() as ctx:
        def sb(n, s, d=F32):
            return k.sb("ssm_" + n, s, d, ctx)
        u, cv, zs = k.wide[:, 16:20, 0:3 + SEQ], sb("conv", [P, 4, SEQ]), k.wide[:, 20:22, 0:SEQ]
        gs = sb("group", [P, 5 * CHUNKS, RPG])
        xt, xd, bt = sb("xdt", [P, 2 * P]), sb("xend", [P, 2 * P]), sb("btok", [P, P])
        cbm, seg, mm = sb("cb", [P, P]), sb("seg", [P, RPG, P]), sb("m", [P, RPG, P])
        ebc, cs = sb("ebc", [P, RPG, P]), sb("cs", [P, RPG, P])
        hs, ht, yg = sb("state", [P, 2 * P]), sb("statet", [P, 2 * P]), sb("yg", [P, 2, SEQ])
        sem = {x: k.sem("ssm_" + x) for x in (
            "lin_done", "lin_free", "conv", "silu", "group", "tr", "cb", "bc", "xt", "xd", "cbm", "seg", "m",
            "bt", "ebc", "dec", "cs", "y", "state", "gate")}
        steps = Steps(k.sem("ssm_steps"))
        dts = sb("dts", [P, 5, CHUNKS, SSM_HEADS])
        dt = StepSizes(k, dts, ctx)
        sqg = sb("squares", [P, SEQ])
        n = k.nsem
        b_acc, b_sq = k.ncount["accumulated"], k.ncount["squared"]
        k.ncount["accumulated"] += 1 + 2 * GROUPS
        k.ncount["squared"] += 2 * GROUPS
        TR, CB, BC, Y, S = ps[:, 2, :], ps[:, 3, :], ps[:, 4, :], (ps[:, 5, :], ps[:, 6, :]), ps[:, 7, :]

        def scal(q, c, r=None):
            return gs[:, q * CHUNKS + c, :] if r is None else gs[:, q * CHUNKS + c, r:r + 1]

        with nc.Block() as block:
            @block.sync
            def _(sp):
                k.stream(sp, st, nxt)

            @block.tensor
            def _(pe):
                def piece(i, p):
                    k.split_ready(pe, st, i, p)
                    wait(pe, sem["lin_free"], 6 * i + p - 1)
                    first = isinstance(i, int) and i == p == 0
                    k.product(st, p, ps[:, p % 2, :], k.hx(0, SEQ), before=(lambda f: pre.ready(pe, f)) if first else None).then_inc(sem["lin_done"], 1)

                def prep(s, c):
                    n, t = 4 * s + c, slice(c * P, (c + 1) * P)
                    wait(pe, sem["silu"], 4 * s + 4)
                    wait(pe, sem["xt"], n)
                    wait(pe, sem["bt"], n)
                    for q in range(3):
                        m = nc.tensor.transpose(TR[:, q * P:(q + 1) * P], cv[:, q, t], k.ident)
                    m.then_inc(sem["tr"], 1)
                    wait(pe, sem["cbm"], n)
                    nc.tensor.matmul(CB[:, 0:P], cv[:, 2, t], cv[:, 3, t], start=True, stop=True).then_inc(sem["cb"], 1)
                    wait(pe, sem["ebc"], 3 * s + max(c - 1, 0))
                    wait(pe, sem["seg"], n)
                    for r in range(RPG):
                        m = nc.tensor.matmul(BC[:, r * P:(r + 1) * P], scal(0, c, r).to_broadcast([P, P]), k.tri, start=True, stop=True)
                    m.then_inc(sem["bc"], 1)

                def out(s, c):
                    n = 4 * s + c
                    wait(pe, sem["m"], n + 1)
                    if c == 0:
                        wait(pe, sem["gate"], 2 * s)
                    else:
                        wait(pe, sem["state"], 3 * s + c)
                        wait(pe, sem["cs"], 3 * s + c)
                    for r in range(RPG):
                        o = Y[r // 2][64 * (r % 2):64 * (r % 2) + 64, c * P:(c + 1) * P]
                        m = nc.tensor.matmul(o, xt[:, 64 * r:64 * r + 64], mm[:, r, :], start=True, stop=c == 0)
                        if c:
                            m = nc.tensor.matmul(o, hs[:, 64 * r:64 * r + 64], cs[:, r, :], start=False, stop=True)
                    if c < CHUNKS - 1:
                        wait(pe, sem["bt"], n + 1)
                        wait(pe, sem["xd"], n + 1)
                        m = nc.tensor.matmul(S[:, 0:2 * P], bt[:], xd[:], start=True, stop=True)
                    m.then_inc(sem["y"], 1)

                def step(i, lin=True, scan=True):
                    for p in range(6):
                        if lin:
                            piece(i, p)
                        if not scan and p == 0:
                            dt.pe_raw(pe)
                        if not scan and p == 2:
                            dt.pe_sums(pe)
                        if scan:
                            if 1 <= p <= 4:
                                out(i - 1, p - 1)
                            if p <= 3:
                                prep(i - 1, p)
                pre.pe(pe)
                step(0, scan=False)
                step(1)
                with pe.Fori(2, GROUPS) as i:
                    step(i)
                step(GROUPS, lin=False)

            @block.scalar
            def _(act):
                def evict(i, p):
                    act.wait_ge(sem["lin_done"], 6 * i + p + 1)
                    if p < 4:
                        wait(act, sem["conv"], 4 * i - 3 + p if not isinstance(i, int) or i else 0)
                        nc.scalar.activation(u[:, p, 3:3 + SEQ], ps[:, p % 2, :], ACT.Copy).then_inc(sem["lin_free"], 1)
                    else:
                        wait(act, sem["gate"], 2 * i)
                        nc.scalar.activation(zs[:, p - 4, :], ps[:, p % 2, :], ACT.Silu).then_inc(sem["lin_free"], 1)

                def chunk(s, c):
                    n = 4 * s + c
                    act.wait_ge(sem["xt"], n + 1)
                    wait(act, sem["y"], n)
                    nc.scalar.activation(bt[:], TR[:, 2 * P:3 * P], ACT.Copy).then_inc(sem["bt"], 1)
                    act.wait_ge(sem["seg"], n + 1)
                    nc.scalar.activation(seg[:], seg[:], ACT.Exp).then_inc(sem["dec"], 1)
                    if c:
                        wait(act, sem["cs"], 3 * s + c - 1)
                        nc.scalar.activation(ebc[:].rearrange("p r l -> p (r l)"), BC, ACT.Exp).then_inc(sem["ebc"], 1)

                def step(i, lin=True, scan=True):
                    if scan:
                        for q in range(4):
                            act.wait_ge(sem["conv"], 4 * (i - 1) + q + 1)
                            nc.scalar.activation(cv[:, q, :], cv[:, q, :], ACT.Silu).then_inc(sem["silu"], 1)
                    for p in range(6):
                        if not scan and p == 0:
                            dt.act_softplus(act)
                        if not scan and p == 3:
                            dt.act_decays(act)
                        if lin:
                            evict(i, p)
                            k.high(act, st, st.after(i, p, st.depth))
                        if scan and p < 4:
                            chunk(i - 1, p)
                k.high_first(act, st)
                pre.act(act)
                step(0, scan=False)
                step(1)
                with act.Fori(2, GROUPS - 1) as i:
                    step(i)
                step(GROUPS - 1)
                step(GROUPS, lin=False)

            @block.gpsimd
            def _(pool):
                def scaled_c(s, c):
                    pool.wait_ge(sem["ebc"], 3 * s + c)
                    wait(pool, sem["y"], 4 * s + c)
                    nc.gpsimd.tensor_tensor(cs[:], ebc[:], cv[:, 3:4, c * P:(c + 1) * P].to_broadcast([P, RPG, P]),
                                            ALU.mult).then_inc(sem["cs"], 1)

                def squares(s):
                    for j in range(2):
                        pool.wait_ge(sem["gate"], 2 * s + j + 1)
                        nc.gpsimd.tensor_tensor(sqg[:], yg[:, j, :], yg[:, j, :], ALU.mult).then_inc(n["squared"], 1)
                        pool.wait_ge(n["squared"], 2 * s + b_sq + j + 1)
                        nc.gpsimd.tensor_tensor(k.acc[:, 0:SEQ], k.acc[:, 0:SEQ], sqg[:], ALU.add).then_inc(n["accumulated"], 1)
                        pool.wait_ge(n["accumulated"], 2 * s + b_acc + j + 2)

                def step(i, lin=True, scan=True):
                    for p in range(6):
                        if lin:
                            k.low(pool, st, st.after(i, p, st.depth))
                        if scan and 1 <= p < CHUNKS:
                            scaled_c(i - 1, p)
                    if scan:
                        squares(i - 1)
                for u in range(st.depth):
                    k.low(pool, st, (0, u))
                pool.wait_ge(n["rstd_steps"], k.ncount["rstd_steps"])
                nc.gpsimd.memset(k.acc[:], 0.0).then_inc(n["accumulated"], 1)
                pool.wait_ge(n["accumulated"], b_acc + 1)
                step(0, scan=False)
                step(1)
                with pool.Fori(2, GROUPS - 1) as i:
                    step(i)
                step(GROUPS - 1)
                step(GROUPS, lin=False)

            @block.vector
            def _(dve):
                def do(ins):
                    steps.mark(ins)
                    steps.settle(dve)

                def conv(s, q):
                    tile = (2 * s, 2 * s + 1, 16 + s, 24 + s)[q]
                    dve.wait_ge(sem["lin_free"], 6 * s + q + 1)
                    acc = cv[:, q, :]
                    do(v.tensor_scalar(acc, u[:, q, 0:SEQ], k.col(V_CW + tile), k.col(V_CB + tile), ALU.mult, ALU.add))
                    for j in range(1, 4):
                        ins = v.scalar_tensor_tensor(acc, u[:, q, j:j + SEQ], k.col(V_CW + 32 * j + tile), acc, ALU.mult, ALU.add)
                        if j < 3:
                            do(ins)
                        else:
                            ins.then_inc(sem["conv"], 1)

                def chunk(s, c):
                    n, b4 = 4 * s + c, [P, RPG, 64]
                    dve.wait_ge(sem["tr"], n + 1)
                    wait(dve, sem["y"], n)
                    x4 = xt[:].rearrange("p (r d) -> p r d", r=RPG)
                    v.tensor_tensor(x4, TR[:, 0:2 * P].rearrange("p (r d) -> p r d", r=RPG),
                                    scal(2, c).unsqueeze(2).to_broadcast(b4), ALU.mult).then_inc(sem["xt"], 1)
                    dve.wait_ge(sem["cb"], n + 1)
                    v.tensor_tensor(cbm[:], CB[:, 0:P], k.tri, ALU.mult).then_inc(sem["cbm"], 1)
                    dve.wait_ge(sem["xt"], n + 1)
                    v.tensor_tensor(xd[:].rearrange("p (r d) -> p r d", r=RPG), x4,
                                    scal(3, c).unsqueeze(2).to_broadcast(b4), ALU.mult).then_inc(sem["xd"], 1)
                    dve.wait_ge(sem["bc"], n + 1)
                    for r in range(RPG):
                        ins = v.tensor_scalar(seg[:, r, :], BC[:, r * P:(r + 1) * P], scal(1, c, r), 0.0, ALU.subtract, ALU.min)
                    ins.then_inc(sem["seg"], 1)
                    dve.wait_ge(sem["dec"], n + 1)
                    dve.wait_ge(sem["cbm"], n + 1)
                    v.tensor_tensor(mm[:], seg[:], cbm[:].unsqueeze(1).to_broadcast([P, RPG, P]), ALU.mult).then_inc(sem["m"], 1)
                    if c == CHUNKS - 1:
                        return
                    if c:
                        do(v.tensor_tensor(ht[:].rearrange("p (r d) -> p r d", r=RPG), hs[:].rearrange("p (r d) -> p r d", r=RPG),
                                           scal(4, c).unsqueeze(2).to_broadcast(b4), ALU.mult))
                        dve.wait_ge(sem["y"], n + 1)
                        v.tensor_tensor(hs[:], ht[:], S[:, 0:2 * P], ALU.add).then_inc(sem["state"], 1)
                    else:
                        dve.wait_ge(sem["y"], n + 1)
                        v.tensor_copy(hs[:], S[:, 0:2 * P]).then_inc(sem["state"], 1)
                    dve.wait_ge(sem["state"], 3 * s + c + 1)

                def gate(s):
                    dve.wait_ge(sem["y"], 4 * s + 4)
                    dve.wait_ge(sem["lin_free"], 6 * s + 6)
                    for j in range(2):
                        wait(dve, n["squared"], 2 * s + j - 1 + b_sq if not isinstance(s, int) or s else 0)
                        do(v.scalar_tensor_tensor(yg[:, j, :], cv[:, j, :], k.dexp[:, bass.ds(2 * s + j, 1)], Y[j], ALU.mult, ALU.add))
                        do(v.tensor_tensor(yg[:, j, :], yg[:, j, :], zs[:, j, :], ALU.mult))
                        v.tensor_copy(k.wide[:, bass.ds(2 * s + j, 1), 0:SEQ].rearrange("p a t -> p (a t)"), yg[:, j, :]).then_inc(sem["gate"], 1)

                def step(s):
                    steps.begin(s)
                    do(v.tensor_copy(gs[:], dts[:].rearrange("p q c h -> p (q c) h")[:, :, bass.ds(RPG * s, RPG)]))
                    for q in range(4):
                        conv(s, q)
                    for c in range(CHUNKS):
                        chunk(s, c)
                    gate(s)
                    steps.end()
                v.memset(u[:, :, 0:3], 0.0).then_inc(sem["group"], 1)
                dve.wait_ge(sem["group"], 1)
                pre.dve(dve)
                dt.dve(dve)
                step(0)
                with dve.Fori(1, GROUPS) as s:
                    step(s)


def project(k, name, st, nxt, ksplit, x, parts, T, store, stored, pre=None):
    nc, ps = k.nc, k.ps
    hs = halves(T)
    per = st.units // ksplit * len(hs)
    tiles = per // len(hs)
    s_done, s_free, s_half = k.sem(name + "_done"), k.sem(name + "_free"), k.sem(name + "_half")
    n = k.nsem
    spread = pre.spread if pre else Spread(k, st.kt * ksplit, x, *parts)
    b_sq, b_acc = k.ncount["squared"], k.ncount["accumulated"]
    k.ncount["squared"] += tiles * st.iterations
    k.ncount["accumulated"] += 1 + tiles * st.iterations
    with nc.Block() as block:
        @block.sync
        def _(sp):
            k.stream(sp, st, nxt)

        @block.gpsimd
        def _(pool):
            k.low_all(pool, st)

        @block.tensor
        def _(pe):
            def step(i):
                for u in range(st.units):
                    tile, part = divmod(u, ksplit)
                    k.split_ready(pe, st, i, u)
                    for b, (c, w) in enumerate(hs):
                        q = tile * len(hs) + b
                        if part == 0:
                            wait(pe, s_free, per * i + q - 1)
                        first = isinstance(i, int) and tile == b == 0
                        xs = spread.parts(c, w)
                        m = k.product(st, u, ps[:, q % (2 * ksplit), 0:w], lambda f: xs(part * st.kt + f), start=part == 0, stop=part == ksplit - 1,
                                      before=(lambda f: spread.ready(pe, part * st.kt + f)) if first else None)
                        if part == ksplit - 1:
                            m.then_inc(s_done, 1)
                        elif b == len(hs) - 1:
                            m.then_inc(s_half, 1)
            if pre:
                pre.pe(pe)
            step(0)
            with pe.Fori(1, st.iterations) as i:
                step(i)

        @block.scalar
        def _(act):
            def step(i):
                for u in range(st.units):
                    tile, part = divmod(u, ksplit)
                    if part == ksplit - 1:
                        act.wait_ge(s_free, per * i + (tile + 1) * len(hs))
                    else:
                        act.wait_ge(s_half, tiles * i + tile + 1)
                    k.high(act, st, st.after(i, u, st.depth))
                    if part == ksplit - 1:
                        nc.scalar.activation(k.sq[:, 0:T], stored(tiles * i + tile), ACT.Square).then_inc(n["squared"], 1)
            k.high_first(act, st)
            if pre:
                pre.act(act)
            else:
                for f in range(st.kt * ksplit):
                    spread.act(act, f)
            step(0)
            if st.iterations > 2:
                with act.Fori(1, st.iterations - 1) as i:
                    step(i)
            step(st.iterations - 1)

        @block.vector
        def _(dve):
            if pre:
                pre.dve(dve)
            else:
                for f in range(st.kt * ksplit):
                    spread.dve(dve, f)
            nc.vector.memset(k.acc[:], 0.0).then_inc(n["accumulated"], 1)
            dve.wait_ge(n["accumulated"], b_acc + 1)
            with dve.Fori(0, st.iterations) as i:
                for t in range(tiles):
                    for b, (c, w) in enumerate(hs):
                        q = t * len(hs) + b
                        dve.wait_ge(s_done, per * i + q + 1)
                        store(tiles * i + t, c, w, ps[:, q % (2 * ksplit), 0:w]).then_inc(s_free, 1)
                    dve.wait_ge(n["squared"], tiles * i + b_sq + t + 1)
                    nc.vector.tensor_tensor(k.acc[:, 0:T], k.acc[:, 0:T], k.sq[:, 0:T], ALU.add).then_inc(n["accumulated"], 1)
                    dve.wait_ge(n["accumulated"], tiles * i + b_acc + t + 2)


def swa(k, st, nxt, pre):
    nc, ps = k.nc, k.ps
    v = nc.vector
    with ExitStack() as ctx:
        def sb(n, s, d=F32):
            return k.sb("swa_" + n, s, d, ctx)
        raw, rop = sb("raw", [P, 3, SEQ]), sb("roped", [P, 3, SEQ])
        vT, vt, gate = sb("vT", [P, SEQ]), sb("v", [P, 4, 64]), k.wide[:, 8:16, 0:SEQ]
        t1, t2 = sb("t1", [P, SEQ]), sb("t2", [P, SEQ])
        p, pn, pt = sb("p", [P, 4, 2 * P]), sb("pn", [P, 4, 2 * P]), sb("pt", [P, 4, 2, P])
        mx, nm, den, es, rd = (sb(x, [P, 4]) for x in ("mx", "nm", "den", "es", "rd"))
        nsg = sb("nsg", [P, 4])
        sem = {x: k.sem("swa_" + x) for x in (
            "lin_done", "lin_free", "rot", "rope", "vtr", "v", "s", "nm", "exp", "es", "pn", "t", "pt", "pv", "out")}
        steps = Steps(k.sem("swa_steps"))
        S = ps[:, 2:4, :].rearrange("p b (x j) -> p (b x) j", x=2)
        PT = ps[:, 4:6, :].rearrange("p b (x j) -> p (b x) j", x=2)
        O = (ps[:, 6, :], ps[:, 7, :])
        order = (0, 2, 3)
        HEAD = (0, 2, 1, 3)

        with nc.Block() as block:
            @block.sync
            def _(sp):
                k.stream(sp, st, nxt)

            @block.gpsimd
            def _(pool):
                k.low_all(pool, st)

            @block.tensor
            def _(pe):
                def piece(i, q):
                    k.split_ready(pe, st, i, q)
                    wait(pe, sem["lin_free"], 6 * i + q - 1)
                    first = isinstance(i, int) and i == q == 0
                    k.product(st, q, ps[:, q % 2, :], k.hx(0, SEQ), before=(lambda f: pre.ready(pe, f)) if first else None).then_inc(sem["lin_done"], 1)

                def rot(s, q):
                    pe.wait_ge(sem["lin_free"], 6 * s + order[q] + 1)
                    if q == 0:
                        wait(pe, sem["pt"], 4 * s)
                    if q == 2:
                        pe.wait_ge(sem["rope"], 3 * s + 1)
                    nc.tensor.matmul(ps[:, 4 + q % 2, :], k.rot1, raw[:, q, :], start=True, stop=True).then_inc(sem["rot"], 1)

                def vtr(s):
                    pe.wait_ge(sem["lin_free"], 6 * s + 2)
                    wait(pe, sem["exp"], 16 * s)
                    for t in range(4):
                        m = nc.tensor.transpose(ps[:, 2, t * P:(t + 1) * P], vT[:, t * P:(t + 1) * P], k.ident)
                    m.then_inc(sem["vtr"], 1)

                def scores(s, n):
                    if n == 0:
                        pe.wait_ge(sem["v"], s + 1)
                        pe.wait_ge(sem["rope"], 3 * s + 3)
                    else:
                        pe.wait_ge(sem["exp"], 16 * s + 4 * n)
                    k0 = 0 if n else P
                    for x, r in enumerate(HEAD):
                        h = slice(64 * (r % 2), 64 * (r % 2) + 64)
                        nc.tensor.matmul(S[:, x, k0:2 * P], k.identb[:], k.maskb[:, k0:2 * P], start=True, stop=False)
                        m = nc.tensor.matmul(S[:, x, k0:2 * P], rop[h, 1 + r // 2, n * P:(n + 1) * P],
                                             rop[h, 0, (n - 1) * P + k0:(n + 1) * P], start=False, stop=True)
                    m.then_inc(sem["s"], 1)

                def trans(s, n):
                    pe.wait_ge(sem["pn"], 4 * s + n + 1)
                    wait(pe, sem["pt"], 4 * s + n)
                    for r in range(4):
                        for b in range(0 if n else 1, 2):
                            m = nc.tensor.transpose(PT[:, r, b * P:(b + 1) * P], pn[:, r, b * P:(b + 1) * P], k.ident)
                    m.then_inc(sem["t"], 1)

                def pv(s, n):
                    pe.wait_ge(sem["pt"], 4 * s + n + 1)
                    if n == 0:
                        wait(pe, sem["out"], 2 * s)
                    for x, r in enumerate(HEAD):
                        o = O[r // 2][64 * (r % 2):64 * (r % 2) + 64, n * P:(n + 1) * P]
                        for b in range(0 if n else 1, 2):
                            m = nc.tensor.matmul(o, vt[:, n - 1 + b, :], pt[:, x, b, :], start=b == 0 or not n, stop=b == 1)
                    m.then_inc(sem["pv"], 1)

                def step(i, lin=True, att=True):
                    s = i - 1
                    for q in range(6):
                        if att:
                            if q == 0:
                                rot(s, 0), rot(s, 1)
                            if q == 1:
                                rot(s, 2), vtr(s)
                            if q == 2:
                                scores(s, 0)
                            if q == 3:
                                trans(s, 0), scores(s, 1)
                            if q == 4:
                                pv(s, 0), trans(s, 1), scores(s, 2)
                            if q == 5:
                                pv(s, 1), trans(s, 2), scores(s, 3)
                        if lin:
                            piece(i, q)
                    if att:
                        pv(s, 2), trans(s, 3), pv(s, 3)
                pre.pe(pe)
                step(0, att=False)
                step(1)
                with pe.Fori(2, KV) as i:
                    step(i)
                step(KV, lin=False)

            @block.scalar
            def _(act):
                def evict(i, q):
                    act.wait_ge(sem["lin_done"], 6 * i + q + 1)
                    src = ps[:, q % 2, :]
                    if q in order:
                        wait(act, sem["rope"], 3 * i - 2 + order.index(q) if not isinstance(i, int) or i else 0)
                        nc.scalar.activation(raw[:, order.index(q), :], src, ACT.Copy).then_inc(sem["lin_free"], 1)
                    elif q == 1:
                        wait(act, sem["vtr"], i)
                        nc.scalar.activation(vT[:], src, ACT.Copy).then_inc(sem["lin_free"], 1)
                    else:
                        nc.scalar.activation(gate[:, bass.ds(2 * i + q - 4, 1), :].rearrange("p a t -> p (a t)"), src, ACT.Silu).then_inc(sem["lin_free"], 1)

                def vtok(s):
                    act.wait_ge(sem["vtr"], s + 1)
                    wait(act, sem["pv"], 4 * s)
                    nc.scalar.activation(vt[:], ps[:, 2, :].rearrange("p (t d) -> p t d", t=4)[:, :, 0:64], ACT.Copy).then_inc(sem["v"], 1)

                def exps(s, n):
                    act.wait_ge(sem["nm"], 4 * s + n + 1)
                    wait(act, sem["pn"], 4 * s + n)
                    k0 = 0 if n else P
                    for r in range(4):
                        nc.scalar.activation(p[:, r, k0:2 * P], S[:, r, k0:2 * P], ACT.Exp, bias=nm[:, r:r + 1], scale=0.125,
                                             accum_out=den[:, r:r + 1]).then_inc(sem["exp"], 1)
                    nc.scalar.activation(es[:], es[:], ACT.Exp).then_inc(sem["es"], 1)

                def store_pt(s, n):
                    act.wait_ge(sem["t"], 4 * s + n + 1)
                    wait(act, sem["pv"], 4 * s + n)
                    b0 = 0 if n else 1
                    nc.scalar.activation(pt[:, :, b0:2, :], PT.rearrange("p r (b q) -> p r b q", b=2)[:, :, b0:2, :],
                                         ACT.Copy).then_inc(sem["pt"], 1)

                def step(i, lin=True, att=True):
                    s = i - 1
                    for q in range(6):
                        if att:
                            if q == 2:
                                vtok(s)
                                exps(s, 0)
                            if q >= 3:
                                store_pt(s, q - 3)
                                exps(s, q - 2)
                        if lin:
                            evict(i, q)
                            k.high(act, st, st.after(i, q, st.depth))
                    if att:
                        store_pt(s, 3)
                k.high_first(act, st)
                pre.act(act)
                step(0, att=False)
                step(1)
                with act.Fori(2, KV - 1) as i:
                    step(i)
                step(KV - 1)
                step(KV, lin=False)

            @block.vector
            def _(dve):
                def do(ins):
                    steps.mark(ins)
                    steps.settle(dve)

                def step(s):
                    steps.begin(s)
                    do(v.tensor_copy(nsg[:].rearrange("p (b f) -> p f b", b=2),
                                     k.nsink[:, bass.ds(4 * s, 4)].rearrange("p (f b) -> p f b", b=2)))
                    for q in range(3):
                        dve.wait_ge(sem["lin_free"], 6 * s + order[q] + 1)
                        do(v.tensor_tensor(t1[:], raw[:, q, :], k.cos1[:], ALU.mult))
                        dve.wait_ge(sem["rot"], 3 * s + q + 1)
                        do(v.tensor_tensor(t2[:], ps[:, 4 + q % 2, :], k.sin1[:], ALU.mult))
                        v.tensor_tensor(rop[:, q, :], t1[:], t2[:], ALU.add).then_inc(sem["rope"], 1)
                        dve.wait_ge(sem["rope"], 3 * s + q + 1)
                    for n in range(4):
                        k0 = 0 if n else P
                        dve.wait_ge(sem["s"], 4 * s + n + 1)
                        do(v.reduce_max(mx[:], S[:, :, k0:2 * P], AX.X))
                        do(v.scalar_tensor_tensor(nm[:], mx[:], -0.125, nsg[:], ALU.mult, ALU.min))
                        v.tensor_tensor(es[:], nm[:], nsg[:], ALU.subtract).then_inc(sem["nm"], 1)
                        dve.wait_ge(sem["es"], 4 * s + n + 1)
                        do(v.tensor_tensor(rd[:], den[:], es[:], ALU.add))
                        do(v.reciprocal(rd[:], rd[:]))
                        wait(dve, sem["t"], 4 * s + n)
                        w = 2 * P - k0
                        v.tensor_tensor(pn[:, :, k0:2 * P], p[:, :, k0:2 * P], rd[:].unsqueeze(2).to_broadcast([P, 4, w]),
                                        ALU.mult).then_inc(sem["pn"], 1)
                    dve.wait_ge(sem["pv"], 4 * s + 4)
                    dve.wait_ge(sem["lin_free"], 6 * s + 6)
                    for j in range(2):
                        v.tensor_tensor(k.wide[:, bass.ds(2 * s + j, 1), 0:SEQ].rearrange("p a t -> p (a t)"), O[j],
                                        gate[:, bass.ds(2 * s + j, 1), :].rearrange("p a t -> p (a t)"), ALU.mult).then_inc(sem["out"], 1)
                    steps.end()
                pre.dve(dve)
                step(0)
                with dve.Fori(1, KV) as s:
                    step(s)


def pairs(k, name, st, nxt, diff, pre=None, mb=None):
    nc, ps = k.nc, k.ps
    v = nc.vector
    NI = 8
    with ExitStack() as ctx:
        def sb(n, s, d=F32):
            return k.sb(f"{name}_{n}", s, d, ctx)
        raw, rop, t1, t2 = k.wide[:, 8:10, :], k.wide[:, 10:12, :], k.wide[:, 12, :], k.wide[:, 13, :]
        vT, vt = k.wide[:, 14, :], sb("v", [P, 5, P])
        maps = 1 if diff else 2
        p, pn = k.wide[:, 15:17, :], k.wide[:, 17:17 + maps, :]
        pt, mx, nm, den, rd = sb("pt", [P, maps, 512]), sb("mx", [P, 2]), sb("nm", [P, 2]), sb("den", [P, 2]), sb("rd", [P, 2])
        ptl = sb("ptl", [META, maps, META])
        osb, osq, lnv, rstd = (k.wide[:, j, :] for j in range(18, 22)) if diff else (None,) * 4
        sem = {x: k.sem(f"{name}_{x}") for x in (
            "lin_done", "lin_free", "rot", "rope", "vtr", "v", "s", "nm", "exp", "pn", "t", "pt", "pv", "o", "osq", "oss", "rstd", "out")}
        steps = Steps(k.sem(name + "_steps"))
        S = ps[:, 2:6, :].rearrange("p (c x) j -> p c (x j)", c=2)
        TP = ps[:, 6:8, :]
        O = ps[:, 7, :] if diff else ps[:, 3, P:3 * P]

        def blocks(n):
            return [(b, *TILES[b]) for b in range(n + 1)]

        with nc.Block() as block:
            @block.sync
            def _(sp):
                k.stream(sp, st, nxt)

            @block.gpsimd
            def _(pool):
                k.low_all(pool, st)

            @block.tensor
            def _(pe):
                def piece(i, q):
                    u, b = divmod(q, 2)
                    k.split_ready(pe, st, i, u)
                    wait(pe, sem["lin_free"], 6 * i + q - 1)
                    first = pre and isinstance(i, int) and i == q == 0
                    k.product(st, u, ps[:, b, 0:HALF], k.hx(b * HALF, HALF), before=(lambda f: pre.ready(pe, f)) if first else None).then_inc(sem["lin_done"], 1)

                def before(s):
                    pe.wait_ge(sem["lin_free"], 6 * s + 6)
                    wait(pe, sem["exp"], 10 * s)
                    if diff:
                        wait(pe, sem["rstd"], 2 * s)
                    wait(pe, sem["o"], 5 * s)
                    for q in range(2):
                        for b in range(2):
                            m = nc.tensor.matmul(ps[:, 2 + 2 * q + b, 0:HALF], k.rot2, raw[:, q, b * HALF:(b + 1) * HALF], start=True, stop=True)
                        m.then_inc(sem["rot"], 1)
                    wait(pe, sem["pt"], 5 * s)
                    for t, (c, n) in enumerate(TILES):
                        m = nc.tensor.transpose(ps[0:n, 6 + t // 4, (t % 4) * P:(t % 4 + 1) * P], vT[:, c:c + n], k.ident)
                    m.then_inc(sem["vtr"], 1)

                def scores(s, n):
                    c, nq = TILES[n]
                    N = c + nq
                    if n == 0:
                        pe.wait_ge(sem["rope"], 2 * s + 2)
                    for x in range(2):
                        h = slice(64 * x, 64 * x + 64)
                        for lo, hi in (((0, c), (c, N)) if diff else ((0, min(N, 512)), (512, N))):
                            if lo >= hi:
                                continue
                            masked = not diff or lo == c
                            m = nc.tensor.matmul(S[0:nq, x, lo:hi], rop[h, 0, c:N], rop[h, 1, lo:hi], start=True, stop=not masked)
                            if masked:
                                mask = k.maskb[0:nq, P:P + nq] if diff else mb[0:nq, n, lo:hi]
                                m = nc.tensor.matmul(S[0:nq, x, lo:hi], k.identb[0:nq, 0:nq], mask, start=False, stop=True)
                    m.then_inc(sem["s"], 1)

                def trans(s, n):
                    _, nq = TILES[n]
                    if n == 0:
                        pe.wait_ge(sem["v"], s + 1)
                    if n < 4:
                        wait(pe, sem["pt"], 5 * s + n)
                        pe.wait_ge(sem["pn"], 5 * s + n + 1)
                    if n == 3 and not diff:
                        pe.wait_ge(sem["o"], 5 * s + 3)
                    for x in range(maps):
                        for b, a, w in blocks(n):
                            m = nc.tensor.transpose(TP[0:w, x, b * nq:(b + 1) * nq], pn[0:nq, x, a:a + w], k.ident[0:nq, 0:nq])
                    m.then_inc(sem["t"], 1)

                def pv(s, n):
                    _, nq = TILES[n]
                    pe.wait_ge(sem["pt"], 5 * s + n + 1)
                    wait(pe, sem["o"], 5 * s + n)
                    if n == 3:
                        pe.wait_ge(sem["pn"], 5 * s + 5)
                    for x in range(maps):
                        d = slice(0, P) if diff else slice(64 * x, 64 * x + 64)
                        for b, a, w in blocks(n):
                            r = pt[0:w, x, b * nq:(b + 1) * nq] if b < 4 else ptl[:, x, :]
                            m = nc.tensor.matmul(O[d, 0:nq], vt[0:w, b, d], r, start=b == 0, stop=b == n)
                    m.then_inc(sem["pv"], 1)

                def step(i, lin=True, att=True):
                    s = i - 1
                    for q in range(6):
                        if att:
                            if q == 0:
                                before(s)
                            if q >= 3:
                                pv(s, q - 3)
                            if q >= 2:
                                trans(s, q - 2)
                            if 1 <= q <= 5:
                                scores(s, q - 1)
                        if lin:
                            piece(i, q)
                    if att:
                        pv(s, 3), trans(s, 4), pv(s, 4)
                        if diff:
                            pe.wait_ge(sem["osq"], s + 1)
                            pe.wait_ge(sem["exp"], 10 * s + 10)
                            for b in range(2):
                                m = nc.tensor.matmul(ps[:, 2 + b, 0:HALF], k.ones, osq[:, b * HALF:(b + 1) * HALF], start=True, stop=True)
                            m.then_inc(sem["oss"], 1)
                if pre:
                    pre.pe(pe)
                step(0, att=False)
                step(1)
                with pe.Fori(2, NI) as i:
                    step(i)
                step(NI, lin=False)

            @block.scalar
            def _(act):
                def evict(i, q):
                    u, b = divmod(q, 2)
                    act.wait_ge(sem["lin_done"], 6 * i + q + 1)
                    if u < 2:
                        wait(act, sem["rope"], 2 * i)
                        dst = raw[:, u, b * HALF:(b + 1) * HALF]
                    else:
                        wait(act, sem["vtr"], i)
                        dst = vT[:, b * HALF:(b + 1) * HALF]
                    nc.scalar.activation(dst, ps[:, b, 0:HALF], ACT.Copy).then_inc(sem["lin_free"], 1)

                def vtok(s):
                    act.wait_ge(sem["vtr"], s + 1)
                    wait(act, sem["pv"], 5 * s)
                    nc.scalar.activation(vt[:, 0:4, :].rearrange("p t d -> p (t d)"), ps[:, 6, :], ACT.Copy)
                    nc.scalar.activation(vt[0:META, 4, :], ps[0:META, 7, 0:P], ACT.Copy).then_inc(sem["v"], 1)

                def exps(s, n):
                    c, nq = TILES[n]
                    act.wait_ge(sem["nm"], 5 * s + n + 1)
                    wait(act, sem["pn"], 5 * s + n)
                    for x in range(2):
                        nc.scalar.activation(p[0:nq, x, 0:c + nq], S[0:nq, x, 0:c + nq], ACT.Exp, bias=nm[0:nq, x:x + 1], scale=0.125,
                                             accum_out=den[0:nq, x:x + 1]).then_inc(sem["exp"], 1)

                def store_pt(s, n):
                    _, nq = TILES[n]
                    act.wait_ge(sem["t"], 5 * s + n + 1)
                    wait(act, sem["pv"], 5 * s + n)
                    if n == 4:
                        nc.scalar.activation(ptl[:], TP[0:META, 0:maps, 4 * META:5 * META], ACT.Copy)
                    w = min(n + 1, 4) * nq
                    nc.scalar.activation(pt[:, :, 0:w], TP[:, 0:maps, 0:w], ACT.Copy).then_inc(sem["pt"], 1)

                def store_o(s, n):
                    c, nq = TILES[n]
                    act.wait_ge(sem["pv"], 5 * s + n + 1)
                    if diff and n == 0:
                        wait(act, sem["out"], s)
                    dst = osb[:, c:c + nq] if diff else k.wide[:, bass.ds(s, 1), c:c + nq].rearrange("p a t -> p (a t)")
                    nc.scalar.activation(dst, O[:, 0:nq], ACT.Copy).then_inc(sem["o"], 1)

                def step(i, lin=True, att=True):
                    s = i - 1
                    for q in range(6):
                        if att:
                            if q == 0:
                                vtok(s)
                            if q >= 3:
                                store_o(s, q - 3)
                            if q >= 2:
                                store_pt(s, q - 2)
                            if q >= 1:
                                exps(s, q - 1)
                        if lin:
                            evict(i, q)
                            if q % 2:
                                k.high(act, st, st.after(i, q // 2, st.depth))
                    if att:
                        store_o(s, 3), store_pt(s, 4), store_o(s, 4)
                        if diff:
                            act.wait_ge(sem["o"], 5 * s + 5)
                            nc.scalar.activation(osq, osb, ACT.Square).then_inc(sem["osq"], 1)
                            act.wait_ge(sem["oss"], s + 1)
                            wait(act, sem["out"], s)
                            nc.scalar.activation(both(lnv), ps[:, 2:4, 0:HALF], ACT.Ln, scale=1.0 / P, bias=k.eps[:]).then_inc(sem["rstd"], 1)
                            act.wait_ge(sem["rstd"], 2 * s + 1)
                            nc.scalar.activation(rstd, lnv, ACT.Exp, scale=-0.5).then_inc(sem["rstd"], 1)
                k.high_first(act, st)
                if pre:
                    pre.act(act)
                step(0, att=False)
                step(1)
                with act.Fori(2, NI - 1) as i:
                    step(i)
                step(NI - 1)
                step(NI, lin=False)

            @block.vector
            def _(dve):
                def do(ins):
                    steps.mark(ins)
                    steps.settle(dve)

                def step(s):
                    steps.begin(s)
                    for q in range(2):
                        dve.wait_ge(sem["lin_free"], 6 * s + 2 * q + 2)
                        do(v.tensor_tensor(t1, raw[:, q, :], k.cos2, ALU.mult))
                        dve.wait_ge(sem["rot"], 2 * s + q + 1)
                        do(v.tensor_tensor(both(t2), ps[:, 2 + 2 * q:4 + 2 * q, 0:HALF], both(k.sin2), ALU.mult))
                        v.tensor_tensor(rop[:, q, :], t1, t2, ALU.add).then_inc(sem["rope"], 1)
                        dve.wait_ge(sem["rope"], 2 * s + q + 1)
                    for n, (c, nq) in enumerate(TILES):
                        N = c + nq
                        dve.wait_ge(sem["s"], 5 * s + n + 1)
                        if diff:
                            do(v.reduce_max(mx[0:nq, :], S[0:nq, :, 0:N], AX.X))
                        else:
                            for x in range(2):
                                do(v.reduce_max(mx[0:nq, x:x + 1], S[0:nq, x, 0:N], AX.X))
                        v.tensor_scalar(nm[0:nq, :], mx[0:nq, :], -0.125, None, ALU.mult).then_inc(sem["nm"], 1)
                        dve.wait_ge(sem["exp"], 10 * s + 2 * n + 2)
                        do(v.reciprocal(rd[0:nq, :], den[0:nq, :]))
                        wait(dve, sem["t"], 5 * s + n)
                        if diff:
                            do(v.tensor_scalar(rd[0:nq, 1:2], rd[0:nq, 1:2], k.neglam[0:nq, :], None, ALU.mult))
                            do(v.tensor_scalar(pn[0:nq, 0, 0:N], p[0:nq, 1, 0:N], rd[0:nq, 1:2], None, ALU.mult))
                            v.scalar_tensor_tensor(pn[0:nq, 0, 0:N], p[0:nq, 0, 0:N], rd[0:nq, 0:1], pn[0:nq, 0, 0:N],
                                                   ALU.mult, ALU.add).then_inc(sem["pn"], 1)
                        else:
                            do(v.tensor_scalar(pn[0:nq, 0, 0:N], p[0:nq, 0, 0:N], rd[0:nq, 0:1], None, ALU.mult))
                            v.tensor_scalar(pn[0:nq, 1, 0:N], p[0:nq, 1, 0:N], rd[0:nq, 1:2], None, ALU.mult).then_inc(sem["pn"], 1)
                    if diff:
                        dve.wait_ge(sem["rstd"], 2 * s + 2)
                        v.scalar_tensor_tensor(k.wide[:, bass.ds(s, 1), :].rearrange("p a t -> p (a t)"), osb, k.sub8[:], rstd,
                                               ALU.mult, ALU.mult).then_inc(sem["out"], 1)
                    steps.end()
                if pre:
                    pre.dve(dve)
                step(0)
                with dve.Fori(1, NI) as s:
                    step(s)


def index(k, st, nxt, pre, mb):
    nc, ps, a = k.nc, k.ps, k.a
    v = nc.vector
    NH = 8
    with ExitStack() as ctx:
        def sb(n, s, d=F32):
            return k.sb("idx_" + n, s, d, ctx)
        raw, rop, t1, t2 = k.wide[:, 0:5, :], k.wide[:, 5:10, :], k.wide[:, 10, :], k.wide[:, 11, :]
        wwi, wi = sb("wwi", [P, KT, NH]), sb("wi", [P, 5, NH])
        kn, lnv, rstd = (k.wide[:, j, :] for j in (12, 13, 14))
        rel, sc, m8 = k.wide[:, 15:17, :], k.wide[:, 17, :], sb("m8", [P, 8])
        s_wi, s_done, s_free, s_wip, s_sq, s_ss, s_r, s_kn, s_rot, s_rope, s_s, s_rel, s_acc, s_ones = (k.sem("idx_" + x) for x in (
            "wi_loaded", "lin_done", "lin_free", "wi_product", "squares", "summed", "rstd", "kn", "rot", "rope", "scores", "relu", "acc", "m"))
        steps = Steps(k.sem("idx_steps"))
        order = [4, 0, 1, 2, 3]
        with nc.Block() as block:
            @block.sync
            def _(sp):
                sp.dma_start(wwi[:], cols(a["dsa_w_in_2"][0], 0, KT, 3648, NH)).then_inc(s_wi, 16)
                k.stream(sp, st, nxt)

            @block.gpsimd
            def _(pool):
                for u in range(st.units):
                    k.low(pool, st, (0, u))

            @block.tensor
            def _(pe):
                pre.pe(pe)
                for j, u in enumerate(order):
                    k.split_ready(pe, st, 0, j)
                    for b in range(2):
                        wait(pe, s_free, 2 * j + b - 1)
                        k.product(st, j, ps[:, b, 0:HALF], k.hx(b * HALF, HALF), before=(lambda f: pre.ready(pe, f)) if j == b == 0 else None).then_inc(s_done, 1)
                pe.wait_ge(s_wi, 16)
                for t, (c, n) in enumerate(TILES):
                    for f in range(2 * KT):
                        m = nc.tensor.matmul(ps[0:n, 6, t * NH:(t + 1) * NH], k.h_parts[:, f, c:c + n].bitcast(F32), wwi[:, f % KT, :], start=f == 0, stop=f == 2 * KT - 1)
                m.then_inc(s_wip, 1)
                pe.wait_ge(s_sq, 1)
                for b in range(2):
                    m = nc.tensor.matmul(ps[:, 4 + b, 0:HALF], k.ones, kn[:, b * HALF:(b + 1) * HALF], start=True, stop=True)
                m.then_inc(s_ss, 1)
                for j, u in enumerate([0, 1, 2, 3, 4]):
                    if u == 4:
                        pe.wait_ge(s_kn, 1)
                    else:
                        pe.wait_ge(s_free, 2 * order.index(u) + 2)
                    wait(pe, s_rope, j)
                    for b in range(2):
                        m = nc.tensor.matmul(ps[:, 2 + b, 0:HALF], k.rot2, raw[:, u, b * HALF:(b + 1) * HALF], start=True, stop=True)
                    m.then_inc(s_rot, 1)
                pe.wait_ge(s_rope, 5)
                for n in range(5):
                    c, nq = TILES[n]
                    N = c + nq
                    for x in range(NH):
                        q = NH * n + x
                        h = slice(64 * (x % 2), 64 * (x % 2) + 64)
                        wait(pe, s_rel, q - 1)
                        for lo, hi in ((0, min(N, 512)), (512, N)):
                            if lo < hi:
                                m = nc.tensor.matmul(ps[0:nq, 2 * (q % 2) + lo // 512, 0:hi - lo], rop[h, x // 2, c:N], rop[h, 4, lo:hi], start=True, stop=True)
                        m.then_inc(s_s, 1)

            @block.scalar
            def _(act):
                k.high_first(act, st)
                pre.act(act)
                for j, u in enumerate(order):
                    for b in range(2):
                        act.wait_ge(s_done, 2 * j + b + 1)
                        nc.scalar.activation(raw[:, u, b * HALF:(b + 1) * HALF], ps[:, b, 0:HALF], ACT.Copy).then_inc(s_free, 1)
                    if j + st.depth < st.units:
                        k.high(act, st, (0, j + st.depth))
                nc.scalar.activation(kn, raw[:, 4, :], ACT.Square).then_inc(s_sq, 1)
                act.wait_ge(s_ss, 1)
                nc.scalar.activation(both(lnv), ps[:, 4:6, 0:HALF], ACT.Ln, scale=1.0 / P, bias=k.eps[:]).then_inc(s_r, 1)
                act.wait_ge(s_r, 1)
                nc.scalar.activation(rstd, lnv, ACT.Exp, scale=-0.5).then_inc(s_r, 1)
                for n in range(5):
                    c, nq = TILES[n]
                    N = c + nq
                    for x in range(NH):
                        q = NH * n + x
                        act.wait_ge(s_s, q + 1)
                        wait(act, s_acc, q - 1)
                        flat = ps[0:nq, 2 * (q % 2):2 * (q % 2) + 2, :].rearrange("p b j -> p (b j)")
                        nc.scalar.activation(rel[0:nq, q % 2, 0:N], flat[:, 0:N], ACT.Relu, scale=0.125).then_inc(s_rel, 1)

            @block.vector
            def _(dve):
                def do(ins):
                    steps.mark(ins)
                    steps.settle(dve)
                pre.dve(dve)
                dve.wait_ge(s_wip, 1)
                for t, (c, n) in enumerate(TILES):
                    do(v.tensor_scalar(wi[0:n, t, :], ps[0:n, 6, t * NH:(t + 1) * NH], float(NH ** -0.5), None, ALU.mult))
                for j, u in enumerate([0, 1, 2, 3, 4]):
                    if u == 4:
                        dve.wait_ge(s_r, 2)
                        v.scalar_tensor_tensor(raw[:, 4, :], raw[:, 4, :], k.col(V_IDX), rstd, ALU.mult, ALU.mult).then_inc(s_kn, 1)
                        dve.wait_ge(s_kn, 1)
                    else:
                        dve.wait_ge(s_free, 2 * order.index(u) + 2)
                    do(v.tensor_tensor(t1, raw[:, u, :], k.cos2, ALU.mult))
                    dve.wait_ge(s_rot, j + 1)
                    do(v.tensor_tensor(both(t2), ps[:, 2:4, 0:HALF], both(k.sin2), ALU.mult))
                    v.tensor_tensor(rop[:, u, :], t1, t2, ALU.add).then_inc(s_rope, 1)
                    dve.wait_ge(s_rope, j + 1)
                for n in range(5):
                    c, nq = TILES[n]
                    N = c + nq
                    for x in range(NH):
                        q = NH * n + x
                        dve.wait_ge(s_rel, q + 1)
                        w = wi[0:nq, n, x:x + 1]
                        if x == 0:
                            v.tensor_scalar(sc[0:nq, 0:N], rel[0:nq, q % 2, 0:N], w, None, ALU.mult).then_inc(s_acc, 1)
                        else:
                            v.scalar_tensor_tensor(sc[0:nq, 0:N], rel[0:nq, q % 2, 0:N], w, sc[0:nq, 0:N], ALU.mult, ALU.add).then_inc(s_acc, 1)
                        dve.wait_ge(s_acc, q + 1)
                    if n == 0:
                        do(v.tensor_copy(mb[:, 0, 0:P], k.maskb[:, P:2 * P]))
                        continue
                    do(v.memset(sc[0:nq, 0:META], 1e30))
                    do(v.scalar_tensor_tensor(sc[0:nq, c:N], k.maskf[0:nq, P:P + nq], 1e8, sc[0:nq, c:N], ALU.mult, ALU.add))
                    for _ in range(TOPK // 8):
                        do(v.max(m8[0:nq, :], sc[0:nq, 0:N]))
                        do(v.match_replace(sc[0:nq, 0:N], m8[0:nq, :], sc[0:nq, 0:N], -3e38))
                    do(v.tensor_scalar(mb[0:nq, n, 0:N], sc[0:nq, 0:N], -2e38, NEG, ALU.is_gt, ALU.mult))
                steps.end()


def ffn_up(k, name, l, st, nxt, pre):
    nc, ps = k.nc, k.ps
    v = nc.vector
    w0, w2 = (2 + 2 * l) * P, (3 + 2 * l) * P
    with ExitStack() as ctx:
        u = k.sb(name + "_u", [P, 4, 2 + T2], F32, ctx)
        cc = k.sb(name + "_c", [P, 4, T2], F32, ctx)
        s_done, s_free, s_conv, s_silu, s_out = (k.sem(f"{name}_{x}") for x in ("done", "free", "conv", "silu", "out"))
        steps = Steps(k.sem(name + "_steps"))
        with nc.Block() as block:
            @block.sync
            def _(sp):
                k.stream(sp, st, nxt)

            @block.gpsimd
            def _(pool):
                k.low_all(pool, st)

            @block.tensor
            def _(pe):
                def step(i):
                    for x in range(4):
                        k.split_ready(pe, st, i, x)
                        for b in range(2):
                            wait(pe, s_free, 8 * i + 2 * x + b - 1)
                            first = isinstance(i, int) and x == b == 0
                            k.product(st, x, ps[:, b, 0:HALF], k.hx(b * HALF, HALF), before=(lambda f: pre.ready(pe, f)) if first else None).then_inc(s_done, 1)
                pre.pe(pe)
                step(0)
                with pe.Fori(1, st.iterations) as i:
                    step(i)

            @block.scalar
            def _(act):
                def step(i):
                    for y in range(2):
                        for x in (2 * y, 2 * y + 1):
                            for b in range(2):
                                act.wait_ge(s_done, 8 * i + 2 * x + b + 1)
                                wait(act, s_conv, 4 * i - 3 + x if not isinstance(i, int) or i else 0)
                                nc.scalar.activation(u[:, x, 2 + b * HALF:2 + (b + 1) * HALF], ps[:, b, 0:HALF], ACT.Copy).then_inc(s_free, 1)
                            k.high(act, st, st.after(i, x, st.depth))
                        act.wait_ge(s_conv, 4 * i + 2 * y + 1)
                        nc.scalar.activation(cc[:, 2 * y, :], cc[:, 2 * y, :], ACT.Silu).then_inc(s_silu, 1)
                k.high_first(act, st)
                pre.act(act)
                step(0)
                with act.Fori(1, st.iterations - 1) as i:
                    step(i)
                step(st.iterations - 1)

            @block.vector
            def _(dve):
                def do(ins):
                    steps.mark(ins)
                    steps.settle(dve)

                def step(i):
                    steps.begin(i)
                    for y in range(2):
                        for x in (2 * y, 2 * y + 1):
                            tile = 2 * i + y + FT * (x % 2)
                            dve.wait_ge(s_free, 8 * i + 2 * x + 2)
                            acc = cc[:, x, :]
                            do(v.tensor_scalar(acc, u[:, x, 0:T2], k.col(w0 + tile), k.col(w2 + 2 * FT + tile), ALU.mult, ALU.add))
                            do(v.scalar_tensor_tensor(acc, u[:, x, 1:1 + T2], k.col(w0 + 2 * FT + tile), acc, ALU.mult, ALU.add))
                            v.scalar_tensor_tensor(acc, u[:, x, 2:2 + T2], k.col(w2 + tile), acc, ALU.mult, ALU.add).then_inc(s_conv, 1)
                            dve.wait_ge(s_conv, 4 * i + x + 1)
                        dve.wait_ge(s_silu, 2 * i + y + 1)
                        v.tensor_tensor(k.wide[:, bass.ds(2 * i + y, 1), :].rearrange("p a t -> p (a t)"), cc[:, 2 * y, :], cc[:, 2 * y + 1, :],
                                        ALU.mult).then_inc(s_out, 1)
                        dve.wait_ge(s_out, 2 * i + y + 1)
                    steps.end()
                first = k.sem(name + "_zero")
                v.memset(u[:, :, 0:2], 0.0).then_inc(first, 1)
                dve.wait_ge(first, 1)
                pre.dve(dve)
                step(0)
                with dve.Fori(1, st.iterations) as i:
                    step(i)


def finish(k, pre):
    nc, ps = k.nc, k.ps
    with ExitStack() as ctx:
        o = k.sb("out_tok", [P, 4, DM], F32, ctx)
        s_t, s_c, s_out = k.sem("fin_transposed"), k.sem("fin_copied"), k.sem("out_stored")
        with nc.Block() as block:
            @block.tensor
            def _(pe):
                pre.pe(pe)
                for t in range(4):
                    for g in range(2):
                        for f in range(4):
                            if t == 0:
                                pre.ready(pe, 4 * g + f)
                            m = nc.tensor.transpose(ps[:, 2 * t + g, f * P:(f + 1) * P],
                                                    k.h[:, KT + 4 * g + f, META + t * P:META + (t + 1) * P], k.ident)
                    m.then_inc(s_t, 1)

            @block.scalar
            def _(act):
                pre.act(act)
                for t in range(4):
                    act.wait_ge(s_t, t + 1)
                    nc.scalar.activation(o[:, t, :].rearrange("p (b n) -> p b n", b=2), ps[:, 2 * t:2 * t + 2, :], ACT.Copy).then_inc(s_c, 1)

            @block.vector
            def _(dve):
                pre.dve(dve)

            @block.sync
            def _(sp):
                for t in range(4):
                    sp.wait_ge(s_c, t + 1)
                    sp.dma_start(k.out[0, t * P:(t + 1) * P, :], o[:, t, :]).then_inc(s_out, 16)
                sp.wait_ge(s_out, 64)


def build(nc, a, out, probe=None, dump=None):
    with ExitStack() as ctx:
        k = Core(nc, a, out, ctx)
        v = nc.vector
        w_in, w_att, w_da, w_dsa = a["ssm_w_in"][0], a["att_w_in"][0], a["da_w_qkv_2"][0], a["dsa_w_in_2"][0]

        def one(w, kt, col, row=lambda i, u: 0):
            return lambda i, u: [(0, P, w, row(i, u), col(i, u))]

        def twice(w, c):
            return [(0, 64, w, 0, c), (64, 64, w, 0, c)]

        def split(w, kt, n=1):
            return Stream(2 * n, 4, kt, lambda i, u: [(0, P, w, (u % n) * kt * P, i * (4 // n * P) + (u // n) * P)])

        def ssm_col(g, u):
            return (2048 + 256 * g, 2176 + 256 * g, 4096 + P * g, 5120 + P * g, 256 * g, 128 + 256 * g)[u]

        def swa_unit(j, u):
            two = (u == 0, u == 1)
            if two[0] or two[1]:
                return twice(w_att, 1024 + 256 * u + 64 * j)
            c = (256 * j, 128 + 256 * j, 1536 + 256 * j, 1664 + 256 * j)[u - 2]
            return [(0, 64, w_att, 0, c), (64, 64, w_att, 0, c + 64)]

        def idx_unit(i, u):
            if u == 0:
                return twice(w_dsa, 3584)
            return [(0, 64, w_dsa, 0, 3072 + P * (u - 1)), (64, 64, w_dsa, 0, 3136 + P * (u - 1))]

        def up(l):
            w = a["ffn_w_up_2"][l]
            return Stream(FT // 2, 4, KT, one(w, KT, lambda i, u: i * (2 * P) + (u // 2) * P + (u % 2) * FF))
        S = {
            "ssm": Stream(GROUPS, 6, KT, one(w_in, KT, ssm_col)),
            "ssm_out": split(a["ssm_w_out"][0], KT, 2),
            "swa": Stream(KV, 6, KT, swa_unit, dmas=2),
            "swa_out": split(a["att_w_out"][0], KT),
            "da": Stream(8, 3, KT, one(w_da, KT, lambda i, u: i * P + u * DM)),
            "da_out": split(a["da_w_o_2"][0], KT),
            "up0": up(0), "down0": split(a["ffn_w_down_2"][0], FK, 2),
            "idx": Stream(1, 5, KT, idx_unit, dmas=2),
            "dsa": Stream(8, 3, KT, one(w_dsa, KT, lambda i, u: i * P + u * DM)),
            "dsa_out": split(a["dsa_w_o_2"][0], KT),
            "up1": up(1), "down1": split(a["ffn_w_down_2"][1], FK, 2),
        }
        names = list(S)
        for n in names:
            k.start_stream(S[n])
        following = {n: (S[names[j + 1]] if j + 1 < len(names) else None) for j, n in enumerate(names)}
        if probe:
            order = ["ssm", "swa", "da", "ffn0", "dsa", "ffn1"]
            ends = {"ssm": "ssm_out", "swa": "swa_out", "da": "da_out", "ffn0": "down0", "dsa": "dsa_out", "ffn1": "down1"}
            following[ends[probe]] = None

        def done(x):
            if probe != x:
                return False
            s = k.sem("dumped")
            with nc.Block() as block:
                @block.sync
                def _(sp):
                    sp.dma_start(dump, k.res[:]).then_inc(s, 16)
                    sp.wait_ge(s, 16)
            return True

        def h1(f):
            return k.h[:, KT + f, 0:SEQ]

        def y1(f):
            return k.h[:, f, 0:SEQ]

        def r1(f):
            return k.res[:, f, META:T2]

        def wide1(f):
            return k.wide[:, f, 0:SEQ]

        def h2(f):
            return k.h[:, KT + f, :]

        def r2(f):
            return k.res[:, f, :]

        def wide2(f):
            return k.wide[:, f, :]

        def to_y(t, c, n, src):
            return v.tensor_copy(k.h[:, bass.ds(t, 1), c:c + n].rearrange("p a t -> p (a t)"), src)

        def y_tile(t):
            return k.h[:, bass.ds(t, 1), 0:SEQ].rearrange("p a t -> p (a t)")

        def res_tile(t):
            return k.res[:, bass.ds(t, 1), :].rearrange("p a t -> p (a t)")

        def to_res(t, c, n, src):
            dst = k.res[:, bass.ds(t, 1), c:c + n].rearrange("p a t -> p (a t)")
            return v.tensor_tensor(dst, src, dst, ALU.add)

        setup(k, S["ssm"])
        parts1 = lambda f: k.h_parts[:, f, 0:SEQ], lambda f: k.h_parts[:, KT + f, 0:SEQ]
        parts2 = lambda f: k.h_parts[:, f, :], lambda f: k.h_parts[:, KT + f, :]
        wide_low1, wide_low2 = lambda f: k.wide_parts[:, f, 0:SEQ], lambda f: k.wide_parts[:, f, :]

        ssm(k, S["ssm"], following["ssm"], Norm(k, r1, KT, SEQ, V_PRE, h1, parts=parts1))
        with ExitStack() as own:
            gated = k.sb("gated_high", [P, 2 * KT, SEQ], F32R, own)
            project(k, "ssm_out", S["ssm_out"], following["ssm_out"], 2, None, None, SEQ, to_y, y_tile,
                    Norm(k, wide1, 2 * KT, SEQ, V_GATE, wide1, parts=(lambda f: gated[:, f, :], wide_low1)))
        buffers = k.wide[:, 20:22, 0:SEQ], k.wide[:, 16:20, 0:SEQ]
        swa(k, S["swa"], following["swa"], Norm(k, r1, KT, SEQ, V_PRE + 8, h1, post=(y1, V_POST, r1, *buffers), parts=parts1))
        project(k, "swa_out", S["swa_out"], following["swa_out"], 1, wide1, (parts1[1], wide_low1), SEQ, to_y, y_tile)
        buffers = k.wide[:, 4:6, 0:SEQ], k.wide[:, 0:4, :]
        pairs(k, "da", S["da"], following["da"], True,
              Norm(k, r2, KT, T2, V_DA, h2, post=(y1, V_POST + 8, r1, *buffers), parts=parts2))
        project(k, "da_out", S["da_out"], following["da_out"], 1, wide2, (parts2[0], wide_low2), T2, to_res, res_tile)
        if done("da"):
            return

        def ffn(l):
            up, down = f"up{l}", f"down{l}"
            ffn_up(k, up, l, S[up], following[up], Norm(k, r2, KT, T2, V_FFN + 8 * l, h2, parts=parts2))
            with ExitStack() as own:
                more = k.sb(f"hidden_high{l}", [P, FT - 2 * KT, T2], F32R, own)
                project(k, down, S[down], following[down], 2, wide2,
                        (lambda f: k.h_parts[:, f, :] if f < 2 * KT else more[:, f - 2 * KT, :], wide_low2), T2, to_res, res_tile)
        ffn(0)
        if done("ffn0"):
            return
        with ExitStack() as own:
            mb = k.sb("mb", [P, 5, T2], BF16, own)
            index(k, S["idx"], following["idx"], Norm(k, r2, KT, T2, V_DSA, h2, parts=parts2), mb)
            pairs(k, "dsa", S["dsa"], following["dsa"], False, mb=mb)
        project(k, "dsa_out", S["dsa_out"], following["dsa_out"], 1, wide2, (parts2[0], wide_low2), T2, to_res, res_tile)
        if done("dsa"):
            return
        ffn(1)
        if done("ffn1"):
            return
        finish(k, Norm(k, r2, KT, T2, V_FIN, h2))


def kernel(**inputs):
    import concourse.bacc as bacc
    from concourse.bass_utils import run_bass_kernel_spmd

    nc = bacc.Bacc("TRN2", target_bir_lowering=False, num_devices=1)
    arrays, aps = {}, {}
    for name, x in inputs.items():
        x = np.ascontiguousarray(x)
        arrays["in_" + name] = x
        aps[name] = nc.dram_tensor("in_" + name, x.shape, mybir.dt.from_np(x.dtype), kind="ExternalInput").ap()
    out = nc.dram_tensor("out", (1, SEQ, DM), F32, kind="ExternalOutput").ap()
    build(nc, aps, out)
    r = run_bass_kernel_spmd(nc, [arrays], core_ids=[0])
    return r.results[0]["out"]
```

```python
import concourse.bass as bass
from concourse import mybir
from contextlib import ExitStack
import numpy as np

F32 = mybir.dt.float32
F32R = mybir.dt.float32r
BF16 = mybir.dt.bfloat16
I32 = mybir.dt.int32
ACT = mybir.ActivationFunctionType
ALU = mybir.AluOpType
AX = mybir.AxisListType

P = 128
DM = 1024
KT = DM // P
SEQ = 512
META = 16
T2 = SEQ + META
HALF = T2 // 2
NEG = -1e30
EPS = 1e-6
DI = 2048
GROUPS = 8
CHUNKS = SEQ // P
SSM_HEADS = 32
RPG = SSM_HEADS // GROUPS
KV = 4
FF = 2816
FT = FF // P
FK = FT // 2
TOPK = 128
TILES = [(a, min(P, T2 - a)) for a in range(0, T2, P)]
LAMBDA_INIT = 0.2

V_PRE, V_POST, V_GATE, V_CB = 0, 16, 32, 48
V_DA, V_DSA, V_FFN, V_FIN, V_SUB, V_IDX = 80, 88, 96, 112, 120, 121
V_CW = P
V_ROWS = [122, 128, 88, 88, 88, 88]


def constants():
    eye = np.eye(P, dtype=np.float32)
    ones = np.ones((P, P), np.float32)
    tri = np.triu(ones)
    rot1, rot2 = np.zeros((P, P), np.float32), np.zeros((P, P), np.float32)
    for m in range(P):
        b, d = m - m % 64, m % 64
        if d < 8:
            rot1[b + d + 8, m] = -1
        elif d < 16:
            rot1[b + d - 8, m] = 1
        if d < 32:
            rot2[b + d + 32, m] = -1
        else:
            rot2[b + d - 32, m] = 1
    causal = np.where(tri.T > 0, 0, NEG).astype(np.float32)
    before = np.where(np.arange(P)[None] > np.arange(P)[:, None], 0, NEG).astype(np.float32)
    d = np.arange(P) % 64
    inv1 = np.float32(500000.0) ** (-(2 * (d % 8)).astype(np.float32) / np.float32(16))
    inv1 = np.where(d < 16, inv1, 0).astype(np.float32)[:, None]
    inv2 = (np.float32(10000.0) ** (-(2 * (d % 32)).astype(np.float32) / np.float32(64))).astype(np.float32)
    ang = (np.arange(T2, dtype=np.float32)[None] * inv2[:, None]).astype(np.float32)
    cos2, sin2 = np.cos(ang).astype(np.float32), np.sin(ang).astype(np.float32)
    return np.concatenate([eye, ones, tri, rot1, rot2, before, causal, cos2, sin2, inv1], axis=1)


def wait(eng, sem, value):
    if not isinstance(value, int) or value > 0:
        eng.wait_ge(sem, value)


class Steps:

    def __init__(self, sem):
        self.sem, self.per, self.base, self.k = sem, 0, 0, 0

    def begin(self, i):
        self.base, self.k = i * self.per, 0

    def mark(self, ins):
        ins.then_inc(self.sem, 1)
        self.k += 1

    def settle(self, eng):
        eng.wait_ge(self.sem, self.base + self.k)

    def end(self):
        self.per = self.per or self.k
        assert self.per == self.k


class Stream:

    def __init__(self, iterations, units, kt, source, dmas=1):
        self.iterations, self.units, self.kt, self.source, self.dmas = iterations, units, kt, source, dmas
        self.depth = 2 if units % 2 == 0 else 3
        assert iterations == 1 or units % self.depth == 0

    def after(self, i, u, d):
        u += d
        if u >= self.units:
            i, u = i + 1, u - self.units
        return None if isinstance(i, int) and i >= self.iterations else (i, u)


class Core:
    def __init__(self, nc, a, out, ctx):
        self.nc, self.a, self.out, self.ctx = nc, a, out, ctx
        sb = self.sb
        self.SLOTS = 6
        self.ring = sb("ring", [P, self.SLOTS * KT * P])
        self.parts = sb("parts", [P, self.SLOTS * KT * P], F32R)
        self.res = sb("res", [P, KT, T2])
        self.h, self.h_parts = self.two_names("h", [P, 2 * KT, T2])
        self.wide, self.wide_parts = self.two_names("wide", [P, FT, T2])
        self.cst = sb("cst", [P, 7 * P + 2 * T2 + 1])
        c = self.cst
        self.ident, self.ones, self.tri = c[:, 0:P], c[:, P:2 * P], c[:, 2 * P:3 * P]
        self.rot1, self.rot2 = c[:, 3 * P:4 * P], c[:, 4 * P:5 * P]
        self.maskf = c[:, 5 * P:7 * P]
        self.cos2, self.sin2 = c[:, 7 * P:7 * P + T2], c[:, 7 * P + T2:7 * P + 2 * T2]
        self.inv1 = c[:, 7 * P + 2 * T2:7 * P + 2 * T2 + 1]
        self.identb = sb("identb", [P, P], BF16)
        self.maskb = sb("maskb", [P, 2 * P], BF16)
        self.cos1, self.sin1 = sb("cos1", [P, SEQ]), sb("sin1", [P, SEQ])
        self.vec = sb("vec", [P, 6 * P])
        self.eps, self.warm = sb("eps", [P, 1]), sb("warm", [P, 1])
        self.sub8 = sb("sub8", [P, 1])
        self.neglam = sb("neglam", [P, 1])
        self.drow = sb("drow", [P, 4, SSM_HEADS])
        self.dexp = sb("dexp", [P, 16])
        self.nsink = sb("nsink", [P, 16])
        self.wdt = sb("wdt", [P, KT, SSM_HEADS])
        self.ps = ctx.enter_context(nc.psum_tensor("ps", [P, 8, 512], F32))
        self.loaded = [self.sem(f"weights_loaded{s}") for s in range(self.SLOTS)]
        self.granted = self.sem("refills_granted")
        self.w_high, self.w_low = self.sem("weights_high"), self.sem("weights_low")
        self.split = 0
        self.loads = [0] * self.SLOTS
        self.acc, self.sq, self.rstd = sb("norm_acc", [P, T2]), sb("norm_sq", [P, T2]), sb("norm_rstd", [P, T2])
        names = ("high", "low", "squared", "accumulated", "summed", "rstd_steps", "post_steps", "normalised")
        self.nsem = {x: self.sem("norm_" + x) for x in names}
        self.ncount = {x: 0 for x in names}

    def two_names(self, name, shape):
        with self.nc.sbuf_tensor(name, shape, F32) as plain:
            pass
        return plain, self.sb(name + "_parts", shape, F32R)

    def sb(self, name, shape, dt=F32, ctx=None):
        return (ctx or self.ctx).enter_context(self.nc.sbuf_tensor(name, shape, dt))

    def sem(self, name):
        return self.ctx.enter_context(self.nc.semaphore(name))

    def col(self, c):
        return self.vec[:, c:c + 1] if isinstance(c, int) else self.vec[:, bass.ds(c, 1)]

    def slot(self, u, kt):
        return self.ring[:, u * kt * P:(u + 1) * kt * P]

    def part(self, st, u, low):
        at = (2 * (u % st.depth) + low) * st.kt * P
        return self.parts[:, at:at + st.kt * P]

    def load(self, sp, st, i, u, refill=False):
        if refill:
            sp.wait_ge(self.w_low, st.first + st.units * (i - 1) + u + 1)
            sp.sem_inc(self.granted, 1)
        slot = self.slot(u, st.kt).rearrange("p (k n) -> p k n", k=st.kt)
        for c0, n, w, r0, c in st.source(i, u):
            sp.dma_start(slot[:, :, c0:c0 + n], cols(w, r0, st.kt, c, n)).then_inc(self.loaded[u], 16)

    def start_stream(self, st):
        st.base = list(self.loads)
        st.first = self.split
        self.split += st.units * st.iterations
        for u in range(st.units):
            self.loads[u] += 16 * st.dmas * st.iterations

    def stream(self, sp, st, nxt):
        if st.iterations > 1:
            with sp.Fori(1, st.iterations) as i:
                for u in range(st.units):
                    self.load(sp, st, i, u, refill=True)
        if nxt is not None:
            sp.wait_ge(self.w_low, st.first + st.units * st.iterations)
            for u in range(nxt.units):
                self.load(sp, nxt, 0, u)

    def high(self, act, st, at):
        if at is None:
            return
        i, u = at
        act.wait_ge(self.loaded[u], st.base[u] + 16 * st.dmas * (i + 1))
        self.nc.scalar.activation(self.part(st, u, 0), self.slot(u, st.kt), ACT.Copy).then_inc(self.w_high, 1)

    def low(self, pool, st, at):
        if at is None:
            return
        i, u = at
        pool.wait_ge(self.w_high, st.first + st.units * i + u + 1)
        self.nc.gpsimd.tensor_tensor(self.part(st, u, 1), self.slot(u, st.kt), self.part(st, u, 0).bitcast(F32), ALU.subtract).then_inc(self.w_low, 1)

    def split_ready(self, pe, st, i, u):
        pe.wait_ge(self.w_low, st.first + st.units * i + u + 1)

    def high_first(self, act, st):
        for u in range(st.depth):
            self.high(act, st, (0, u))

    def low_all(self, pool, st):
        with pool.Fori(0, st.iterations) as i:
            for u in range(st.units):
                self.low(pool, st, (i, u))

    def product(self, st, u, out, x, start=True, stop=True, before=None, tiles=None):
        hi, lo = self.part(st, u, 0), self.part(st, u, 1)
        for f in tiles or range(st.kt):
            if before is not None:
                before(f)
            xh, xl = x(f)
            n = slice(f * P, (f + 1) * P)
            for j, (w, b) in enumerate(((hi, xh), (hi, xl), (lo, xh))):
                m = self.nc.tensor.matmul(out, w[:, n], b, start=start and f == j == 0, stop=stop and f == st.kt - 1 and j == 2)
        return m

    def hx(self, c, n):
        return lambda f: (self.h_parts[:, f, c:c + n], self.h_parts[:, KT + f, c:c + n])


class Spread:

    def __init__(self, k, kt, x, high, low):
        self.k, self.kt, self.x, self.high, self.low = k, kt, x, high, low
        self.base = dict(k.ncount)
        k.ncount["high"] += kt
        k.ncount["low"] += kt

    def act(self, act, f):
        k = self.k
        k.nc.scalar.activation(self.high(f), self.x(f), ACT.Copy).then_inc(k.nsem["high"], 1)

    def dve(self, dve, f):
        k = self.k
        dve.wait_ge(k.nsem["high"], self.base["high"] + f + 1)
        k.nc.vector.tensor_tensor(self.low(f), self.x(f), self.high(f).bitcast(F32), ALU.subtract).then_inc(k.nsem["low"], 1)

    def ready(self, pe, f):
        pe.wait_ge(self.k.nsem["low"], self.base["low"] + f + 1)

    def parts(self, c, n):
        return lambda f: (self.high(f)[:, c:c + n], self.low(f)[:, c:c + n])


def cols(w, r0, kt, c, n=P):
    return w[r0:r0 + kt * P, bass.ds(c, n)].rearrange("(k p) n -> p k n", p=P)


def both(ap):
    return ap.rearrange("p (a n) -> p a n", a=2)


def halves(T):
    return [(0, SEQ)] if T == SEQ else [(0, HALF), (HALF, HALF)]


def setup(k, first, tables):
    nc, a, ps = k.nc, k.a, k.ps
    with ExitStack() as ctx:
        def sb(n, s, d=F32):
            return k.sb(n, s, d, ctx)
        xin, meta = sb("xin", [P, 4, DM]), sb("metain", [META, DM])
        stage = sb("stage", [P, 6, P])
        s_cst, s_x, s_row = k.sem("const_loaded"), (k.sem("x_first_half_loaded"), k.sem("x_and_meta_loaded")), k.sem("rows_loaded")
        s_ident = k.sem("identity_loaded")
        s_xt, s_xfree = k.sem("x_transposed"), k.sem("x_stored")
        s_vt, s_small = k.sem("vec_transposed"), tables.s_small
        ns = k.nsem
        k.ncount["squared"] += KT
        k.ncount["accumulated"] += KT + 1
        const = nc.inline_tensor(constants(), name="shape_constants").ap()
        rows = []

        def put(tile, r, src, n, w=P, c=0):
            rows.append((stage[r:r + n, tile, c:c + w], src))
        for l in range(2):
            put(0, V_PRE + 8 * l, a["pre_norm"][l].rearrange("(r c) -> r c", c=P), 8)
            put(0, V_POST + 8 * l, a["post_norm"][l].rearrange("(r c) -> r c", c=P), 8)
            put(0, V_FFN + 8 * l, a["ffn_norm_2"][l].rearrange("(r c) -> r c", c=P), 8)
            w = a["ffn_conv_w_2"][l].rearrange("j (r c) -> (j r) c", c=P)
            put(2 + 2 * l, 0, w[0:4 * FT], 4 * FT)
            put(3 + 2 * l, 0, w[4 * FT:6 * FT], 2 * FT)
            put(3 + 2 * l, 2 * FT, a["ffn_conv_b_2"][l].rearrange("(r c) -> r c", c=P), 2 * FT)
        put(0, V_GATE, a["ssm_gate_norm"][0].rearrange("(r c) -> r c", c=P), 16)
        put(0, V_CB, a["ssm_conv_b"][0].rearrange("(r c) -> r c", c=P), 32)
        put(0, V_DA, a["da_norm_2"][0].rearrange("(r c) -> r c", c=P), 8)
        put(0, V_DSA, a["dsa_norm_2"][0].rearrange("(r c) -> r c", c=P), 8)
        put(0, V_FIN, a["final_norm_2"].rearrange("(r c) -> r c", c=P), 8)
        put(0, V_SUB, a["da_subln_2"], 1)
        put(0, V_IDX, a["dsa_idx_k_norm_2"], 1, 64)
        put(0, V_IDX, a["dsa_idx_k_norm_2"], 1, 64, 64)
        put(1, 0, a["ssm_conv_w"][0].rearrange("j (r c) -> (j r) c", c=P), 4 * 32)
        small = [(k.drow[:, j, :], a[n].to_broadcast([P, SSM_HEADS]))
                 for j, n in enumerate(["ssm_d", "ssm_dt_bias", "ssm_a_log"])]
        small += [(k.nsink[:], a["att_sinks"].to_broadcast([P, 16]))]
        small += [(tables.lam[:, j, :], a[n].to_broadcast([P, 64]))
                  for j, n in enumerate(["da_lambda_q1_2", "da_lambda_q2_2", "da_lambda_k1_2", "da_lambda_k2_2"])]

        tables.loads = 2 + len(small)
        with nc.Block() as block:
            @block.sync
            def _(sp):
                sp.dma_start(k.cst[:, 0:P], const[:, 0:P]).then_inc(s_ident, 16)
                for j, c in enumerate((0, DM // 2)):
                    sp.dma_start(xin[:, :, c:c + DM // 2], a["x"][0, :, c:c + DM // 2].rearrange("(t p) d -> p t d", p=P)).then_inc(s_x[j], 16)
                sp.dma_start(meta[:], a["meta_tokens_2"]).then_inc(s_x[1], 16)
                for dst, src in rows:
                    sp.dma_start(dst, src).then_inc(s_row, 16)
                sp.dma_start(k.cst[:, P:], const[:, P:]).then_inc(s_cst, 16)
                for u in range(first.units):
                    k.load(sp, first, 0, u)

            @block.gpsimd
            def _(pool):
                pool.dma_start(k.wdt[:], cols(a["ssm_w_in"][0], 0, KT, 6144, SSM_HEADS)).then_inc(s_small, 16)
                for dst, src in small:
                    pool.dma_start(dst, src).then_inc(s_small, 16)
                pool.dma_start(tables.posi, a["positions"].to_broadcast([P, SEQ])).then_inc(s_small, 16)
                pool.wait_ge(s_small, 16 * tables.loads)
                pool.wait_ge(s_cst, 16)

            @block.tensor
            def _(pe):
                pe.wait_ge(s_ident, 16)
                for f in range(KT):
                    pe.wait_ge(s_x[f // 4], 16 * (f // 4 + 1))
                    wait(pe, s_xfree, f - 3)
                    for t in range(4):
                        m = nc.tensor.transpose(ps[:, f % 4, t * P:(t + 1) * P], xin[:, t, f * P:(f + 1) * P], k.ident)
                    m.then_inc(s_xt, 1)
                for f in range(KT):
                    m = nc.tensor.transpose(ps[:, 4, f * META:(f + 1) * META], meta[:, f * P:(f + 1) * P], k.ident[0:META, 0:META])
                m.then_inc(s_xt, 1)
                pe.wait_ge(s_row, 16 * len(rows))
                for t, n in enumerate(V_ROWS):
                    m = nc.tensor.transpose(ps[:, 5 + t // 3, (t % 3) * P:(t % 3) * P + n], stage[0:n, t, :], k.ident[0:n, 0:n])
                m.then_inc(s_vt, 1)
                pe.wait_ge(s_cst, 16)

            @block.scalar
            def _(act):
                for f in range(KT):
                    act.wait_ge(s_xfree, f + 1)
                    act.wait_ge(ns["accumulated"], f + 1)
                    nc.scalar.activation(k.sq[:, 0:SEQ], k.res[:, f, META:T2], ACT.Square).then_inc(ns["squared"], 1)

            @block.vector
            def _(dve):
                steps = Steps(k.sem("setup_steps"))

                def do(ins):
                    steps.mark(ins)
                    steps.settle(dve)
                do(nc.vector.memset(k.eps[:], EPS))
                nc.vector.memset(k.acc[:], 0.0).then_inc(ns["accumulated"], 1)
                for f in range(KT + 1):
                    if f < KT:
                        dve.wait_ge(s_xt, f + 1)
                        nc.vector.tensor_copy(k.res[:, f, META:T2], ps[:, f % 4, :]).then_inc(s_xfree, 1)
                    if f:
                        dve.wait_ge(ns["accumulated"], f)
                        dve.wait_ge(ns["squared"], f)
                        nc.vector.tensor_tensor(k.acc[:, 0:SEQ], k.acc[:, 0:SEQ], k.sq[:, 0:SEQ], ALU.add).then_inc(ns["accumulated"], 1)
                dve.wait_ge(s_xt, KT + 1)
                do(nc.vector.tensor_copy(k.res[:, :, 0:META], ps[:, 4, 0:KT * META].rearrange("p (f t) -> p f t", f=KT)))
                dve.wait_ge(s_vt, 1)
                for t, n in enumerate(V_ROWS):
                    do(nc.vector.tensor_copy(k.vec[:, t * P:t * P + n], ps[:, 5 + t // 3, (t % 3) * P:(t % 3) * P + n]))
                do(nc.vector.tensor_scalar(k.sub8[:], k.col(V_SUB), 1.0 - LAMBDA_INIT, None, ALU.mult))
                dve.wait_ge(s_cst, 16)
                do(nc.vector.tensor_copy(k.identb[:], k.ident))
                do(nc.vector.tensor_copy(k.maskb[:], k.maskf))


class Tables:

    def __init__(self, k):
        self.k = k
        w = k.wide
        self.posi, self.ang, self.turns = w[:, 0, 0:SEQ].bitcast(I32), w[:, 1, 0:SEQ], w[:, 2, 0:SEQ]
        self.lam = w[:, 3, 0:256].rearrange("p (j d) -> p j d", j=4)
        self.lprod, self.lsum = w[:, 4, 0:128].rearrange("p (j d) -> p j d", j=2), w[:, 5, 0:2]
        self.s_small, self.s_v, self.s_a = k.sem("small_loaded"), k.sem("tables_vector"), k.sem("tables_scalar")
        self.steps = Steps(k.sem("table_steps"))

    def act(self, act):
        nc, k = self.k.nc, self.k
        act.wait_ge(self.s_v, 1)
        nc.scalar.activation(k.drow[:, 3, :], k.drow[:, 2, :], ACT.Exp).then_inc(self.s_a, 1)
        nc.scalar.activation(self.lsum, self.lsum, ACT.Exp).then_inc(self.s_a, 1)
        act.wait_ge(self.s_v, 3)
        nc.scalar.activation(k.sin1[:], self.ang, ACT.Sin).then_inc(self.s_a, 1)
        nc.scalar.activation(k.cos1[:], self.turns, ACT.Sin).then_inc(self.s_a, 1)

    def dve(self, dve):
        nc, k, ang, turns = self.k.nc, self.k, self.ang, self.turns
        steps = self.steps

        def do(ins):
            steps.mark(ins)
            steps.settle(dve)
        dve.wait_ge(self.s_small, 16 * self.loads)
        do(nc.vector.tensor_tensor(self.lprod, self.lam[:, 0:2, :], self.lam[:, 2:4, :], ALU.mult))
        nc.vector.reduce_sum(self.lsum, self.lprod, AX.X).then_inc(self.s_v, 1)
        for b in range(2):
            do(nc.vector.tensor_copy(k.dexp[64 * b:64 * b + 64, :],
                                     k.drow[64 * b:64 * b + 64, 0, :].rearrange("p (f b) -> p b f", b=2)[:, b, :]))
        do(nc.vector.tensor_scalar(k.nsink[:], k.nsink[:], -1.0, None, ALU.mult))
        do(nc.vector.tensor_copy(ang, self.posi))
        do(nc.vector.tensor_scalar(ang, ang, k.inv1, None, ALU.mult))
        do(nc.vector.tensor_scalar(turns, ang, float(1 / (2 * np.pi)), 12582912.0, ALU.mult, ALU.add))
        do(nc.vector.tensor_scalar(turns, turns, 12582912.0, None, ALU.subtract))
        c1 = 6.28125
        c2 = float(np.float32(int((2 * np.pi - c1) * 2 ** 21) / 2 ** 21))
        c3 = float(np.float32(2 * np.pi - c1 - c2))
        for c in (c1, c2, c3):
            do(nc.vector.scalar_tensor_tensor(ang, turns, -c, ang, ALU.mult, ALU.add))
        pi = float(np.nextafter(np.float32(np.pi), np.float32(0)))
        nc.vector.tensor_scalar(ang, ang, -pi, pi, ALU.max, ALU.min).then_inc(self.s_v, 1)
        dve.wait_ge(self.s_v, 2)
        do(nc.vector.scalar_tensor_tensor(turns, ang, -1.0, ang, ALU.mult, ALU.max))
        nc.vector.tensor_scalar(turns, turns, -1.0, float(np.pi / 2), ALU.mult, ALU.add).then_inc(self.s_v, 1)
        dve.wait_ge(self.s_a, 2)
        do(nc.vector.tensor_scalar(k.drow[:, 3, :], k.drow[:, 3, :], -1.0, None, ALU.mult))
        do(nc.vector.tensor_tensor(k.neglam[:], self.lsum[:, 1:2], self.lsum[:, 0:1], ALU.subtract))
        do(nc.vector.tensor_scalar(k.neglam[:], k.neglam[:], -LAMBDA_INIT, None, ALU.add))
        dve.wait_ge(self.s_a, 4)


class Norm:

    def __init__(self, k, src, kt, T, gain, dst, post=None, parts=None):
        self.spread = Spread(k, kt, dst, *parts) if parts else None
        self.k, self.src, self.kt, self.T, self.gain, self.dst, self.post = k, src, kt, T, gain, dst, post
        self.base = dict(k.ncount)
        c = k.ncount
        c["summed"] += 1 + (kt if post else 0)
        c["rstd_steps"] += 4 if post else 2
        c["squared"] += kt if post else 0
        c["post_steps"] += 2 * kt if post else 0
        c["normalised"] += kt

    @staticmethod
    def view(x, T):
        return x[:, 0:SEQ] if T == SEQ else both(x)

    def sum_over_partitions(self, T, bank, x, first=True, last=True):
        k = self.k
        for b, (c, w) in enumerate(halves(T)):
            m = k.nc.tensor.matmul(k.ps[:, bank + b, 0:w], k.ones, x[:, c:c + w], start=first, stop=last)
        m.then_inc(k.nsem["summed"], 1)

    def pe(self, pe):
        k, n, at = self.k, self.k.nsem, self.base
        pe.wait_ge(n["accumulated"], at["accumulated"])
        if self.post:
            self.sum_over_partitions(SEQ, 5, k.acc)
            for f in range(self.kt):
                pe.wait_ge(n["squared"], at["squared"] + f + 1)
                self.sum_over_partitions(self.T, 6, self.post[4][:, f % 4, :], f == 0, f == self.kt - 1)
        else:
            self.sum_over_partitions(self.T, 6, k.acc)

    def ready(self, pe, f):
        if self.spread:
            self.spread.ready(pe, f)
            return
        pe.wait_ge(self.k.nsem["normalised"], self.base["normalised"] + f + 1)

    def rms(self, act, j, T, bank, summed):
        nc, k, n, at = self.k.nc, self.k, self.k.nsem, self.base
        act.wait_ge(n["summed"], at["summed"] + summed)
        total = k.ps[:, bank, :] if T == SEQ else k.ps[:, bank:bank + 2, 0:HALF]
        nc.scalar.activation(self.view(k.sq, T), total, ACT.Ln, scale=1.0 / (self.kt * P), bias=k.eps[:]).then_inc(n["rstd_steps"], 1)
        act.wait_ge(n["rstd_steps"], at["rstd_steps"] + 2 * j + 1)
        nc.scalar.activation(k.rstd[:, 0:T], k.sq[:, 0:T], ACT.Exp, scale=-0.5).then_inc(n["rstd_steps"], 1)

    def act(self, act):
        nc, n, at = self.k.nc, self.k.nsem, self.base
        nc.scalar.activation(self.k.warm[:], self.k.eps[:], ACT.Ln)
        if not self.post:
            self.rms(act, 0, self.T, 6, 1)
            self.high(act)
            return
        self.rms(act, 0, SEQ, 5, 1)
        for f in range(self.kt):
            act.wait_ge(n["post_steps"], at["post_steps"] + 2 * f + 2)
            if f >= 4:
                act.wait_ge(n["summed"], at["summed"] + f - 2)
            nc.scalar.activation(self.post[4][:, f % 4, :], self.src(f), ACT.Square).then_inc(n["squared"], 1)
        self.rms(act, 1, self.T, 6, 1 + self.kt)
        self.high(act)

    def high(self, act):
        if self.spread:
            for f in range(self.kt):
                act.wait_ge(self.k.nsem["normalised"], self.base["normalised"] + f + 1)
                self.spread.act(act, f)

    def dve(self, dve):
        nc, k, n, at = self.k.nc, self.k, self.k.nsem, self.base
        dve.wait_ge(n["rstd_steps"], at["rstd_steps"] + 2)
        if self.post:
            y, gain, res, tmp, _ = self.post
            for f in range(self.kt):
                if f >= 2:
                    dve.wait_ge(n["post_steps"], at["post_steps"] + 2 * f - 2)
                nc.vector.scalar_tensor_tensor(tmp[:, f % 2, :], y(f), k.col(gain + f), k.rstd[:, 0:SEQ], ALU.mult, ALU.mult).then_inc(n["post_steps"], 1)
                dve.wait_ge(n["post_steps"], at["post_steps"] + 2 * f + 1)
                nc.vector.tensor_tensor(res(f), res(f), tmp[:, f % 2, :], ALU.add).then_inc(n["post_steps"], 1)
            dve.wait_ge(n["rstd_steps"], at["rstd_steps"] + 4)
        for f in range(self.kt):
            nc.vector.scalar_tensor_tensor(self.dst(f), self.src(f), k.col(self.gain + f), k.rstd[:, 0:self.T],
                                           ALU.mult, ALU.mult).then_inc(n["normalised"], 1)
            if self.spread and f:
                self.spread.dve(dve, f - 1)
        if self.spread:
            self.spread.dve(dve, self.kt - 1)


class StepSizes:

    def __init__(self, k, dts, ctx):
        self.k, self.dts = k, dts
        self.n = CHUNKS * SSM_HEADS
        self.raw, self.e, self.u, self.r, self.big = (
            k.sb("dt_" + x, [P, CHUNKS, SSM_HEADS], F32, ctx) for x in ("raw", "e", "u", "r", "big"))
        self.s_pe, self.s_act = k.sem("dt_products"), k.sem("dt_scalar")
        self.steps = Steps(k.sem("dt_steps"))

    def pe_raw(self, pe):
        nc, k = self.k.nc, self.k
        for c in range(CHUNKS):
            for f in range(2 * KT):
                m = nc.tensor.matmul(k.ps[:, 2, c * SSM_HEADS:(c + 1) * SSM_HEADS], k.h_parts[:, f, c * P:(c + 1) * P].bitcast(F32),
                                     k.wdt[:, f % KT, :], start=f == 0, stop=f == 2 * KT - 1)
        m.then_inc(self.s_pe, 1)

    def pe_sums(self, pe):
        nc, k, n = self.k.nc, self.k, self.n
        pe.wait_ge(self.steps.sem, 13)
        a_all = self.dts[:, 0, :, :].rearrange("p c h -> p (c h)")
        nc.tensor.matmul(k.ps[:, 3, 0:n], k.tri, a_all, start=True, stop=True)
        nc.tensor.matmul(k.ps[:, 4, 0:n], k.ones, a_all, start=True, stop=True).then_inc(self.s_pe, 1)

    def act_softplus(self, act):
        nc = self.k.nc
        act.wait_ge(self.steps.sem, 3)
        nc.scalar.activation(self.e[:], self.e[:], ACT.Exp, scale=-1.0).then_inc(self.s_act, 1)
        act.wait_ge(self.steps.sem, 4)
        nc.scalar.activation(self.big[:], self.u[:], ACT.Ln).then_inc(self.s_act, 1)

    def act_decays(self, act):
        nc, dts = self.k.nc, self.dts
        act.wait_ge(self.steps.sem, 15)
        nc.scalar.activation(dts[:, 3, :, :], self.e[:], ACT.Exp).then_inc(self.s_act, 1)
        nc.scalar.activation(dts[:, 4, :, :], self.k.ps[:, 4, 0:self.n].rearrange("p (c h) -> p c h", c=CHUNKS), ACT.Exp).then_inc(self.s_act, 1)

    def dve(self, dve):
        k, n, dts, steps = self.k, self.n, self.dts, self.steps
        raw, e, u, r, big = self.raw, self.e, self.u, self.r, self.big

        def do(ins):
            steps.mark(ins)
            steps.settle(dve)

        def head(q):
            return k.drow[:, q:q + 1, :].to_broadcast([P, CHUNKS, SSM_HEADS])
        v = k.nc.vector
        dve.wait_ge(self.s_pe, 1)
        do(v.tensor_tensor(raw[:], k.ps[:, 2, 0:n].rearrange("p (c h) -> p c h", c=CHUNKS), head(1), ALU.add))
        do(v.tensor_scalar(r[:], raw[:], -1.0, None, ALU.mult))
        do(v.tensor_tensor(e[:], raw[:], r[:], ALU.max))
        dve.wait_ge(self.s_act, 1)
        do(v.tensor_scalar(u[:], e[:], 1.0, None, ALU.add))
        dve.wait_ge(self.s_act, 2)
        do(v.tensor_scalar(u[:], u[:], 1.0, None, ALU.subtract))
        do(v.tensor_scalar(r[:], u[:], 1e-30, None, ALU.max))
        do(v.reciprocal(r[:], r[:]))
        do(v.tensor_tensor(r[:], r[:], big[:], ALU.mult))
        do(v.scalar_tensor_tensor(r[:], u[:], 0.0, r[:], ALU.is_le, ALU.add))
        do(v.tensor_tensor(r[:], r[:], e[:], ALU.mult))
        do(v.scalar_tensor_tensor(dts[:, 2, :, :], raw[:], 0.0, r[:], ALU.max, ALU.add))
        do(v.tensor_copy(u[:], dts[:, 2, :, :]))
        do(v.tensor_tensor(dts[:, 0, :, :], u[:], head(3), ALU.mult))
        dve.wait_ge(self.s_pe, 2)
        pre, tot = (k.ps[:, b, 0:n].rearrange("p (c h) -> p c h", c=CHUNKS) for b in (3, 4))
        do(v.tensor_copy(dts[:, 1, :, :], pre))
        do(v.tensor_tensor(e[:], tot, dts[:, 1, :, :], ALU.subtract))
        dve.wait_ge(self.s_act, 4)


def ssm(k, st, nxt, pre, tables):
    nc, ps = k.nc, k.ps
    v = nc.vector
    with ExitStack() as ctx:
        def sb(n, s, d=F32):
            return k.sb("ssm_" + n, s, d, ctx)
        u, cw, cv, zs = k.wide[:, 16:20, 0:3 + SEQ], sb("conv", [P, 4, SEQ]), sb("xbc", [P, 4, SEQ]), k.wide[:, 20:22, 0:SEQ]
        gs = sb("group", [P, 5 * CHUNKS, RPG])
        xt, xd, bt = sb("xdt", [P, 2 * P]), sb("xend", [P, 2 * P]), sb("btok", [P, P])
        cbm, seg, mm = sb("cb", [P, P]), sb("seg", [P, RPG, P]), sb("m", [P, RPG, P])
        ebc, cs = sb("ebc", [P, RPG, P]), sb("cs", [P, RPG, P])
        hs, ht, yg = sb("state", [P, 2 * P]), sb("statet", [P, 2 * P]), sb("yg", [P, 2, SEQ])
        sem = {x: k.sem("ssm_" + x) for x in (
            "lin_done", "lin_free", "conv", "silu", "group", "tr", "cb", "bc", "xt", "xd", "cbm", "seg", "m",
            "bt", "ebc", "dec", "cs", "y", "state", "gate")}
        steps, conv_steps = Steps(k.sem("ssm_steps")), Steps(k.sem("ssm_conv_steps"))
        dts = sb("dts", [P, 5, CHUNKS, SSM_HEADS])
        dt = StepSizes(k, dts, ctx)
        sqg = sb("squares", [P, SEQ])
        n = k.nsem
        b_acc, b_sq = k.ncount["accumulated"], k.ncount["squared"]
        k.ncount["accumulated"] += 1 + 2 * GROUPS
        k.ncount["squared"] += 2 * GROUPS
        TR, CB, BC, Y, S = ps[:, 2, :], ps[:, 3, :], ps[:, 4, :], (ps[:, 5, :], ps[:, 6, :]), ps[:, 7, :]

        def scal(q, c, r=None):
            return gs[:, q * CHUNKS + c, :] if r is None else gs[:, q * CHUNKS + c, r:r + 1]

        with nc.Block() as block:
            @block.sync
            def _(sp):
                k.stream(sp, st, nxt)

            @block.tensor
            def _(pe):
                def piece(i, p):
                    k.split_ready(pe, st, i, p)
                    wait(pe, sem["lin_free"], 6 * i + p - 1)
                    first = isinstance(i, int) and i == p == 0
                    k.product(st, p, ps[:, p % 2, :], k.hx(0, SEQ), before=(lambda f: pre.ready(pe, f)) if first else None).then_inc(sem["lin_done"], 1)

                def prep(s, c):
                    n, t = 4 * s + c, slice(c * P, (c + 1) * P)
                    wait(pe, sem["silu"], 4 * s + 4)
                    if c == 0:
                        pe.wait_ge(sem["group"], s + 2)
                    wait(pe, sem["xt"], n)
                    wait(pe, sem["bt"], n)
                    for q in range(3):
                        m = nc.tensor.transpose(TR[:, q * P:(q + 1) * P], cv[:, q, t], k.ident)
                    m.then_inc(sem["tr"], 1)
                    wait(pe, sem["cbm"], n)
                    nc.tensor.matmul(CB[:, 0:P], cv[:, 2, t], cv[:, 3, t], start=True, stop=True).then_inc(sem["cb"], 1)
                    wait(pe, sem["ebc"], 3 * s + max(c - 1, 0))
                    wait(pe, sem["seg"], n)
                    for r in range(RPG):
                        m = nc.tensor.matmul(BC[:, r * P:(r + 1) * P], scal(0, c, r).to_broadcast([P, P]), k.tri, start=True, stop=True)
                    m.then_inc(sem["bc"], 1)

                def out(s, c):
                    n = 4 * s + c
                    wait(pe, sem["m"], n + 1)
                    if c == 0:
                        wait(pe, sem["gate"], 2 * s)
                    else:
                        wait(pe, sem["state"], 3 * s + c)
                        wait(pe, sem["cs"], 3 * s + c)
                    for r in range(RPG):
                        o = Y[r // 2][64 * (r % 2):64 * (r % 2) + 64, c * P:(c + 1) * P]
                        m = nc.tensor.matmul(o, xt[:, 64 * r:64 * r + 64], mm[:, r, :], start=True, stop=c == 0)
                        if c:
                            m = nc.tensor.matmul(o, hs[:, 64 * r:64 * r + 64], cs[:, r, :], start=False, stop=True)
                    if c < CHUNKS - 1:
                        wait(pe, sem["bt"], n + 1)
                        wait(pe, sem["xd"], n + 1)
                        m = nc.tensor.matmul(S[:, 0:2 * P], bt[:], xd[:], start=True, stop=True)
                    m.then_inc(sem["y"], 1)

                def step(i, lin=True, scan=True):
                    for p in range(6):
                        if lin:
                            piece(i, p)
                        if not scan and p == 0:
                            dt.pe_raw(pe)
                        if not scan and p == 2:
                            dt.pe_sums(pe)
                        if scan:
                            if 1 <= p <= 4:
                                out(i - 1, p - 1)
                            if p <= 3:
                                prep(i - 1, p)
                pre.pe(pe)
                step(0, scan=False)
                step(1)
                with pe.Fori(2, GROUPS) as i:
                    step(i)
                step(GROUPS, lin=False)

            @block.scalar
            def _(act):
                def evict(i, p):
                    act.wait_ge(sem["lin_done"], 6 * i + p + 1)
                    k.high(act, st, st.after(i, p, st.depth))
                    if p < 4:
                        wait(act, sem["conv"], 4 * i - 3 + p if not isinstance(i, int) or i else 0)
                        nc.scalar.activation(u[:, p, 3:3 + SEQ], ps[:, p % 2, :], ACT.Copy).then_inc(sem["lin_free"], 1)
                    else:
                        wait(act, sem["gate"], 2 * i)
                        nc.scalar.activation(zs[:, p - 4, :], ps[:, p % 2, :], ACT.Silu).then_inc(sem["lin_free"], 1)

                def chunk(s, c):
                    n = 4 * s + c
                    act.wait_ge(sem["xt"], n + 1)
                    wait(act, sem["y"], n)
                    nc.scalar.activation(bt[:], TR[:, 2 * P:3 * P], ACT.Copy).then_inc(sem["bt"], 1)
                    act.wait_ge(sem["seg"], n + 1)
                    nc.scalar.activation(seg[:], seg[:], ACT.Exp).then_inc(sem["dec"], 1)
                    if c:
                        wait(act, sem["cs"], 3 * s + c - 1)
                        nc.scalar.activation(ebc[:].rearrange("p r l -> p (r l)"), BC, ACT.Exp).then_inc(sem["ebc"], 1)

                def step(i, lin=True, scan=True):
                    if scan:
                        wait(act, sem["gate"], 2 * (i - 1))
                        for q in (2, 3, 0, 1):
                            act.wait_ge(sem["conv"], 4 * (i - 1) + q + 1)
                            nc.scalar.activation(cv[:, q, :], cw[:, q, :], ACT.Silu).then_inc(sem["silu"], 1)
                    for p in range(6):
                        if not scan and p == 0:
                            dt.act_softplus(act)
                        if not scan and p == 3:
                            dt.act_decays(act)
                        if lin:
                            evict(i, p)
                        if scan and p < 4:
                            chunk(i - 1, p)
                k.high_first(act, st)
                pre.act(act)
                tables.act(act)
                step(0, scan=False)
                step(1)
                with act.Fori(2, GROUPS - 1) as i:
                    step(i)
                step(GROUPS - 1)
                step(GROUPS, lin=False)

            @block.gpsimd
            def _(pool):
                def scaled_c(s, c):
                    pool.wait_ge(sem["ebc"], 3 * s + c)
                    wait(pool, sem["y"], 4 * s + c)
                    nc.gpsimd.tensor_tensor(cs[:], ebc[:], cv[:, 3:4, c * P:(c + 1) * P].to_broadcast([P, RPG, P]),
                                            ALU.mult).then_inc(sem["cs"], 1)

                def squares(s):
                    for j in range(2):
                        pool.wait_ge(sem["gate"], 2 * s + j + 1)
                        nc.gpsimd.tensor_tensor(sqg[:], yg[:, j, :], yg[:, j, :], ALU.mult).then_inc(n["squared"], 1)
                        pool.wait_ge(n["squared"], 2 * s + b_sq + j + 1)
                        nc.gpsimd.tensor_tensor(k.acc[:, 0:SEQ], k.acc[:, 0:SEQ], sqg[:], ALU.add).then_inc(n["accumulated"], 1)
                        pool.wait_ge(n["accumulated"], 2 * s + b_acc + j + 2)

                def step(i, lin=True, scan=True):
                    for p in range(6):
                        if lin:
                            k.low(pool, st, st.after(i, p, st.depth))
                        if scan and 1 <= p < CHUNKS:
                            scaled_c(i - 1, p)
                    if scan:
                        squares(i - 1)
                for u in range(st.depth):
                    k.low(pool, st, (0, u))
                pool.wait_ge(n["rstd_steps"], k.ncount["rstd_steps"])
                nc.gpsimd.memset(k.acc[:], 0.0).then_inc(n["accumulated"], 1)
                pool.wait_ge(n["accumulated"], b_acc + 1)
                step(0, scan=False)
                step(1)
                with pool.Fori(2, GROUPS - 1) as i:
                    step(i)
                step(GROUPS - 1)
                step(GROUPS, lin=False)

            @block.vector
            def _(dve):
                def do(ins):
                    steps.mark(ins)
                    steps.settle(dve)

                def conv(s, q):
                    tile = (2 * s, 2 * s + 1, 16 + s, 24 + s)[q]
                    dve.wait_ge(sem["lin_free"], 6 * s + q + 1)
                    wait(dve, sem["silu"], 4 * s)
                    acc = cw[:, q, :]

                    def do(ins):
                        conv_steps.mark(ins)
                        conv_steps.settle(dve)
                    do(v.tensor_scalar(acc, u[:, q, 0:SEQ], k.col(V_CW + tile), k.col(V_CB + tile), ALU.mult, ALU.add))
                    for j in range(1, 4):
                        ins = v.scalar_tensor_tensor(acc, u[:, q, j:j + SEQ], k.col(V_CW + 32 * j + tile), acc, ALU.mult, ALU.add)
                        if j < 3:
                            do(ins)
                        else:
                            ins.then_inc(sem["conv"], 1)

                def chunk(s, c):
                    n, b4 = 4 * s + c, [P, RPG, 64]
                    dve.wait_ge(sem["tr"], n + 1)
                    wait(dve, sem["y"], n)
                    x4 = xt[:].rearrange("p (r d) -> p r d", r=RPG)
                    v.tensor_tensor(x4, TR[:, 0:2 * P].rearrange("p (r d) -> p r d", r=RPG),
                                    scal(2, c).unsqueeze(2).to_broadcast(b4), ALU.mult).then_inc(sem["xt"], 1)
                    dve.wait_ge(sem["cb"], n + 1)
                    v.tensor_tensor(cbm[:], CB[:, 0:P], k.tri, ALU.mult).then_inc(sem["cbm"], 1)
                    dve.wait_ge(sem["xt"], n + 1)
                    v.tensor_tensor(xd[:].rearrange("p (r d) -> p r d", r=RPG), x4,
                                    scal(3, c).unsqueeze(2).to_broadcast(b4), ALU.mult).then_inc(sem["xd"], 1)
                    dve.wait_ge(sem["bc"], n + 1)
                    for r in range(RPG):
                        ins = v.tensor_scalar(seg[:, r, :], BC[:, r * P:(r + 1) * P], scal(1, c, r), 0.0, ALU.subtract, ALU.min)
                    ins.then_inc(sem["seg"], 1)
                    dve.wait_ge(sem["dec"], n + 1)
                    dve.wait_ge(sem["cbm"], n + 1)
                    v.tensor_tensor(mm[:], seg[:], cbm[:].unsqueeze(1).to_broadcast([P, RPG, P]), ALU.mult).then_inc(sem["m"], 1)

                def carry(s, c):
                    n, b4 = 4 * s + c, [P, RPG, 64]
                    if c == CHUNKS - 1:
                        return
                    if c:
                        do(v.tensor_tensor(ht[:].rearrange("p (r d) -> p r d", r=RPG), hs[:].rearrange("p (r d) -> p r d", r=RPG),
                                           scal(4, c).unsqueeze(2).to_broadcast(b4), ALU.mult))
                        dve.wait_ge(sem["y"], n + 1)
                        v.tensor_tensor(hs[:], ht[:], S[:, 0:2 * P], ALU.add).then_inc(sem["state"], 1)
                    else:
                        dve.wait_ge(sem["y"], n + 1)
                        v.tensor_copy(hs[:], S[:, 0:2 * P]).then_inc(sem["state"], 1)
                    dve.wait_ge(sem["state"], 3 * s + c + 1)

                def gate(s):
                    dve.wait_ge(sem["y"], 4 * s + 4)
                    dve.wait_ge(sem["lin_free"], 6 * s + 6)
                    for j in range(2):
                        wait(dve, n["squared"], 2 * s + j - 1 + b_sq if not isinstance(s, int) or s else 0)
                        do(v.scalar_tensor_tensor(yg[:, j, :], cv[:, j, :], k.dexp[:, bass.ds(2 * s + j, 1)], Y[j], ALU.mult, ALU.add))
                        do(v.tensor_tensor(yg[:, j, :], yg[:, j, :], zs[:, j, :], ALU.mult))
                        v.tensor_copy(k.wide[:, bass.ds(2 * s + j, 1), 0:SEQ].rearrange("p a t -> p (a t)"), yg[:, j, :]).then_inc(sem["gate"], 1)

                def step(i, lin=True, scan=True):
                    if scan:
                        steps.begin(i - 1)
                        v.tensor_copy(gs[:], dts[:].rearrange("p q c h -> p (q c) h")[:, :, bass.ds(RPG * (i - 1), RPG)]).then_inc(sem["group"], 1)
                        dve.wait_ge(sem["group"], i + 1)
                    if lin:
                        conv_steps.begin(i)
                    for p in range(4):
                        if scan:
                            chunk(i - 1, p)
                        if lin:
                            conv(i, p)
                        if scan:
                            carry(i - 1, p)
                    if lin:
                        conv_steps.end()
                    if scan:
                        gate(i - 1)
                        steps.end()
                v.memset(u[:, :, 0:3], 0.0).then_inc(sem["group"], 1)
                dve.wait_ge(sem["group"], 1)
                pre.dve(dve)
                tables.dve(dve)
                dt.dve(dve)
                step(0, scan=False)
                step(1)
                with dve.Fori(2, GROUPS) as i:
                    step(i)
                step(GROUPS, lin=False)


def project(k, name, st, nxt, ksplit, x, parts, T, store, stored, pre=None):
    nc, ps = k.nc, k.ps
    hs = halves(T)
    per = st.units // ksplit * len(hs)
    tiles = per // len(hs)
    s_done, s_free = k.sem(name + "_done"), k.sem(name + "_free")
    s_half = k.sem(name + "_half") if ksplit > 1 else None
    n = k.nsem
    spread = pre.spread if pre else Spread(k, st.kt * ksplit, x, *parts)
    b_sq, b_acc = k.ncount["squared"], k.ncount["accumulated"]
    k.ncount["squared"] += tiles * st.iterations
    k.ncount["accumulated"] += 1 + tiles * st.iterations
    with nc.Block() as block:
        @block.sync
        def _(sp):
            k.stream(sp, st, nxt)

        @block.gpsimd
        def _(pool):
            k.low_all(pool, st)

        @block.tensor
        def _(pe):
            def step(i):
                for u in range(st.units):
                    tile, part = divmod(u, ksplit)
                    k.split_ready(pe, st, i, u)
                    for b, (c, w) in enumerate(hs):
                        q = tile * len(hs) + b
                        if part == 0:
                            wait(pe, s_free, per * i + q - 1)
                        first = isinstance(i, int) and tile == b == 0
                        xs = spread.parts(c, w)
                        m = k.product(st, u, ps[:, q % (2 * ksplit), 0:w], lambda f: xs(part * st.kt + f), start=part == 0, stop=part == ksplit - 1,
                                      before=(lambda f: spread.ready(pe, part * st.kt + f)) if first else None)
                        if part == ksplit - 1:
                            m.then_inc(s_done, 1)
                        elif b == len(hs) - 1:
                            m.then_inc(s_half, 1)
            if pre:
                pre.pe(pe)
            step(0)
            with pe.Fori(1, st.iterations) as i:
                step(i)

        @block.scalar
        def _(act):
            def step(i):
                for u in range(st.units):
                    tile, part = divmod(u, ksplit)
                    if part == ksplit - 1:
                        act.wait_ge(s_free, per * i + (tile + 1) * len(hs))
                    else:
                        act.wait_ge(s_half, tiles * i + tile + 1)
                    k.high(act, st, st.after(i, u, st.depth))
                    if part == ksplit - 1:
                        nc.scalar.activation(k.sq[:, 0:T], stored(tiles * i + tile), ACT.Square).then_inc(n["squared"], 1)
            k.high_first(act, st)
            if pre:
                pre.act(act)
            else:
                for f in range(st.kt * ksplit):
                    spread.act(act, f)
            step(0)
            if st.iterations > 2:
                with act.Fori(1, st.iterations - 1) as i:
                    step(i)
            step(st.iterations - 1)

        @block.vector
        def _(dve):
            if pre:
                pre.dve(dve)
            else:
                for f in range(st.kt * ksplit):
                    spread.dve(dve, f)
            nc.vector.memset(k.acc[:], 0.0).then_inc(n["accumulated"], 1)
            dve.wait_ge(n["accumulated"], b_acc + 1)
            with dve.Fori(0, st.iterations) as i:
                for t in range(tiles):
                    for b, (c, w) in enumerate(hs):
                        q = t * len(hs) + b
                        dve.wait_ge(s_done, per * i + q + 1)
                        store(tiles * i + t, c, w, ps[:, q % (2 * ksplit), 0:w]).then_inc(s_free, 1)
                    dve.wait_ge(n["squared"], tiles * i + b_sq + t + 1)
                    nc.vector.tensor_tensor(k.acc[:, 0:T], k.acc[:, 0:T], k.sq[:, 0:T], ALU.add).then_inc(n["accumulated"], 1)
                    dve.wait_ge(n["accumulated"], tiles * i + b_acc + t + 2)


def swa(k, st, nxt, pre):
    nc, ps = k.nc, k.ps
    v = nc.vector
    with ExitStack() as ctx:
        def sb(n, s, d=F32):
            return k.sb("swa_" + n, s, d, ctx)
        raw, rop = sb("raw", [P, 3, SEQ]), sb("roped", [P, 3, SEQ])
        vT, vt, gate = sb("vT", [P, SEQ]), sb("v", [P, 4, 64]), k.wide[:, 8:16, 0:SEQ]
        t1, t2 = sb("t1", [P, SEQ]), sb("t2", [P, SEQ])
        p, pn, pt = sb("p", [P, 4, 2 * P]), sb("pn", [P, 4, 2 * P]), sb("pt", [P, 4, 2, P])
        mx, nm, den, es, rd = (sb(x, [P, 4]) for x in ("mx", "nm", "den", "es", "rd"))
        nsg = sb("nsg", [P, 4])
        sem = {x: k.sem("swa_" + x) for x in (
            "lin_done", "lin_free", "rot", "rope", "vtr", "v", "s", "nm", "exp", "es", "pn", "t", "pt", "pv", "out")}
        steps = Steps(k.sem("swa_steps"))
        S = ps[:, 2:4, :].rearrange("p b (x j) -> p (b x) j", x=2)
        PT = ps[:, 4:6, :].rearrange("p b (x j) -> p (b x) j", x=2)
        O = (ps[:, 6, :], ps[:, 7, :])
        order = (0, 2, 3)
        HEAD = (0, 2, 1, 3)

        with nc.Block() as block:
            @block.sync
            def _(sp):
                k.stream(sp, st, nxt)

            @block.gpsimd
            def _(pool):
                k.low_all(pool, st)

            @block.tensor
            def _(pe):
                def piece(i, q):
                    k.split_ready(pe, st, i, q)
                    wait(pe, sem["lin_free"], 6 * i + q - 1)
                    first = isinstance(i, int) and i == q == 0
                    k.product(st, q, ps[:, q % 2, :], k.hx(0, SEQ), before=(lambda f: pre.ready(pe, f)) if first else None).then_inc(sem["lin_done"], 1)

                def rot(s, q):
                    pe.wait_ge(sem["lin_free"], 6 * s + order[q] + 1)
                    if q == 0:
                        wait(pe, sem["pt"], 4 * s)
                    if q == 2:
                        pe.wait_ge(sem["rope"], 3 * s + 1)
                    nc.tensor.matmul(ps[:, 4 + q % 2, :], k.rot1, raw[:, q, :], start=True, stop=True).then_inc(sem["rot"], 1)

                def vtr(s):
                    pe.wait_ge(sem["lin_free"], 6 * s + 2)
                    wait(pe, sem["exp"], 16 * s)
                    for t in range(4):
                        m = nc.tensor.transpose(ps[:, 2, t * P:(t + 1) * P], vT[:, t * P:(t + 1) * P], k.ident)
                    m.then_inc(sem["vtr"], 1)

                def scores(s, n):
                    if n == 0:
                        pe.wait_ge(sem["v"], s + 1)
                        pe.wait_ge(sem["rope"], 3 * s + 3)
                    else:
                        pe.wait_ge(sem["exp"], 16 * s + 4 * n)
                    k0 = 0 if n else P
                    for x, r in enumerate(HEAD):
                        h = slice(64 * (r % 2), 64 * (r % 2) + 64)
                        nc.tensor.matmul(S[:, x, k0:2 * P], k.identb[:], k.maskb[:, k0:2 * P], start=True, stop=False)
                        m = nc.tensor.matmul(S[:, x, k0:2 * P], rop[h, 1 + r // 2, n * P:(n + 1) * P],
                                             rop[h, 0, (n - 1) * P + k0:(n + 1) * P], start=False, stop=True)
                    m.then_inc(sem["s"], 1)

                def trans(s, n):
                    pe.wait_ge(sem["pn"], 4 * s + n + 1)
                    wait(pe, sem["pt"], 4 * s + n)
                    for r in range(4):
                        for b in range(0 if n else 1, 2):
                            m = nc.tensor.transpose(PT[:, r, b * P:(b + 1) * P], pn[:, r, b * P:(b + 1) * P], k.ident)
                    m.then_inc(sem["t"], 1)

                def pv(s, n):
                    pe.wait_ge(sem["pt"], 4 * s + n + 1)
                    if n == 0:
                        wait(pe, sem["out"], 2 * s)
                    for x, r in enumerate(HEAD):
                        o = O[r // 2][64 * (r % 2):64 * (r % 2) + 64, n * P:(n + 1) * P]
                        for b in range(0 if n else 1, 2):
                            m = nc.tensor.matmul(o, vt[:, n - 1 + b, :], pt[:, x, b, :], start=b == 0 or not n, stop=b == 1)
                    m.then_inc(sem["pv"], 1)

                def step(i, lin=True, att=True):
                    s = i - 1
                    for q in range(6):
                        if att:
                            if q == 0:
                                rot(s, 0), rot(s, 1)
                            if q == 1:
                                rot(s, 2), vtr(s)
                            if q == 2:
                                scores(s, 0)
                            if q == 3:
                                trans(s, 0), scores(s, 1)
                            if q == 4:
                                pv(s, 0), trans(s, 1), scores(s, 2)
                            if q == 5:
                                pv(s, 1), trans(s, 2), scores(s, 3)
                        if lin:
                            piece(i, q)
                    if att:
                        pv(s, 2), trans(s, 3), pv(s, 3)
                pre.pe(pe)
                step(0, att=False)
                step(1)
                with pe.Fori(2, KV) as i:
                    step(i)
                step(KV, lin=False)

            @block.scalar
            def _(act):
                def evict(i, q):
                    act.wait_ge(sem["lin_done"], 6 * i + q + 1)
                    k.high(act, st, st.after(i, q, st.depth))
                    src = ps[:, q % 2, :]
                    if q in order:
                        wait(act, sem["rope"], 3 * i - 2 + order.index(q) if not isinstance(i, int) or i else 0)
                        nc.scalar.activation(raw[:, order.index(q), :], src, ACT.Copy).then_inc(sem["lin_free"], 1)
                    elif q == 1:
                        wait(act, sem["vtr"], i)
                        nc.scalar.activation(vT[:], src, ACT.Copy).then_inc(sem["lin_free"], 1)
                    else:
                        nc.scalar.activation(gate[:, bass.ds(2 * i + q - 4, 1), :].rearrange("p a t -> p (a t)"), src, ACT.Silu).then_inc(sem["lin_free"], 1)

                def vtok(s):
                    act.wait_ge(sem["vtr"], s + 1)
                    wait(act, sem["pv"], 4 * s)
                    nc.scalar.activation(vt[:], ps[:, 2, :].rearrange("p (t d) -> p t d", t=4)[:, :, 0:64], ACT.Copy).then_inc(sem["v"], 1)

                def exps(s, n):
                    act.wait_ge(sem["nm"], 4 * s + n + 1)
                    wait(act, sem["pn"], 4 * s + n)
                    k0 = 0 if n else P
                    for r in range(4):
                        nc.scalar.activation(p[:, r, k0:2 * P], S[:, r, k0:2 * P], ACT.Exp, bias=nm[:, r:r + 1], scale=0.125,
                                             accum_out=den[:, r:r + 1]).then_inc(sem["exp"], 1)
                    nc.scalar.activation(es[:], es[:], ACT.Exp).then_inc(sem["es"], 1)

                def store_pt(s, n):
                    act.wait_ge(sem["t"], 4 * s + n + 1)
                    wait(act, sem["pv"], 4 * s + n)
                    b0 = 0 if n else 1
                    nc.scalar.activation(pt[:, :, b0:2, :], PT.rearrange("p r (b q) -> p r b q", b=2)[:, :, b0:2, :],
                                         ACT.Copy).then_inc(sem["pt"], 1)

                def step(i, lin=True, att=True):
                    s = i - 1
                    for q in range(6):
                        if att:
                            if q == 2:
                                vtok(s)
                                exps(s, 0)
                            if q >= 3:
                                store_pt(s, q - 3)
                                exps(s, q - 2)
                        if lin:
                            evict(i, q)
                    if att:
                        store_pt(s, 3)
                k.high_first(act, st)
                pre.act(act)
                step(0, att=False)
                step(1)
                with act.Fori(2, KV - 1) as i:
                    step(i)
                step(KV - 1)
                step(KV, lin=False)

            @block.vector
            def _(dve):
                def do(ins):
                    steps.mark(ins)
                    steps.settle(dve)

                def step(s):
                    steps.begin(s)
                    do(v.tensor_copy(nsg[:].rearrange("p (b f) -> p f b", b=2),
                                     k.nsink[:, bass.ds(4 * s, 4)].rearrange("p (f b) -> p f b", b=2)))
                    for q in range(3):
                        dve.wait_ge(sem["lin_free"], 6 * s + order[q] + 1)
                        do(v.tensor_tensor(t1[:], raw[:, q, :], k.cos1[:], ALU.mult))
                        dve.wait_ge(sem["rot"], 3 * s + q + 1)
                        do(v.tensor_tensor(t2[:], ps[:, 4 + q % 2, :], k.sin1[:], ALU.mult))
                        v.tensor_tensor(rop[:, q, :], t1[:], t2[:], ALU.add).then_inc(sem["rope"], 1)
                        dve.wait_ge(sem["rope"], 3 * s + q + 1)
                    for n in range(4):
                        k0 = 0 if n else P
                        dve.wait_ge(sem["s"], 4 * s + n + 1)
                        do(v.reduce_max(mx[:], S[:, :, k0:2 * P], AX.X))
                        do(v.scalar_tensor_tensor(nm[:], mx[:], -0.125, nsg[:], ALU.mult, ALU.min))
                        v.tensor_tensor(es[:], nm[:], nsg[:], ALU.subtract).then_inc(sem["nm"], 1)
                        dve.wait_ge(sem["es"], 4 * s + n + 1)
                        do(v.tensor_tensor(rd[:], den[:], es[:], ALU.add))
                        do(v.reciprocal(rd[:], rd[:]))
                        wait(dve, sem["t"], 4 * s + n)
                        w = 2 * P - k0
                        v.tensor_tensor(pn[:, :, k0:2 * P], p[:, :, k0:2 * P], rd[:].unsqueeze(2).to_broadcast([P, 4, w]),
                                        ALU.mult).then_inc(sem["pn"], 1)
                    dve.wait_ge(sem["pv"], 4 * s + 4)
                    dve.wait_ge(sem["lin_free"], 6 * s + 6)
                    for j in range(2):
                        v.tensor_tensor(k.wide[:, bass.ds(2 * s + j, 1), 0:SEQ].rearrange("p a t -> p (a t)"), O[j],
                                        gate[:, bass.ds(2 * s + j, 1), :].rearrange("p a t -> p (a t)"), ALU.mult).then_inc(sem["out"], 1)
                    steps.end()
                pre.dve(dve)
                step(0)
                with dve.Fori(1, KV) as s:
                    step(s)


def pairs(k, name, st, nxt, diff, pre=None, mb=None, vall=None, head=None):
    sync_first, pool_first, pe_first, act_first, dve_first = head or (lambda engine: None,) * 5
    nc, ps = k.nc, k.ps
    v = nc.vector
    NI = 8
    NP = 6 if diff else 4
    whole, halved = range(KT), (range(KT // 2), range(KT // 2, KT))
    if diff:
        slots = [[(q, whole)] for q in range(6)] + [[]]
    else:
        parts = [(j // 2, halved[j % 2]) for j in range(8)]
        slots = [parts[0:2]] + [parts[j:j + 1] for j in range(2, 8)]
    with ExitStack() as ctx:
        def sb(n, s, d=F32):
            return k.sb(f"{name}_{n}", s, d, ctx)
        raw = k.wide[:, 8:10, :] if diff else k.wide[:, 20:22, :]
        rop, t1, t2 = k.wide[:, 10:12, :], k.wide[:, 12:14, :], k.wide[:, 14, :]
        vT, vt = k.wide[:, 15, :], sb("v", [P, 5, P])
        maps = 1 if diff else 2
        p, pn = k.wide[:, 16:18, :], k.wide[:, 18:18 + maps, :]
        pt, mx, nm, den, rd = sb("pt", [P, maps, 512]), sb("mx", [P, 2]), sb("nm", [P, 2]), sb("den", [P, 2]), sb("rd", [P, 2])
        ptl = sb("ptl", [META, maps, META])
        osq, lnv, rstd = (k.wide[:, j, :] for j in range(19, 22)) if diff else (None,) * 3

        def head(s):
            return k.wide[:, bass.ds(s, 1), :].rearrange("p a t -> p (a t)")
        sem = {x: k.sem(f"{name}_{x}") for x in (
            "lin_done", "lin_free", "cos", "rot", "rope", "v", "s", "nm", "exp", "pn", "t", "pt", "pv", "o") + (
            ("vtr", "osq", "oss", "rstd", "out") if diff else ())}
        steps = Steps(k.sem(name + "_steps"))
        S = ps[:, 2:6, :].rearrange("p (c x) j -> p c (x j)", c=2)
        TP = ps[:, 6:8, :]
        O = ps[:, 7, :] if diff else ps[:, 3, P:3 * P]

        def blocks(n):
            return [(b, *TILES[b]) for b in range(n + 1)]

        with nc.Block() as block:
            @block.sync
            def _(sp):
                sync_first(sp)
                k.stream(sp, st, nxt)

            @block.gpsimd
            def _(pool):
                pool_first(pool)
                k.low_all(pool, st)

            @block.tensor
            def _(pe):
                pe_first(pe)

                def piece(i, q, tiles):
                    u, b = divmod(q, 2)
                    if tiles[0] == 0:
                        k.split_ready(pe, st, i, u)
                        wait(pe, sem["lin_free"], NP * i + q - 1)
                    first = pre and isinstance(i, int) and i == q == 0
                    m = k.product(st, u, ps[:, b, 0:HALF], k.hx(b * HALF, HALF), before=(lambda f: pre.ready(pe, f)) if first else None, tiles=tiles)
                    if tiles[-1] == KT - 1:
                        m.then_inc(sem["lin_done"], 1)

                def rot(s, q):
                    if q == 0:
                        pe.wait_ge(sem["lin_free"], NP * s + NP)
                        wait(pe, sem["exp"], 10 * s)
                    elif not diff:
                        wait(pe, sem["o"], 5 * s)
                    for b in range(2):
                        m = nc.tensor.matmul(ps[:, 4 - 2 * q + b, 0:HALF], k.rot2, raw[:, q, b * HALF:(b + 1) * HALF], start=True, stop=True)
                    m.then_inc(sem["rot"], 1)

                def vtr(s):
                    wait(pe, sem["o"], 5 * s)
                    wait(pe, sem["pt"], 5 * s)
                    for t, (c, n) in enumerate(TILES):
                        m = nc.tensor.transpose(ps[0:n, 6 + t // 4, (t % 4) * P:(t % 4 + 1) * P], vT[:, c:c + n], k.ident)
                    m.then_inc(sem["vtr"], 1)

                def scores(s, n):
                    c, nq = TILES[n]
                    N = c + nq
                    if n == 0:
                        pe.wait_ge(sem["rope"], 2 * s + 2)
                    elif n < 4:
                        pe.wait_ge(sem["exp"], 10 * s + 2 * n)
                    for x in range(2):
                        h = slice(64 * x, 64 * x + 64)
                        for lo, hi in (((0, c), (c, N)) if diff else ((0, min(N, 512)), (512, N))):
                            if lo >= hi:
                                continue
                            masked = not diff or lo == c
                            m = nc.tensor.matmul(S[0:nq, x, lo:hi], rop[h, 0, c:N], rop[h, 1, lo:hi], start=True, stop=not masked)
                            if masked:
                                mask = k.maskb[0:nq, P:P + nq] if diff else mb[0:nq, n, lo:hi]
                                m = nc.tensor.matmul(S[0:nq, x, lo:hi], k.identb[0:nq, 0:nq], mask, start=False, stop=True)
                    m.then_inc(sem["s"], 1)

                def trans(s, n):
                    _, nq = TILES[n]
                    if n == 0:
                        pe.wait_ge(sem["v"], s + 1)
                        if diff:
                            wait(pe, sem["rstd"], 3 * s - 2)
                    if n < 4:
                        wait(pe, sem["pt"], 5 * s + n)
                        pe.wait_ge(sem["pn"], 5 * s + n + 1)
                    if n == 3 and not diff:
                        pe.wait_ge(sem["o"], 5 * s + 3)
                    for x in range(maps):
                        for b, a, w in blocks(n):
                            m = nc.tensor.transpose(TP[0:w, x, b * nq:(b + 1) * nq], pn[0:nq, x, a:a + w], k.ident[0:nq, 0:nq])
                    m.then_inc(sem["t"], 1)

                def pv(s, n):
                    _, nq = TILES[n]
                    pe.wait_ge(sem["pt"], 5 * s + n + 1)
                    wait(pe, sem["o"], 5 * s + n)
                    if n == 2:
                        pe.wait_ge(sem["exp"], 10 * s + 8)
                    if n == 3:
                        pe.wait_ge(sem["pn"], 5 * s + 5)
                    for x in range(maps):
                        d = slice(0, P) if diff else slice(64 * x, 64 * x + 64)
                        for b, a, w in blocks(n):
                            r = pt[0:w, x, b * nq:(b + 1) * nq] if b < 4 else ptl[:, x, :]
                            m = nc.tensor.matmul(O[d, 0:nq], vt[0:w, b, d], r, start=b == 0, stop=b == n)
                    m.then_inc(sem["pv"], 1)

                def squares(s):
                    pe.wait_ge(sem["osq"], s + 1)
                    for b in range(2):
                        m = nc.tensor.matmul(ps[:, 6 + b, 0:HALF], k.ones, osq[:, b * HALF:(b + 1) * HALF], start=True, stop=True)
                    m.then_inc(sem["oss"], 1)

                def step(i, lin=True, att=True, tail=True):
                    s = i - 1
                    for q in range(6):
                        if lin:
                            for j, tiles in slots[q]:
                                piece(i, j, tiles)
                        if q == 0:
                            if tail:
                                pv(s - 1, 3), trans(s - 1, 4)
                            if att:
                                rot(s, 0)
                            if tail:
                                pv(s - 1, 4)
                            if att:
                                rot(s, 1)
                                if diff:
                                    vtr(s)
                        if q == 1 and tail and diff:
                            if att:
                                pe.wait_ge(sem["v"], s + 1)
                            squares(s - 1)
                        if att:
                            if q >= 3:
                                pv(s, q - 3)
                        for j, tiles in slots[6] if lin and q == 5 else ():
                            piece(i, j, tiles)
                        if att:
                            if q == 5 and not diff:
                                trans(s, 3), scores(s, 4)
                            else:
                                if q >= 1:
                                    scores(s, q - 1)
                                if q >= 2:
                                    trans(s, q - 2)
                if pre:
                    pre.pe(pe)
                step(0, att=False, tail=False)
                step(1, tail=False)
                with pe.Fori(2, NI) as i:
                    step(i)
                step(NI, lin=False)
                pv(NI - 1, 3), trans(NI - 1, 4), pv(NI - 1, 4)
                if diff:
                    pe.wait_ge(sem["pt"], 5 * NI)
                    pe.wait_ge(sem["o"], 5 * NI)
                    squares(NI - 1)

            @block.scalar
            def _(act):
                act_first(act)

                def evict(i, q):
                    u, b = divmod(q, 2)
                    act.wait_ge(sem["lin_done"], NP * i + q + 1)
                    if u < 2:
                        wait(act, sem["rot"], 2 * i - 1 + u if not isinstance(i, int) or i else 0)
                        wait(act, sem["cos"], 2 * i - 1 + u if not isinstance(i, int) or i else 0)
                        dst = raw[:, u, b * HALF:(b + 1) * HALF]
                    else:
                        wait(act, sem["vtr"], i)
                        dst = vT[:, b * HALF:(b + 1) * HALF]
                    nc.scalar.activation(dst, ps[:, b, 0:HALF], ACT.Copy).then_inc(sem["lin_free"], 1)

                def vtok(s):
                    if not diff:
                        wait(act, sem["pv"], 5 * s)
                        nc.scalar.activation(vt[:, 0:4, :], vall[:, bass.ds(s, 1), 0:4, :].rearrange("p a t d -> p (a t) d"), ACT.Copy)
                        nc.scalar.activation(vt[0:META, 4, :], vall[0:META, bass.ds(s, 1), 4, :].rearrange("p a d -> p (a d)"),
                                             ACT.Copy).then_inc(sem["v"], 1)
                        return
                    act.wait_ge(sem["vtr"], s + 1)
                    wait(act, sem["pv"], 5 * s)
                    nc.scalar.activation(vt[:, 0:4, :].rearrange("p t d -> p (t d)"), ps[:, 6, :], ACT.Copy)
                    nc.scalar.activation(vt[0:META, 4, :], ps[0:META, 7, 0:P], ACT.Copy).then_inc(sem["v"], 1)

                def exps(s, n):
                    c, nq = TILES[n]
                    act.wait_ge(sem["nm"], 5 * s + n + 1)
                    wait(act, sem["pn"], 5 * s + n)
                    for x in range(2):
                        nc.scalar.activation(p[0:nq, x, 0:c + nq], S[0:nq, x, 0:c + nq], ACT.Exp, bias=nm[0:nq, x:x + 1], scale=0.125,
                                             accum_out=den[0:nq, x:x + 1]).then_inc(sem["exp"], 1)

                def store_pt(s, n):
                    _, nq = TILES[n]
                    act.wait_ge(sem["t"], 5 * s + n + 1)
                    wait(act, sem["pv"], 5 * s + n)
                    if n == 4:
                        nc.scalar.activation(ptl[:], TP[0:META, 0:maps, 4 * META:5 * META], ACT.Copy)
                    w = min(n + 1, 4) * nq
                    nc.scalar.activation(pt[:, :, 0:w], TP[:, 0:maps, 0:w], ACT.Copy).then_inc(sem["pt"], 1)

                def store_o(s, n):
                    c, nq = TILES[n]
                    act.wait_ge(sem["pv"], 5 * s + n + 1)
                    nc.scalar.activation(head(s)[:, c:c + nq], O[:, 0:nq], ACT.Copy).then_inc(sem["o"], 1)

                def pieces(i, slot):
                    for j, tiles in slots[slot]:
                        if tiles[-1] == KT - 1:
                            evict(i, j)
                            if j % 2:
                                k.high(act, st, st.after(i, j // 2, st.depth))

                def take_sum(s):
                    act.wait_ge(sem["oss"], s + 1)
                    nc.scalar.activation(both(lnv), ps[:, 6:8, 0:HALF], ACT.Copy).then_inc(sem["rstd"], 1)

                def rms(s):
                    act.wait_ge(sem["rstd"], 3 * s + 1)
                    nc.scalar.activation(lnv, lnv, ACT.Ln, scale=1.0 / P, bias=k.eps[:]).then_inc(sem["rstd"], 1)
                    act.wait_ge(sem["rstd"], 3 * s + 2)
                    wait(act, sem["out"], s)
                    nc.scalar.activation(rstd, lnv, ACT.Exp, scale=-0.5).then_inc(sem["rstd"], 1)

                def squares(s):
                    act.wait_ge(sem["o"], 5 * s + 5)
                    nc.scalar.activation(osq, head(s), ACT.Square).then_inc(sem["osq"], 1)

                def step(i, lin=True, att=True, tail=True):
                    s = i - 1
                    if tail:
                        store_o(s - 1, 3), store_pt(s - 1, 4), store_o(s - 1, 4)
                    if att:
                        vtok(s)
                    if tail and diff:
                        squares(s - 1)
                    for q in range(6):
                        if lin:
                            pieces(i, q)
                        if q == 1 and tail and diff:
                            take_sum(s - 1)
                        if att:
                            if q >= 3:
                                store_o(s, q - 3)
                        if lin and q == 5:
                            pieces(i, 6)
                        if att:
                            if q >= 2:
                                store_pt(s, q - 2)
                            if q >= 1:
                                exps(s, q - 1)
                    if tail and diff:
                        rms(s - 1)
                k.high_first(act, st)
                if pre:
                    pre.act(act)
                step(0, att=False, tail=False)
                step(1, tail=False)
                with act.Fori(2, NI - 1) as i:
                    step(i)
                step(NI - 1)
                step(NI, lin=False)
                store_o(NI - 1, 3), store_pt(NI - 1, 4), store_o(NI - 1, 4)
                if diff:
                    squares(NI - 1), take_sum(NI - 1), rms(NI - 1)

            @block.vector
            def _(dve):
                dve_first(dve)

                def do(ins):
                    steps.mark(ins)
                    steps.settle(dve)

                def head_norm(s):
                    dve.wait_ge(sem["rstd"], 3 * s + 3)
                    v.scalar_tensor_tensor(head(s), head(s), k.sub8[:], rstd,
                                           ALU.mult, ALU.mult).then_inc(sem["out"], 1)

                def step(s, tail=True):
                    steps.begin(s)
                    for q in range(2):
                        dve.wait_ge(sem["lin_free"], NP * s + 2 * q + 2)
                        v.tensor_tensor(t1[:, q, :], raw[:, q, :], k.cos2, ALU.mult).then_inc(sem["cos"], 1)
                    dve.wait_ge(sem["cos"], 2 * s + 2)
                    for q in range(2):
                        dve.wait_ge(sem["rot"], 2 * s + q + 1)
                        do(v.tensor_tensor(both(t2), ps[:, 4 - 2 * q:6 - 2 * q, 0:HALF], both(k.sin2), ALU.mult))
                        v.tensor_tensor(rop[:, q, :], t1[:, q, :], t2, ALU.add).then_inc(sem["rope"], 1)
                        dve.wait_ge(sem["rope"], 2 * s + q + 1)
                    for n, (c, nq) in enumerate(TILES):
                        N = c + nq
                        dve.wait_ge(sem["s"], 5 * s + n + 1)
                        if diff:
                            do(v.reduce_max(mx[0:nq, :], S[0:nq, :, 0:N], AX.X))
                        else:
                            for x in range(2):
                                do(v.reduce_max(mx[0:nq, x:x + 1], S[0:nq, x, 0:N], AX.X))
                        v.tensor_scalar(nm[0:nq, :], mx[0:nq, :], -0.125, None, ALU.mult).then_inc(sem["nm"], 1)
                        dve.wait_ge(sem["exp"], 10 * s + 2 * n + 2)
                        do(v.reciprocal(rd[0:nq, :], den[0:nq, :]))
                        wait(dve, sem["t"], 5 * s + n)
                        if diff:
                            do(v.tensor_scalar(rd[0:nq, 1:2], rd[0:nq, 1:2], k.neglam[0:nq, :], None, ALU.mult))
                            do(v.tensor_scalar(pn[0:nq, 0, 0:N], p[0:nq, 1, 0:N], rd[0:nq, 1:2], None, ALU.mult))
                            v.scalar_tensor_tensor(pn[0:nq, 0, 0:N], p[0:nq, 0, 0:N], rd[0:nq, 0:1], pn[0:nq, 0, 0:N],
                                                   ALU.mult, ALU.add).then_inc(sem["pn"], 1)
                        else:
                            do(v.tensor_scalar(pn[0:nq, 0, 0:N], p[0:nq, 0, 0:N], rd[0:nq, 0:1], None, ALU.mult))
                            v.tensor_scalar(pn[0:nq, 1, 0:N], p[0:nq, 1, 0:N], rd[0:nq, 1:2], None, ALU.mult).then_inc(sem["pn"], 1)
                    if diff and tail:
                        head_norm(s - 1)
                    steps.end()
                if pre:
                    pre.dve(dve)
                step(0, tail=False)
                with dve.Fori(1, NI) as s:
                    step(s)
                if diff:
                    head_norm(NI - 1)


def index(k, st, vst, nxt, pre, mb, vall, ctx):
    nc, ps = k.nc, k.ps
    v = nc.vector
    NH = 8

    def sb(n, s, d=F32):
        return k.sb("idx_" + n, s, d, ctx)
    rop, raw, t1, t2 = k.wide[:, 0:5, :], k.wide[:, 5:10, :], k.wide[:, 10, :], k.wide[:, 11, :]
    wiT, wi = k.wide[:, 16, :], sb("wi", [P, 5, NH])
    kn, lnv, rstd = (k.wide[:, j, :] for j in (12, 13, 14))
    rel, sc, m8 = k.wide[:, 5:5 + NH, :], k.wide[:, 15, :], sb("m8", [P, 8])
    s_done, s_free, s_wip, s_sq, s_ss, s_r, s_kn, s_rot, s_rope, s_s, s_rel, s_acc = (k.sem("idx_" + x) for x in (
        "lin_done", "lin_free", "wi_product", "squares", "summed", "rstd", "kn", "rot", "rope", "scores", "relu", "acc"))
    s_vdone, s_vfree, s_vtr, s_vout = (k.sem("values_" + x) for x in ("lin_done", "lin_free", "transposed", "stored"))
    vT = k.wide[:, 18:20, :]
    values_after = [None, [0, 1], [2, 3], [4, 5], [6, 7]]
    steps = Steps(k.sem("idx_steps"))
    order = [4, 0, 1, 2, 3, 5]

    def sync_program(sp):
        k.stream(sp, st, vst)
        k.stream(sp, vst, nxt)

    def pool_program(pool):
        for u in range(st.units):
            k.low(pool, st, (0, u))
        k.low_all(pool, vst)

    def pe_program(pe):
        pre.pe(pe)

        def rotate(j):
            if j == 4:
                pe.wait_ge(s_kn, 1)
            else:
                pe.wait_ge(s_free, 2 * order.index(j) + 2)
            wait(pe, s_rope, j)
            for b in range(2):
                m = nc.tensor.matmul(ps[:, 2 + b, 0:HALF], k.rot2, raw[:, j, b * HALF:(b + 1) * HALF], start=True, stop=True)
            m.then_inc(s_rot, 1)

        for j in range(st.units):
            k.split_ready(pe, st, 0, j)
            for b in range(2):
                wait(pe, s_free, 2 * j + b - 1)
                k.product(st, j, ps[:, b, 0:HALF], k.hx(b * HALF, HALF), before=(lambda f: pre.ready(pe, f)) if j == b == 0 else None).then_inc(s_done, 1)
            if j == 1:
                pe.wait_ge(s_sq, 1)
                for b in range(2):
                    m = nc.tensor.matmul(ps[:, 4 + b, 0:HALF], k.ones, kn[:, b * HALF:(b + 1) * HALF], start=True, stop=True)
                m.then_inc(s_ss, 1)
            if j >= 2:
                rotate(j - 2)
        rotate(4)
        pe.wait_ge(s_free, 2 * st.units)
        for t, (c, n) in enumerate(TILES):
            m = nc.tensor.transpose(ps[0:n, 6 + t // 4, (t % 4) * P:(t % 4 + 1) * P], wiT[:, c:c + n], k.ident)
        m.then_inc(s_wip, 1)
        pe.wait_ge(s_rope, 5)

        def values(j):
            k.split_ready(pe, vst, *divmod(j, 4))
            for b in range(2):
                wait(pe, s_vfree, 2 * j + b - 1)
                k.product(vst, j % 4, ps[:, 4 + b, 0:HALF], k.hx(b * HALF, HALF)).then_inc(s_vdone, 1)

        def values_transposed(j):
            pe.wait_ge(s_vfree, 2 * j + 2)
            wait(pe, s_vout, j)
            for t, (c, n) in enumerate(TILES):
                m = nc.tensor.transpose(ps[0:n, 6 + t // 4, (t % 4) * P:(t % 4 + 1) * P], vT[:, j % 2, c:c + n], k.ident)
            m.then_inc(s_vtr, 1)
        def scores(n):
            c, nq = TILES[n]
            N = c + nq
            for x in range(NH):
                q = NH * (n - 1) + x
                h = slice(64 * (x % 2), 64 * (x % 2) + 64)
                wait(pe, s_rel, q - 1)
                for lo, hi in ((0, min(N, 512)), (512, N)):
                    if lo < hi:
                        m = nc.tensor.matmul(ps[0:nq, 2 * (q % 2) + lo // 512, 0:hi - lo], rop[h, x // 2, c:N], rop[h, 4, lo:hi], start=True, stop=True)
                m.then_inc(s_s, 1)
        scores(1)
        for n in range(1, 5):
            if n < 4:
                scores(n + 1)
            if n == 1:
                pe.wait_ge(s_acc, 1)
            for j in values_after[n]:
                values(j)
                if j:
                    values_transposed(j - 1)
        values_transposed(7)
        pe.wait_ge(s_rel, 4 * NH)
        pe.wait_ge(s_vout, 8)

    def act_program(act):
        k.high_first(act, st)
        pre.act(act)
        for j, u in enumerate(order):
            for b in range(2):
                act.wait_ge(s_done, 2 * j + b + 1)
                dst = wiT if u == 5 else raw[:, u, :]
                nc.scalar.activation(dst[:, b * HALF:(b + 1) * HALF], ps[:, b, 0:HALF], ACT.Copy).then_inc(s_free, 1)
            if j + 2 < st.units:
                k.high(act, st, (0, j + 2))
            else:
                k.high(act, vst, (0, j + 2 - st.units))
            if j == 0:
                act.wait_ge(s_free, 2)
                nc.scalar.activation(kn, raw[:, 4, :], ACT.Square).then_inc(s_sq, 1)
            if j == 1:
                act.wait_ge(s_ss, 1)
                nc.scalar.activation(both(lnv), ps[:, 4:6, 0:HALF], ACT.Ln, scale=1.0 / P, bias=k.eps[:]).then_inc(s_r, 1)
                act.wait_ge(s_r, 1)
                nc.scalar.activation(rstd, lnv, ACT.Exp, scale=-0.5).then_inc(s_r, 1)

        def store_values(j):
            act.wait_ge(s_vtr, j + 1)
            nc.scalar.activation(vall[:, j, 0:4, :].rearrange("p t d -> p (t d)"), ps[:, 6, :], ACT.Copy)
            nc.scalar.activation(vall[0:META, j, 4, :], ps[0:META, 7, 0:P], ACT.Copy).then_inc(s_vout, 1)

        def relus(n):
            c, nq = TILES[n]
            N = c + nq
            for x in range(NH):
                q = NH * (n - 1) + x
                act.wait_ge(s_s, q + 1)
                wait(act, s_acc, q - NH + 1)
                flat = ps[0:nq, 2 * (q % 2):2 * (q % 2) + 2, :].rearrange("p b j -> p (b j)")
                nc.scalar.activation(rel[0:nq, x, 0:N], flat[:, 0:N], ACT.Relu, scale=0.125).then_inc(s_rel, 1)
        relus(1)
        for n in range(1, 5):
            if n < 4:
                relus(n + 1)
            for j in values_after[n]:
                for b in range(2):
                    act.wait_ge(s_vdone, 2 * j + b + 1)
                    wait(act, s_vtr, j - 1)
                    nc.scalar.activation(vT[:, j % 2, b * HALF:(b + 1) * HALF], ps[:, 4 + b, 0:HALF], ACT.Copy).then_inc(s_vfree, 1)
                if j + 2 < 8:
                    k.high(act, vst, divmod(j + 2, 4))
                if j:
                    store_values(j - 1)
        store_values(7)
        act.wait_ge(s_vout, 8)

    def dve_program(dve):
        def do(ins):
            steps.mark(ins)
            steps.settle(dve)
        pre.dve(dve)
        for j, u in enumerate([0, 1, 2, 3, 4]):
            if u == 4:
                dve.wait_ge(s_r, 2)
                v.scalar_tensor_tensor(raw[:, 4, :], raw[:, 4, :], k.col(V_IDX), rstd, ALU.mult, ALU.mult).then_inc(s_kn, 1)
                dve.wait_ge(s_kn, 1)
            else:
                dve.wait_ge(s_free, 2 * order.index(u) + 2)
            do(v.tensor_tensor(t1, raw[:, u, :], k.cos2, ALU.mult))
            dve.wait_ge(s_rot, j + 1)
            do(v.tensor_tensor(both(t2), ps[:, 2:4, 0:HALF], both(k.sin2), ALU.mult))
            v.tensor_tensor(rop[:, u, :], t1, t2, ALU.add).then_inc(s_rope, 1)
            dve.wait_ge(s_rope, j + 1)
        dve.wait_ge(s_wip, 1)
        for t, (c, n) in list(enumerate(TILES))[1:]:
            do(v.tensor_scalar(wi[0:n, t, :], ps[0:n, 6 + t // 4, (t % 4) * P:(t % 4) * P + NH], float(NH ** -0.5), None, ALU.mult))
        do(v.tensor_copy(mb[:, 0, 0:P], k.maskb[:, P:2 * P]))
        for n in range(1, 5):
            c, nq = TILES[n]
            N = c + nq
            for x in range(NH):
                q = NH * (n - 1) + x
                dve.wait_ge(s_rel, q + 1)
                w = wi[0:nq, n, x:x + 1]
                if x == 0:
                    v.tensor_scalar(sc[0:nq, 0:N], rel[0:nq, x, 0:N], w, None, ALU.mult).then_inc(s_acc, 1)
                else:
                    v.scalar_tensor_tensor(sc[0:nq, 0:N], rel[0:nq, x, 0:N], w, sc[0:nq, 0:N], ALU.mult, ALU.add).then_inc(s_acc, 1)
                dve.wait_ge(s_acc, q + 1)
            do(v.memset(sc[0:nq, 0:META], 1e30))
            do(v.scalar_tensor_tensor(sc[0:nq, c:N], k.maskf[0:nq, P:P + nq], 1e8, sc[0:nq, c:N], ALU.mult, ALU.add))
            for _ in range(TOPK // 8):
                do(v.max(m8[0:nq, :], sc[0:nq, 0:N]))
                do(v.match_replace(sc[0:nq, 0:N], m8[0:nq, :], sc[0:nq, 0:N], -3e38))
            do(v.tensor_scalar(mb[0:nq, n, 0:N], sc[0:nq, 0:N], -2e38, NEG, ALU.is_gt, ALU.mult))
        steps.end()
    return sync_program, pool_program, pe_program, act_program, dve_program


def ffn_up(k, name, l, st, nxt, pre):
    nc, ps = k.nc, k.ps
    v = nc.vector
    w0, w2 = (2 + 2 * l) * P, (3 + 2 * l) * P
    with ExitStack() as ctx:
        u = k.sb(name + "_u", [P, 4, 2 + T2], F32, ctx)
        cc = k.sb(name + "_c", [P, 4, T2], F32, ctx)
        s_done, s_free, s_conv, s_silu, s_out = (k.sem(f"{name}_{x}") for x in ("done", "free", "conv", "silu", "out"))
        steps = Steps(k.sem(name + "_steps"))
        with nc.Block() as block:
            @block.sync
            def _(sp):
                k.stream(sp, st, nxt)

            @block.gpsimd
            def _(pool):
                k.low_all(pool, st)

            @block.tensor
            def _(pe):
                def step(i):
                    for x in range(4):
                        k.split_ready(pe, st, i, x)
                        for b in range(2):
                            wait(pe, s_free, 8 * i + 2 * x + b - 1)
                            first = isinstance(i, int) and x == b == 0
                            k.product(st, x, ps[:, b, 0:HALF], k.hx(b * HALF, HALF), before=(lambda f: pre.ready(pe, f)) if first else None).then_inc(s_done, 1)
                pre.pe(pe)
                step(0)
                with pe.Fori(1, st.iterations) as i:
                    step(i)

            @block.scalar
            def _(act):
                def step(i):
                    for y in range(2):
                        for x in (2 * y, 2 * y + 1):
                            for b in range(2):
                                act.wait_ge(s_done, 8 * i + 2 * x + b + 1)
                                wait(act, s_conv, 4 * i - 3 + x if not isinstance(i, int) or i else 0)
                                nc.scalar.activation(u[:, x, 2 + b * HALF:2 + (b + 1) * HALF], ps[:, b, 0:HALF], ACT.Copy).then_inc(s_free, 1)
                            k.high(act, st, st.after(i, x, st.depth))
                        act.wait_ge(s_conv, 4 * i + 2 * y + 1)
                        nc.scalar.activation(cc[:, 2 * y, :], cc[:, 2 * y, :], ACT.Silu).then_inc(s_silu, 1)
                k.high_first(act, st)
                pre.act(act)
                step(0)
                with act.Fori(1, st.iterations - 1) as i:
                    step(i)
                step(st.iterations - 1)

            @block.vector
            def _(dve):
                def do(ins):
                    steps.mark(ins)
                    steps.settle(dve)

                def step(i):
                    steps.begin(i)
                    for y in range(2):
                        for x in (2 * y, 2 * y + 1):
                            tile = 2 * i + y + FT * (x % 2)
                            dve.wait_ge(s_free, 8 * i + 2 * x + 2)
                            acc = cc[:, x, :]
                            do(v.tensor_scalar(acc, u[:, x, 0:T2], k.col(w0 + tile), k.col(w2 + 2 * FT + tile), ALU.mult, ALU.add))
                            do(v.scalar_tensor_tensor(acc, u[:, x, 1:1 + T2], k.col(w0 + 2 * FT + tile), acc, ALU.mult, ALU.add))
                            v.scalar_tensor_tensor(acc, u[:, x, 2:2 + T2], k.col(w2 + tile), acc, ALU.mult, ALU.add).then_inc(s_conv, 1)
                            dve.wait_ge(s_conv, 4 * i + x + 1)
                        dve.wait_ge(s_silu, 2 * i + y + 1)
                        v.tensor_tensor(k.wide[:, bass.ds(2 * i + y, 1), :].rearrange("p a t -> p (a t)"), cc[:, 2 * y, :], cc[:, 2 * y + 1, :],
                                        ALU.mult).then_inc(s_out, 1)
                        dve.wait_ge(s_out, 2 * i + y + 1)
                    steps.end()
                first = k.sem(name + "_zero")
                v.memset(u[:, :, 0:2], 0.0).then_inc(first, 1)
                dve.wait_ge(first, 1)
                pre.dve(dve)
                step(0)
                with dve.Fori(1, st.iterations) as i:
                    step(i)


def finish(k, pre):
    nc, ps = k.nc, k.ps
    with ExitStack() as ctx:
        o = k.sb("out_tok", [P, 4, DM], F32, ctx)
        s_t, s_c, s_out = k.sem("fin_transposed"), k.sem("fin_copied"), k.sem("out_stored")
        with nc.Block() as block:
            @block.tensor
            def _(pe):
                pre.pe(pe)
                for t in range(4):
                    for g in range(2):
                        for f in range(4):
                            if t == 0:
                                pre.ready(pe, 4 * g + f)
                            m = nc.tensor.transpose(ps[:, 2 * t + g, f * P:(f + 1) * P],
                                                    k.h[:, KT + 4 * g + f, META + t * P:META + (t + 1) * P], k.ident)
                    m.then_inc(s_t, 1)

            @block.scalar
            def _(act):
                pre.act(act)
                for t in range(4):
                    act.wait_ge(s_t, t + 1)
                    nc.scalar.activation(o[:, t, :].rearrange("p (b n) -> p b n", b=2), ps[:, 2 * t:2 * t + 2, :], ACT.Copy).then_inc(s_c, 1)

            @block.vector
            def _(dve):
                pre.dve(dve)

            @block.sync
            def _(sp):
                for t in range(4):
                    sp.wait_ge(s_c, t + 1)
                    sp.dma_start(k.out[0, t * P:(t + 1) * P, :], o[:, t, :]).then_inc(s_out, 16)
                sp.wait_ge(s_out, 64)


def build(nc, a, out, probe=None, dump=None):
    with ExitStack() as ctx:
        k = Core(nc, a, out, ctx)
        v = nc.vector
        w_in, w_att, w_da, w_dsa = a["ssm_w_in"][0], a["att_w_in"][0], a["da_w_qkv_2"][0], a["dsa_w_in_2"][0]

        def one(w, kt, col, row=lambda i, u: 0):
            return lambda i, u: [(0, P, w, row(i, u), col(i, u))]

        def twice(w, c):
            return [(0, 64, w, 0, c), (64, 64, w, 0, c)]

        def split(w, kt, n=1):
            return Stream(2 * n, 4, kt, lambda i, u: [(0, P, w, (u % n) * kt * P, i * (4 // n * P) + (u // n) * P)])

        def ssm_col(g, u):
            return (2048 + 256 * g, 2176 + 256 * g, 4096 + P * g, 5120 + P * g, 256 * g, 128 + 256 * g)[u]

        def swa_unit(j, u):
            two = (u == 0, u == 1)
            if two[0] or two[1]:
                return twice(w_att, 1024 + 256 * u + 64 * j)
            c = (256 * j, 128 + 256 * j, 1536 + 256 * j, 1664 + 256 * j)[u - 2]
            return [(0, 64, w_att, 0, c), (64, 64, w_att, 0, c + 64)]

        def idx_unit(i, u):
            if u == 0:
                return twice(w_dsa, 3584)
            if u == 5:
                return [(0, 8, w_dsa, 0, 3648), (8, 120, w_dsa, 0, 3528)]
            return [(0, 64, w_dsa, 0, 3072 + P * (u - 1)), (64, 64, w_dsa, 0, 3136 + P * (u - 1))]

        def up(l):
            w = a["ffn_w_up_2"][l]
            return Stream(FT // 2, 4, KT, one(w, KT, lambda i, u: i * (2 * P) + (u // 2) * P + (u % 2) * FF))
        S = {
            "ssm": Stream(GROUPS, 6, KT, one(w_in, KT, ssm_col)),
            "ssm_out": split(a["ssm_w_out"][0], KT, 2),
            "swa": Stream(KV, 6, KT, swa_unit, dmas=2),
            "swa_out": split(a["att_w_out"][0], KT),
            "da": Stream(8, 3, KT, one(w_da, KT, lambda i, u: i * P + u * DM)),
            "da_out": split(a["da_w_o_2"][0], KT),
            "up0": up(0), "down0": split(a["ffn_w_down_2"][0], FK, 2),
            "idx": Stream(1, 6, KT, idx_unit, dmas=2),
            "values": Stream(2, 4, KT, one(w_dsa, KT, lambda i, u: 4 * i * P + u * P + 2 * DM)),
            "dsa": Stream(8, 2, KT, one(w_dsa, KT, lambda i, u: i * P + u * DM)),
            "dsa_out": split(a["dsa_w_o_2"][0], KT),
            "up1": up(1), "down1": split(a["ffn_w_down_2"][1], FK, 2),
        }
        names = list(S)
        for n in names:
            k.start_stream(S[n])
        following = {n: (S[names[j + 1]] if j + 1 < len(names) else None) for j, n in enumerate(names)}
        if probe:
            order = ["ssm", "swa", "da", "ffn0", "dsa", "ffn1"]
            ends = {"ssm": "ssm_out", "swa": "swa_out", "da": "da_out", "ffn0": "down0", "dsa": "dsa_out", "ffn1": "down1"}
            following[ends[probe]] = None

        def done(x):
            if probe != x:
                return False
            s = k.sem("dumped")
            with nc.Block() as block:
                @block.sync
                def _(sp):
                    sp.dma_start(dump, k.res[:]).then_inc(s, 16)
                    sp.wait_ge(s, 16)
            return True

        def h1(f):
            return k.h[:, KT + f, 0:SEQ]

        def y1(f):
            return k.h[:, f, 0:SEQ]

        def r1(f):
            return k.res[:, f, META:T2]

        def wide1(f):
            return k.wide[:, f, 0:SEQ]

        def h2(f):
            return k.h[:, KT + f, :]

        def r2(f):
            return k.res[:, f, :]

        def wide2(f):
            return k.wide[:, f, :]

        def to_y(t, c, n, src):
            return v.tensor_copy(k.h[:, bass.ds(t, 1), c:c + n].rearrange("p a t -> p (a t)"), src)

        def y_tile(t):
            return k.h[:, bass.ds(t, 1), 0:SEQ].rearrange("p a t -> p (a t)")

        def res_tile(t):
            return k.res[:, bass.ds(t, 1), :].rearrange("p a t -> p (a t)")

        def to_res(t, c, n, src):
            dst = k.res[:, bass.ds(t, 1), c:c + n].rearrange("p a t -> p (a t)")
            return v.tensor_tensor(dst, src, dst, ALU.add)

        tables = Tables(k)
        setup(k, S["ssm"], tables)
        parts1 = lambda f: k.h_parts[:, f, 0:SEQ], lambda f: k.h_parts[:, KT + f, 0:SEQ]
        parts2 = lambda f: k.h_parts[:, f, :], lambda f: k.h_parts[:, KT + f, :]
        wide_low1, wide_low2 = lambda f: k.wide_parts[:, f, 0:SEQ], lambda f: k.wide_parts[:, f, :]

        ssm(k, S["ssm"], following["ssm"], Norm(k, r1, KT, SEQ, V_PRE, h1, parts=parts1), tables)
        with ExitStack() as own:
            gated = k.sb("gated_high", [P, 2 * KT, SEQ], F32R, own)
            project(k, "ssm_out", S["ssm_out"], following["ssm_out"], 2, None, None, SEQ, to_y, y_tile,
                    Norm(k, wide1, 2 * KT, SEQ, V_GATE, wide1, parts=(lambda f: gated[:, f, :], wide_low1)))
        buffers = k.wide[:, 20:22, 0:SEQ], k.wide[:, 16:20, 0:SEQ]
        swa(k, S["swa"], following["swa"], Norm(k, r1, KT, SEQ, V_PRE + 8, h1, post=(y1, V_POST, r1, *buffers), parts=parts1))
        project(k, "swa_out", S["swa_out"], following["swa_out"], 1, wide1, (parts1[1], wide_low1), SEQ, to_y, y_tile)
        buffers = k.wide[:, 4:6, 0:SEQ], k.wide[:, 0:4, :]
        pairs(k, "da", S["da"], following["da"], True,
              Norm(k, r2, KT, T2, V_DA, h2, post=(y1, V_POST + 8, r1, *buffers), parts=parts2))
        project(k, "da_out", S["da_out"], following["da_out"], 1, wide2, (parts2[0], wide_low2), T2, to_res, res_tile)
        if done("da"):
            return

        def ffn(l):
            up, down = f"up{l}", f"down{l}"
            ffn_up(k, up, l, S[up], following[up], Norm(k, r2, KT, T2, V_FFN + 8 * l, h2, parts=parts2))
            with ExitStack() as own:
                more = k.sb(f"hidden_high{l}", [P, FT - 2 * KT, T2], F32R, own)
                project(k, down, S[down], following[down], 2, wide2,
                        (lambda f: k.h_parts[:, f, :] if f < 2 * KT else more[:, f - 2 * KT, :], wide_low2), T2, to_res, res_tile)
        ffn(0)
        if done("ffn0"):
            return
        with ExitStack() as own:
            mb = k.sb("mb", [P, 5, T2], BF16, own)
            vall = k.sb("values", [P, 8, 5, P], F32, own)
            head = index(k, S["idx"], S["values"], following["values"], Norm(k, r2, KT, T2, V_DSA, h2, parts=parts2), mb, vall, own)
            pairs(k, "dsa", S["dsa"], following["dsa"], False, mb=mb, vall=vall, head=head)
        project(k, "dsa_out", S["dsa_out"], following["dsa_out"], 1, wide2, (parts2[0], wide_low2), T2, to_res, res_tile)
        if done("dsa"):
            return
        ffn(1)
        if done("ffn1"):
            return
        finish(k, Norm(k, r2, KT, T2, V_FIN, h2))


def kernel(**inputs):
    import concourse.bacc as bacc
    from concourse.bass_utils import run_bass_kernel_spmd

    nc = bacc.Bacc("TRN2", target_bir_lowering=False, num_devices=1)
    arrays, aps = {}, {}
    for name, x in inputs.items():
        x = np.ascontiguousarray(x)
        arrays["in_" + name] = x
        aps[name] = nc.dram_tensor("in_" + name, x.shape, mybir.dt.from_np(x.dtype), kind="ExternalInput").ap()
    out = nc.dram_tensor("out", (1, SEQ, DM), F32, kind="ExternalOutput").ap()
    build(nc, aps, out)
    r = run_bass_kernel_spmd(nc, [arrays], core_ids=[0])
    return r.results[0]["out"]
```
